# Optimizing a Trainium2 kernel written in Bass

```python
import math
import jax, jax.numpy as jnp
from jax import lax
import numpy as np

D_MODEL = 1024
BATCH = 1
SEQ = 1024
DEPTH = 2
DEC_BATCH = 8
DEC_SEQ = 4
PAST_LEN = 512
PAGE_SIZE = 128

N_A_LAYERS = DEPTH // 2
N_B_LAYERS = DEPTH - N_A_LAYERS
SSM_GROUP = 16
SSM_GROUPS = D_MODEL // SSM_GROUP
SSM_STATE = 64
DT_MIN = 0.001
DT_MAX = 0.1
N_HEADS = 8
HEAD_DIM = D_MODEL // (2 * N_HEADS)
V_DIM = 2 * HEAD_DIM
Q_DIM = N_HEADS * 2 * HEAD_DIM
KV_DIM = Q_DIM + N_HEADS * V_DIM
D_FF = 4 * D_MODEL
NUM_BUCKETS = 32
MAX_DISTANCE = 128
Q_BLOCK = 128
N_MOD = 6
ALPHA = (2.0 * DEPTH) ** 0.25
BETA = (8.0 * DEPTH) ** -0.25
LN_EPS = 1e-5
NEG_INF = -1e30

kernel_name = "yoco_s5_diffattn_decoder_step"

def _layer_norm(x, g, b):
    xf = x.astype(jnp.float32)
    mu = jnp.mean(xf, -1, keepdims=True)
    var = jnp.mean(jnp.square(xf - mu), -1, keepdims=True)
    return ((xf - mu) * lax.rsqrt(var + LN_EPS) * g.astype(jnp.float32) + b.astype(jnp.float32)).astype(x.dtype)

def _rms_norm(x, g):
    xf = x.astype(jnp.float32)
    return (xf * lax.rsqrt(jnp.mean(jnp.square(xf), -1, keepdims=True) + LN_EPS) * g.astype(jnp.float32)).astype(x.dtype)

def _rel_bucket(rel):
    n = jnp.maximum(rel, 0)
    max_exact = NUM_BUCKETS // 2
    large = max_exact + (jnp.log(jnp.maximum(n, 1).astype(jnp.float32) / max_exact)
                         / math.log(MAX_DISTANCE / max_exact) * (NUM_BUCKETS - max_exact)).astype(jnp.int32)
    large = jnp.minimum(large, NUM_BUCKETS - 1)
    return jnp.where(n < max_exact, n, large)

def _rel_bias(rel_bias, q_pos, k_pos):
    b = rel_bias[_rel_bucket(q_pos[:, None] - k_pos[None, :])]
    return jnp.transpose(b, (2, 0, 1)).astype(jnp.float32)

def _ssm_combine(e1, e2):
    a1r, a1i, b1r, b1i = e1
    a2r, a2i, b2r, b2i = e2
    return (a2r * a1r - a2i * a1i, a2r * a1i + a2i * a1r,
            a2r * b1r - a2i * b1i + b2r, a2r * b1i + a2i * b1r + b2i)

def _ssm_mixer(u, h0_re, h0_im, lam_re, lam_im, log_dt, b_re, b_im, c_re, c_im, d_skip, w_glu_a, w_glu_b):
    f32 = jnp.float32
    nb, t = u.shape[0], u.shape[1]
    uf = u.astype(f32).reshape(nb, t, SSM_GROUPS, SSM_GROUP)
    dt = jnp.exp(log_dt.astype(f32))[:, None]
    lr = lam_re.astype(f32)
    li = lam_im.astype(f32)
    mag = jnp.exp(lr * dt)
    ar = mag * jnp.cos(li * dt)
    ai = mag * jnp.sin(li * dt)
    den = lr * lr + li * li
    er = ((ar - 1.0) * lr + ai * li) / den
    ei = (ai * lr - (ar - 1.0) * li) / den
    br = b_re.astype(f32)
    bi = b_im.astype(f32)
    bbr = er[..., None] * br - ei[..., None] * bi
    bbi = er[..., None] * bi + ei[..., None] * br
    bu_r = jnp.einsum('btgh,gph->btgp', uf, bbr)
    bu_i = jnp.einsum('btgh,gph->btgp', uf, bbi)
    h0r = h0_re.astype(f32)
    h0i = h0_im.astype(f32)
    bu_r = bu_r.at[:, 0].add(ar * h0r - ai * h0i)
    bu_i = bu_i.at[:, 0].add(ar * h0i + ai * h0r)
    a_r = jnp.broadcast_to(ar, (t,) + ar.shape)
    a_i = jnp.broadcast_to(ai, (t,) + ai.shape)

    def scan_one(xr, xi):
        _, _, sr, si = lax.associative_scan(_ssm_combine, (a_r, a_i, xr, xi))
        return sr, si

    sr, si = jax.vmap(scan_one)(bu_r, bu_i)
    y = (jnp.einsum('btgp,ghp->btgh', sr, c_re.astype(f32))
         - jnp.einsum('btgp,ghp->btgh', si, c_im.astype(f32))
         + d_skip.astype(f32).reshape(SSM_GROUPS, SSM_GROUP) * uf)
    y = y.reshape(nb, t, D_MODEL).astype(u.dtype)
    g = jax.nn.gelu(y)
    out = (g @ w_glu_a) * jax.nn.sigmoid(g @ w_glu_b)
    return out, sr[:, -1].astype(h0_re.dtype), si[:, -1].astype(h0_im.dtype)

def _diff_weights(logits, lam):
    p = jax.nn.softmax(logits, axis=-1)
    return p[:, :, 0] - lam * p[:, :, 1]

def _diff_attn_prompt(q, k, v, rel_bias, lam):
    nb, t = q.shape[0], q.shape[1]
    n_blk = t // Q_BLOCK
    qb = jnp.moveaxis(q.reshape(nb, n_blk, Q_BLOCK, N_HEADS, 2, HEAD_DIM), 1, 0)
    starts = jnp.arange(n_blk, dtype=jnp.int32) * Q_BLOCK
    k_pos = jnp.arange(t, dtype=jnp.int32)
    scale = HEAD_DIM ** -0.5

    def block(args):
        q_i, start = args
        q_pos = start + jnp.arange(Q_BLOCK, dtype=jnp.int32)
        logits = jnp.einsum('bqhcd,bkhcd->bhcqk', q_i, k).astype(jnp.float32) * scale
        logits = logits + _rel_bias(rel_bias, q_pos, k_pos)[None, :, None]
        logits = jnp.where(k_pos[None, :] <= q_pos[:, None], logits, NEG_INF)
        w = _diff_weights(logits, lam)
        return jnp.einsum('bhqk,bkhe->bqhe', w.astype(v.dtype), v)

    o = lax.map(block, (qb, starts))
    return jnp.moveaxis(o, 0, 1).reshape(nb, t, N_HEADS, V_DIM)

def _diff_attn_sample(q, k, v, k_past, v_past, rel_bias, lam):
    t = q.shape[1]
    past = k_past.shape[1]
    q_pos = past + jnp.arange(t, dtype=jnp.int32)
    k_pos = jnp.arange(past + t, dtype=jnp.int32)
    scale = HEAD_DIM ** -0.5
    lp = jnp.einsum('bqhcd,bkhcd->bhcqk', q, k_past)
    ln = jnp.einsum('bqhcd,bkhcd->bhcqk', q, k)
    logits = jnp.concatenate([lp, ln], axis=-1).astype(jnp.float32) * scale
    logits = logits + _rel_bias(rel_bias, q_pos, k_pos)[None, :, None]
    logits = jnp.where(k_pos[None, :] <= q_pos[:, None], logits, NEG_INF)
    w = _diff_weights(logits, lam).astype(v.dtype)
    return (jnp.einsum('bhqk,bkhe->bqhe', w[..., :past], v_past)
            + jnp.einsum('bhqk,bkhe->bqhe', w[..., past:], v))

def _trunk(x, c, h0_re, h0_im, attend, p):
    nb, t = x.shape[0], x.shape[1]
    sc = jax.nn.silu(c)
    ssm_re, ssm_im = [], []
    k = None
    v = None
    for layer in range(DEPTH):
        mod = (sc @ p['w_ada'][layer] + p['b_ada'][layer]).reshape(nb, 1, N_MOD, D_MODEL)
        shift_m, scale_m, gate_m = mod[:, :, 0], mod[:, :, 1], mod[:, :, 2]
        shift_f, scale_f, gate_f = mod[:, :, 3], mod[:, :, 4], mod[:, :, 5]
        h = x * (1.0 + scale_m) + shift_m
        if layer < N_A_LAYERS:
            out, fr, fi = _ssm_mixer(h, h0_re[layer], h0_im[layer],
                                     p['ssm_lam_re'][layer], p['ssm_lam_im'][layer], p['ssm_log_dt'][layer],
                                     p['ssm_b_re'][layer], p['ssm_b_im'][layer],
                                     p['ssm_c_re'][layer], p['ssm_c_im'][layer], p['ssm_d'][layer],
                                     p['ssm_w_glu_a'][layer], p['ssm_w_glu_b'][layer])
            ssm_re.append(fr)
            ssm_im.append(fi)
        else:
            j = layer - N_A_LAYERS
            lam_init = 0.8 - 0.6 * math.exp(-0.3 * layer)
            lp = p['attn_lam'][j].astype(jnp.float32)
            lam = jnp.exp(jnp.sum(lp[0] * lp[1])) - jnp.exp(jnp.sum(lp[2] * lp[3])) + lam_init
            q = (h @ p['attn_w_q'][j]).reshape(nb, t, N_HEADS, 2, HEAD_DIM)
            o = attend(q, k, v, lam)
            o = _rms_norm(o, p['attn_subln_g'][j]) * (1.0 - lam_init)
            out = o.reshape(nb, t, D_MODEL) @ p['attn_w_o'][j]
        x = _layer_norm(ALPHA * x + (1.0 + gate_m) * out, p['ln_g'][layer, 0], p['ln_b'][layer, 0])
        h = x * (1.0 + scale_f) + shift_f
        hid = jnp.square(jax.nn.relu(h @ p['mlp_w1'][layer]))
        x = _layer_norm(ALPHA * x + (1.0 + gate_f) * (hid @ p['mlp_w2'][layer]),
                        p['ln_g'][layer, 1], p['ln_b'][layer, 1])
        if layer == N_A_LAYERS - 1:
            mkv = (sc @ p['w_ada_kv'] + p['b_ada_kv']).reshape(nb, 1, 2, D_MODEL)
            hkv = x * (1.0 + mkv[:, :, 1]) + mkv[:, :, 0]
            kv = hkv @ p['w_kv']
            k = kv[..., :Q_DIM].reshape(nb, t, N_HEADS, 2, HEAD_DIM)
            v = kv[..., Q_DIM:].reshape(nb, t, N_HEADS, V_DIM)
    return x, jnp.stack(ssm_re), jnp.stack(ssm_im), k, v

def setup_inputs(seed: int = 0) -> dict:
    key = jax.random.key(seed)
    ks = jax.random.split(key, 40)
    f32 = jnp.float32
    n_pages = PAST_LEN // PAGE_SIZE
    n_phys = (5 * DEC_BATCH * n_pages + 3) // 4
    nrm = lambda k, shape, s: jax.random.normal(k, shape, f32) * s
    page_table = jax.random.permutation(ks[0], n_phys)[:DEC_BATCH * n_pages].reshape(DEC_BATCH, n_pages).astype(jnp.int32)
    lam_im_base = (math.pi * jnp.arange(SSM_STATE, dtype=f32))[None, None, :]
    return {
        'x_prompt': nrm(ks[1], (BATCH, SEQ, D_MODEL), 1.0),
        'x_sample': nrm(ks[2], (DEC_BATCH, DEC_SEQ, D_MODEL), 1.0),
        'state_ssm_re': nrm(ks[3], (N_A_LAYERS, DEC_BATCH, SSM_GROUPS, SSM_STATE), 0.1),
        'state_ssm_im': nrm(ks[4], (N_A_LAYERS, DEC_BATCH, SSM_GROUPS, SSM_STATE), 0.1),
        'cache_k': nrm(ks[5], (n_phys, PAGE_SIZE, N_HEADS, 2, HEAD_DIM), 1.0),
        'cache_v': nrm(ks[6], (n_phys, PAGE_SIZE, N_HEADS, V_DIM), 1.0),
        'page_table': page_table,
        'c_prompt': nrm(ks[7], (BATCH, D_MODEL), 1.0),
        'c_sample': nrm(ks[8], (DEC_BATCH, D_MODEL), 1.0),
        'rel_bias': nrm(ks[9], (NUM_BUCKETS, N_HEADS), 0.5),
        'w_ada': nrm(ks[10], (DEPTH, D_MODEL, N_MOD * D_MODEL), 0.1 * D_MODEL ** -0.5),
        'b_ada': nrm(ks[11], (DEPTH, N_MOD * D_MODEL), 0.02),
        'ln_g': 1.0 + nrm(ks[12], (DEPTH, 2, D_MODEL), 0.02),
        'ln_b': nrm(ks[13], (DEPTH, 2, D_MODEL), 0.02),
        'ssm_lam_re': -0.5 + nrm(ks[14], (N_A_LAYERS, SSM_GROUPS, SSM_STATE), 0.01),
        'ssm_lam_im': lam_im_base + nrm(ks[15], (N_A_LAYERS, SSM_GROUPS, SSM_STATE), 0.01),
        'ssm_log_dt': jax.random.uniform(ks[16], (N_A_LAYERS, SSM_GROUPS), f32, math.log(DT_MIN), math.log(DT_MAX)),
        'ssm_b_re': nrm(ks[17], (N_A_LAYERS, SSM_GROUPS, SSM_STATE, SSM_GROUP), (2.0 * SSM_GROUP) ** -0.5),
        'ssm_b_im': nrm(ks[18], (N_A_LAYERS, SSM_GROUPS, SSM_STATE, SSM_GROUP), (2.0 * SSM_GROUP) ** -0.5),
        'ssm_c_re': nrm(ks[19], (N_A_LAYERS, SSM_GROUPS, SSM_GROUP, SSM_STATE), (2.0 / SSM_STATE) ** 0.5),
        'ssm_c_im': nrm(ks[20], (N_A_LAYERS, SSM_GROUPS, SSM_GROUP, SSM_STATE), (2.0 / SSM_STATE) ** 0.5),
        'ssm_d': nrm(ks[21], (N_A_LAYERS, D_MODEL), 1.0),
        'ssm_w_glu_a': nrm(ks[22], (N_A_LAYERS, D_MODEL, D_MODEL), BETA * D_MODEL ** -0.5),
        'ssm_w_glu_b': nrm(ks[23], (N_A_LAYERS, D_MODEL, D_MODEL), D_MODEL ** -0.5),
        'w_ada_kv': nrm(ks[24], (D_MODEL, 2 * D_MODEL), 0.1 * D_MODEL ** -0.5),
        'b_ada_kv': nrm(ks[25], (2 * D_MODEL,), 0.02),
        'w_kv': nrm(ks[26], (D_MODEL, KV_DIM), D_MODEL ** -0.5),
        'attn_w_q': nrm(ks[27], (N_B_LAYERS, D_MODEL, Q_DIM), D_MODEL ** -0.5),
        'attn_lam': nrm(ks[28], (N_B_LAYERS, 4, HEAD_DIM), 0.1),
        'attn_subln_g': 1.0 + nrm(ks[29], (N_B_LAYERS, V_DIM), 0.02),
        'attn_w_o': nrm(ks[30], (N_B_LAYERS, D_MODEL, D_MODEL), BETA * D_MODEL ** -0.5),
        'mlp_w1': nrm(ks[31], (DEPTH, D_MODEL, D_FF), D_MODEL ** -0.5),
        'mlp_w2': nrm(ks[32], (DEPTH, D_FF, D_MODEL), BETA * D_FF ** -0.5),
    }

def reference(x_prompt, x_sample, state_ssm_re, state_ssm_im, cache_k, cache_v, page_table,
              c_prompt, c_sample, rel_bias, w_ada, b_ada, ln_g, ln_b,
              ssm_lam_re, ssm_lam_im, ssm_log_dt, ssm_b_re, ssm_b_im, ssm_c_re, ssm_c_im, ssm_d,
              ssm_w_glu_a, ssm_w_glu_b, w_ada_kv, b_ada_kv, w_kv,
              attn_w_q, attn_lam, attn_subln_g, attn_w_o, mlp_w1, mlp_w2):
    params = dict(w_ada=w_ada, b_ada=b_ada, ln_g=ln_g, ln_b=ln_b,
                  ssm_lam_re=ssm_lam_re, ssm_lam_im=ssm_lam_im, ssm_log_dt=ssm_log_dt,
                  ssm_b_re=ssm_b_re, ssm_b_im=ssm_b_im, ssm_c_re=ssm_c_re, ssm_c_im=ssm_c_im, ssm_d=ssm_d,
                  ssm_w_glu_a=ssm_w_glu_a, ssm_w_glu_b=ssm_w_glu_b,
                  w_ada_kv=w_ada_kv, b_ada_kv=b_ada_kv, w_kv=w_kv,
                  attn_w_q=attn_w_q, attn_lam=attn_lam, attn_subln_g=attn_subln_g, attn_w_o=attn_w_o,
                  mlp_w1=mlp_w1, mlp_w2=mlp_w2)
    h0_p = jnp.zeros((N_A_LAYERS, x_prompt.shape[0], SSM_GROUPS, SSM_STATE), state_ssm_re.dtype)

    def attend_prompt(q, k, v, lam):
        return _diff_attn_prompt(q, k, v, rel_bias, lam)

    y_prompt, ssm_re_p, ssm_im_p, k_p, v_p = _trunk(x_prompt, c_prompt, h0_p, h0_p, attend_prompt, params)

    n_seq = page_table.shape[0]
    k_past = cache_k[page_table].reshape(n_seq, -1, N_HEADS, 2, HEAD_DIM)
    v_past = cache_v[page_table].reshape(n_seq, -1, N_HEADS, V_DIM)

    def attend_sample(q, k, v, lam):
        return _diff_attn_sample(q, k, v, k_past, v_past, rel_bias, lam)

    y_sample, ssm_re_s, ssm_im_s, k_s, v_s = _trunk(x_sample, c_sample, state_ssm_re, state_ssm_im,
                                                    attend_sample, params)
    return (y_prompt, y_sample, ssm_re_p, ssm_im_p, k_p, v_p, ssm_re_s, ssm_im_s, k_s, v_s)


_drawn_inputs = setup_inputs


def setup_inputs(seed=0):
    import zlib

    import numpy as np

    out = dict(_drawn_inputs(seed))
    spreads = {}
    factors = {'ssm_lam_re': 4.029,
     'ssm_c_re': 3.199,
     'ssm_c_im': 3.172,
     'attn_lam': 8.0,
     'attn_subln_g': 8.0}
    for name, (base, spread) in spreads.items():
        noise = np.random.default_rng([zlib.crc32(name.encode()), seed]).standard_normal(out[name].shape)
        drawn = base * np.exp(spread * noise) if base else spread * noise
        out[name] = __import__('jax').numpy.asarray(drawn.astype(out[name].dtype))
    for name, factor in factors.items():
        out[name] = (out[name] * factor).astype(out[name].dtype)
    return out
```

```python
import math
from contextlib import ExitStack, contextmanager

import numpy as np
import concourse.bass as bass
from concourse import mybir

F32 = mybir.dt.float32
F32R = mybir.dt.float32r
I32 = mybir.dt.int32
ALU = mybir.AluOpType
ACT = mybir.ActivationFunctionType
AX = mybir.AxisListType

P = 128
D = 1024
KT = D // P
SEQ = 1024
NB, ST = 8, 4
NS = NB * ST
NT = SEQ + NS
NCH = 3
CH = NT // NCH
LASTP = SEQ - 2 * CH
NC9 = 1 + NB
G, GC, NP = 64, 16, 64
GB = P // GC
L = 8
NCK = SEQ // L
H, HD, VD = 8, 64, 128
DFF = 4096
PAGE = 128
PAST = 512
NPG = PAST // PAGE
NPHYS = 40
ALPHA = (2.0 * 2) ** 0.25
LN_EPS = 1e-5
NEG = -1e30
LAM_INIT = 0.8 - 0.6 * math.exp(-0.3)
NMOD = 14
WC = 256
FM = 1152
NPOW = L + 1
NROT = 7
IMP, ROTC, ROTS, R8, ERD, EIS = NPOW, 2 * NPOW, 2 * NPOW + NROT, 2 * NPOW + 2 * NROT, 2 * NPOW + 2 * NROT + 1, 2 * NPOW + 2 * NROT + 2
NPT = EIS + 1


class Chain:

    def __init__(self, eng, sem):
        self.eng, self.sem, self.n, self.base = eng, sem, 0, 0

    def __call__(self, ins):
        self.n += 1
        ins.then_inc(self.sem, 1)
        self.eng.wait_ge(self.sem, self.base + self.n)

    def turn(self, i, per_turn, before=0):
        self.base, self.n = i * per_turn + before, 0


@contextmanager
def semaphores(nc):
    taken = []

    def take(name):
        taken.append(nc.alloc_semaphore(name=name))
        return taken[-1]

    yield take
    nc.clear_and_free_semaphores(taken)
    nc.all_engine_barrier()


def bucket_onehot():
    dist = (D - 1) - np.arange(FM)
    n = np.maximum(dist, 0)
    large = 16 + (np.log(np.maximum(n, 1).astype(np.float32) / np.float32(16))
                  / np.float32(math.log(8.0)) * np.float32(16)).astype(np.int32)
    b = np.where(n < 16, n, np.minimum(large, 31))
    out = np.zeros((33, FM), np.float32)
    out[b, np.arange(FM)] = (dist >= 0)
    out[32] = (dist < 0)
    return out


def constants():
    ident = np.eye(P, dtype=np.float32)
    swap = np.roll(ident, P // 2, axis=1)
    flip = ident[::-1].copy()
    select = np.zeros((P, GB, L, GC), np.float32)
    for g in range(GB):
        for h in range(GC):
            select[g * GC + h, g, :, h] = 1
    comb = np.zeros((H, 2, ST, H, ST), np.float32)
    for h in range(H):
        for t in range(ST):
            comb[h, :, t, h, t] = 1
    comp = np.zeros((H, 2, ST, 2), np.float32)
    comp[:, 0, :, 0] = comp[:, 1, :, 1] = 1
    return {"c_comp": comp.reshape(2 * NS, 2), "c_ident": ident, "c_swap": swap, "c_flip": flip, "c_select": select.reshape(P, GB * P),
            "c_comb": comb.reshape(2 * NS, NS), "c_bucket": bucket_onehot()}


def params_block(nc, a, m):
    MAG = 12582912.0
    with ExitStack() as c:
        sb = lambda n, s, d=F32: c.enter_context(nc.sbuf_tensor(n, s, d, side="right"))
        lamr, lami, logdt = sb("lamr", [G, NP]), sb("lami", [G, NP]), sb("logdt", [G, 1])
        tmp = sb("ptmp", [G, 12, 4 * NP])
        tmpi = sb("ptmpi", [G, NP], I32)
        ar, ai = sb("ar", [G, NPOW, NP]), sb("ai", [G, NPOW, NP])
        rc, rs = sb("rc", [G, NROT, NP]), sb("rs", [G, NROT, NP])
        rows = sb("prows", [G, NPT, P])
        brow, browx = sb("brow", [G, P, GC]), sb("browx", [G, P, GC])
        crow, crowx = sb("crow", [P, KT, P]), sb("crowx", [P, KT, P])
        hrow, hrowx = sb("hrow", [P, 4, P]), sb("hrowx", [P, 4, P])
        bst0, bsw0 = sb("bst0", [P, GC, G]), sb("bsw0", [P, GC, G])
        mix = sb("bmix", [P, G, GC])
        cond = sb("cond", [NC9, D])
        csig = sb("csig", [NC9, D])
        brows1, brows2 = sb("brows1", [112, P]), sb("brows2", [65, P])
        onehot, relx = sb("onehot", [33, FM]), sb("relx", [33, H])
        fdist = sb("fdist", [H, FM])
        eps = m.eps
        signal = c.enter_context(semaphores(nc))
        S = lambda n: signal(n)
        small_in, trig_in, tables_in, dist_out = S("p_small_in"), S("p_trig_in"), S("p_tables_in"), S("p_dist_out")
        params_ready, angle_ready, trig_done = S("p_rows_ready"), S("p_angle"), S("p_trig")
        turned, turned_out, silu_half, dve_chain, relx_set = S("p_turned"), S("p_turned_out"), S("p_silu"), S("p_dve"), S("p_relx")
        blk = c.enter_context(nc.Block())
        n_tables = 0

        @blk.sync
        def _(sp):
            for out, src in ((lamr, a["ssm_lam_re"][0]), (lami, a["ssm_lam_im"][0]),
                             (logdt, a["ssm_log_dt"].rearrange("l (g o) -> (l g) o", o=1))):
                sp.dma_start(out[:], src).then_inc(small_in, 16)
            tables = [
                (m.ident[:], a["c_ident"]), (m.swap[:], a["c_swap"]), (m.select[:], a["c_select"]),
                (m.comb[:], a["c_comb"]), (onehot[:], a["c_bucket"]), (relx[0:32, :], a["rel_bias"]),
                (cond[0:1, :], a["c_prompt"]), (cond[1:NC9, :], a["c_sample"]),
                (brows1[0:96, :], a["b_ada"].rearrange("l (r f) -> (l r) f", f=P)),
                (brows1[96:112, :], a["b_ada_kv"].rearrange("(r f) -> r f", f=P)),
                (brows2[0:32, :], a["ln_g"].rearrange("l i (r f) -> (l i r) f", f=P)),
                (brows2[32:64, :], a["ln_b"].rearrange("l i (r f) -> (l i r) f", f=P)),
                (brows2[64:65, :], a["attn_subln_g"]),
                (brow[:, 0:NP, :], a["ssm_b_re"][0]), (brow[:, NP:P, :], a["ssm_b_im"][0]),
                (browx[:, 0:NP, :], a["ssm_b_im"][0]), (browx[:, NP:P, :], a["ssm_b_re"][0]),
            ]
            for half, (x, y) in enumerate((("ssm_c_re", "ssm_c_im"), ("ssm_c_im", "ssm_c_re"))):
                dst = (crow, crowx)[half]
                for k, src in enumerate((x, y)):
                    tables.append((dst[:, :, k * NP:(k + 1) * NP],
                                   a[src][0].rearrange("(t g) h p -> (g h) t p", g=GB)))
            for half, (x, y) in enumerate((("state_ssm_re", "state_ssm_im"), ("state_ssm_im", "state_ssm_re"))):
                dst = (hrow, hrowx)[half]
                for k, src in enumerate((x, y)):
                    tables.append((dst[:, :, k * NP:(k + 1) * NP],
                                   a[src][0].rearrange("(q b) g p -> (b g) q p", b=2)))
            nonlocal n_tables
            n_tables = len(tables) + 1
            for out, src in tables:
                sp.dma_start(out, src).then_inc(tables_in, 16)
            with nc.allow_non_contiguous_dma(reason="1024 single values, once"):
                sp.dma_start(m.dskip[:], a["ssm_d"].rearrange("l (g h) -> (l h) g", h=GC)).then_inc(tables_in, 16)
            sp.wait_ge(turned_out, 11)
            sp.dma_start(a["s_dist"], fdist[:]).then_inc(dist_out, 16)
            sp.wait_ge(dist_out, 16)

        @blk.gpsimd
        def _(pool):
            for n, (dst, value) in enumerate(((m.ones[:], 1.0 / D), (m.onesv[:], 1.0 / VD), (eps[:], LN_EPS),
                                              (relx[32:33, :], NEG))):
                pool.memset(dst, value).then_inc(relx_set, 1)
                pool.wait_ge(relx_set, n + 1)

        @blk.scalar
        def _(act):
            act.wait_ge(angle_ready, 1)
            act.activation(tmp[:, 1, 0:NP], tmp[:, 0, 0:NP], ACT.Sin).then_inc(trig_done, 1)
            act.activation(tmp[:, 3, 0:NP], tmp[:, 2, 0:NP], ACT.Sin).then_inc(trig_done, 1)
            act.wait_ge(tables_in, 16 * n_tables)
            act.activation(csig[:], cond[:], ACT.Sigmoid).then_inc(silu_half, 1)

        @blk.vector
        def _(v):
            ch = Chain(v, dve_chain)
            t = lambda i: tmp[:, i, 0:NP]
            tt, ts = v.tensor_tensor, v.tensor_scalar

            def exp(out, x, p1, p2, p3, pi):
                ch(ts(p1, x, -87.0, 88.0, ALU.max, ALU.min))
                ch(ts(p2, p1, 1.0 / math.log(2.0), MAG + 127.0, ALU.mult, ALU.add))
                ch(ts(p3, p2, MAG + 127.0, None, ALU.subtract))
                ch(ts(pi, p2.bitcast(I32), 23, None, ALU.logical_shift_left))
                ch(v.scalar_tensor_tensor(p1, p3, -0.693359375, p1, ALU.mult, ALU.add))
                ch(v.scalar_tensor_tensor(p1, p3, 2.12194440e-4, p1, ALU.mult, ALU.add))
                ch(ts(p2, p1, 1.0 / 5040, None, ALU.mult))
                for k in (720, 120, 24, 6, 2, 1):
                    ch(v.scalar_tensor_tensor(p2, p2, 1.0 / k, p1, ALU.add, ALU.mult))
                ch(ts(p2, p2, 1.0, None, ALU.add))
                ch(tt(out, p2, pi.bitcast(F32), ALU.mult))

            v.wait_ge(small_in, 48)
            dt = tmp[:, 11, 0:1]
            exp(dt, logdt[:], tmp[:, 8, 0:1], tmp[:, 9, 0:1], tmp[:, 10, 0:1], tmpi[:, 0:1])
            ch(ts(t(4), lamr[:], dt, None, ALU.mult))
            exp(t(5), t(4), t(8), t(9), t(10), tmpi[:])
            ch(ts(t(0), lami[:], dt, None, ALU.mult))
            ch(ts(t(8), t(0), 1.0 / (2 * math.pi), MAG, ALU.mult, ALU.add))
            ch(ts(t(8), t(8), MAG, None, ALU.subtract))
            c1 = 6.28125
            c2 = float(np.float32(2 * math.pi - c1))
            c2 = float(np.round(c2 * 2 ** 19) / 2 ** 19)
            for cc in (c1, c2, 2 * math.pi - c1 - c2):
                ch(v.scalar_tensor_tensor(t(0), t(8), -cc, t(0), ALU.mult, ALU.add))
            lim = float(np.float32(3.1415925))
            ch(ts(t(0), t(0), -lim, lim, ALU.max, ALU.min))
            ch(v.scalar_tensor_tensor(t(2), t(0), -1.0, t(0), ALU.mult, ALU.min))
            t2 = ts(t(2), t(2), math.pi / 2, None, ALU.add)
            t2.then_inc(angle_ready, 1)
            v.wait_ge(trig_done, 2)
            v.memset(ar[:, 0, :], 1.0)
            v.memset(ai[:, 0, :], 0.0)
            tt(ar[:, 1, :], t(5), t(3), ALU.mult)
            ch(tt(ai[:, 1, :], t(5), t(1), ALU.mult))

            def cmul(outr, outi, xr, xi, yr, yi, w):
                p = [tmp[:, i, 0:w * NP] if w == 1 else tmp[:, i, 0:w * NP].rearrange("g (w p) -> g w p", w=w)
                     for i in (6, 7, 8, 9)]
                tt(p[0], xr, yr, ALU.mult)
                tt(p[1], xi, yi, ALU.mult)
                tt(p[2], xr, yi, ALU.mult)
                ch(tt(p[3], xi, yr, ALU.mult))
                tt(outr, p[0], p[1], ALU.subtract)
                ch(tt(outi, p[2], p[3], ALU.add))

            for w in (1, 2, 4):
                b = lambda x: x[:, w:w + 1, :].to_broadcast([G, w, NP]) if w > 1 else x[:, 1, :]
                s = lambda x: x[:, 1:w + 1, :] if w > 1 else x[:, 1, :]
                o = lambda x: x[:, w + 1:2 * w + 1, :] if w > 1 else x[:, 2, :]
                cmul(o(ar), o(ai), b(ar), b(ai), s(ar), s(ai), w)

            def unit(r, i):
                tt(t(6), r, r, ALU.mult)
                ch(tt(t(7), i, i, ALU.mult))
                ch(tt(t(6), t(6), t(7), ALU.add))
                ch(ts(t(6), t(6), -0.5, 1.5, ALU.mult, ALU.add))
                tt(r, r, t(6), ALU.mult)
                ch(tt(i, i, t(6), ALU.mult))

            unit(t(3), t(1))
            xr, xi = t(3), t(1)
            for k in range(3 + NROT - 1):
                o = (t(3), t(1)) if k < 2 else (rc[:, k - 2, :], rs[:, k - 2, :])
                cmul(o[0], o[1], xr, xi, xr, xi, 1)
                unit(*o)
                xr, xi = o
            for _ in range(3):
                ch(tt(t(5), t(5), t(5), ALU.mult))
            tt(t(6), lamr[:], lamr[:], ALU.mult)
            ch(tt(t(7), lami[:], lami[:], ALU.mult))
            ch(tt(t(6), t(6), t(7), ALU.add))
            ts(t(8), ar[:, 1, :], -1.0, None, ALU.add)
            ch(v.reciprocal(t(6), t(6)))
            tt(t(0), t(8), lamr[:], ALU.mult)
            tt(t(1), ai[:, 1, :], lami[:], ALU.mult)
            tt(t(2), ai[:, 1, :], lamr[:], ALU.mult)
            ch(tt(t(3), t(8), lami[:], ALU.mult))
            tt(t(0), t(0), t(1), ALU.add)
            ch(tt(t(2), t(2), t(3), ALU.subtract))
            tt(t(0), t(0), t(6), ALU.mult)
            ch(tt(t(2), t(2), t(6), ALU.mult))
            lo, hi = slice(0, NP), slice(NP, P)
            for half in (lo, hi):
                v.tensor_copy(rows[:, 0:NPOW, half], ar[:])
                v.tensor_copy(rows[:, ROTC:ROTC + NROT, half], rc[:])
                v.tensor_copy(rows[:, R8, half], t(5))
                v.tensor_copy(rows[:, ERD, half], t(0))
            ts(rows[:, IMP:IMP + NPOW, lo], ai[:], -1.0, None, ALU.mult)
            v.tensor_copy(rows[:, IMP:IMP + NPOW, hi], ai[:])
            v.tensor_copy(rows[:, ROTS:ROTS + NROT, lo], rs[:])
            ts(rows[:, ROTS:ROTS + NROT, hi], rs[:], -1.0, None, ALU.mult)
            ts(rows[:, EIS, lo], t(2), -1.0, None, ALU.mult)
            ch(v.tensor_copy(rows[:, EIS, hi], t(2)))
            v.wait_ge(tables_in, 16 * n_tables)
            ts(crow[:, :, NP:P], crow[:, :, NP:P], -1.0, None, ALU.mult)
            ch(ts(crowx[:, :, 0:NP], crowx[:, :, 0:NP], -1.0, None, ALU.mult))
            v.wait_ge(silu_half, 1)
            tt(cond[:], cond[:], csig[:], ALU.mult).then_inc(params_ready, 1)
            k = 0

            def out(dst, src):
                nonlocal k
                k += 1
                v.wait_ge(turned, k)
                v.tensor_copy(dst, src).then_inc(turned_out, 1)

            for j in range(5):
                w = min(8, NPT - 8 * j)
                out(m.pt[:, 8 * j:8 * j + w, :], m.ps[:, j, 0:w * G].rearrange("p (n g) -> p n g", g=G))
            out(m.sct[:], m.ps[:, 5, 0:KT * NC9].rearrange("p (k b) -> p k b", b=NC9))
            out(m.bat[:], m.ps[:, 6, 0:112])
            out(m.lnt[:], m.ps[:, 7, 0:65])
            for j in range(3):
                out(fdist[:, j * 384:(j + 1) * 384], m.ps[0:H, j, 0:384])
            for j in range(2):
                out(bst0[:, 8 * j:8 * j + 8, :], m.ps[:, 3 + j, :].rearrange("p (h g) -> p h g", g=G))
            for j in range(2):
                out(bsw0[:, 8 * j:8 * j + 8, :], m.ps[:, 5 + j, :].rearrange("p (h g) -> p h g", g=G))
            for j in range(2):
                out(m.cst[:, 4 * j:4 * j + 4, :], m.ps[:, j, :].rearrange("p (t q) -> p t q", q=P))
            for j in range(2):
                out(m.csx[:, 4 * j:4 * j + 4, :], m.ps[:, 3 + j, :].rearrange("p (t q) -> p t q", q=P))
            out(m.h0s[:].rearrange("p b g -> p (b g)"), m.ps[:, 5, :])
            out(m.h0x[:].rearrange("p b g -> p (b g)"), m.ps[:, 6, :])
            v.wait_ge(turned_out, k)
            bc = lambda n: m.pt[:, n:n + 1, :].rearrange("p o g -> p g o").to_broadcast([P, G, GC])
            b0, bx = bst0[:].rearrange("p h g -> p g h"), bsw0[:].rearrange("p h g -> p g h")
            tt(m.bst[:], b0, bc(ERD), ALU.mult)
            tt(m.bsw[:], bx, bc(ERD), ALU.mult)
            ch(tt(mix[:], bx, bc(EIS), ALU.mult))
            ch(tt(m.bst[:], m.bst[:], mix[:], ALU.add))
            ch(tt(mix[:], b0, bc(EIS), ALU.mult))
            ch(tt(m.bsw[:], m.bsw[:], mix[:], ALU.subtract))
            for n in range(L):
                v.tensor_copy(m.ptr[:, n, :], m.pt[:, L - 1 - n, :])
                v.tensor_copy(m.ptr[:, L + n, :], m.pt[:, IMP + L - 1 - n, :])
            ch(tt(m.dskipd[:], m.ident[0:GC, 0:GC].rearrange("h (o j) -> h o j", o=1).to_broadcast([GC, G, GC]),
                  m.dskip[:].rearrange("h (g o) -> h g o", o=1).to_broadcast([GC, G, GC]), ALU.mult))

        @blk.tensor
        def _(pe):
            pe.wait_ge(tables_in, 16 * n_tables)
            pe.wait_ge(params_ready, 1)
            idg = m.ident[0:G, 0:G]
            for j in range(5):
                for n in range(8 * j, min(8 * j + 8, NPT)):
                    q = pe.transpose(m.ps[:, j, (n % 8) * G:(n % 8 + 1) * G], rows[:, n, :], idg)
                q.then_inc(turned, 1)
            for k in range(KT):
                q = pe.transpose(m.ps[:, 5, k * NC9:(k + 1) * NC9], cond[:, k * P:(k + 1) * P], m.ident[0:NC9, 0:NC9])
            q.then_inc(turned, 1)
            pe.transpose(m.ps[:, 6, 0:112], brows1[:], m.ident[0:112, 0:112]).then_inc(turned, 1)
            pe.transpose(m.ps[:, 7, 0:65], brows2[:], m.ident[0:65, 0:65]).then_inc(turned, 1)
            pe.wait_ge(relx_set, 4)
            for j in range(3):
                pe.wait_ge(turned_out, j + 1)
                pe.matmul(m.ps[0:H, j, 0:384], relx[:], onehot[:, j * 384:(j + 1) * 384],
                          start=True, stop=True).then_inc(turned, 1)
            for first, src, free in ((3, brow, 5), (5, browx, 7)):
                pe.wait_ge(turned_out, free)
                for j in range(2):
                    for h in range(8):
                        q = pe.transpose(m.ps[:, first + j, h * G:(h + 1) * G], src[:, :, 8 * j + h], idg)
                    q.then_inc(turned, 1)
            for first, src, free in ((0, crow, 10), (3, crowx, 13)):
                pe.wait_ge(turned_out, free)
                for j in range(2):
                    for t in range(4):
                        q = pe.transpose(m.ps[:, first + j, t * P:(t + 1) * P], src[:, 4 * j + t, :], m.ident[:])
                    q.then_inc(turned, 1)
            for bank, src in ((5, hrow), (6, hrowx)):
                pe.wait_ge(turned_out, 15)
                for t in range(4):
                    q = pe.transpose(m.ps[:, bank, t * P:(t + 1) * P], src[:, t, :], m.ident[:])
                q.then_inc(turned, 1)


def ada_block(nc, a, m):
    NSL = D // WC
    with ExitStack() as c:
        sb = lambda n, s, d=F32: c.enter_context(nc.sbuf_tensor(n, s, d, side="right"))
        wada = sb("wada", [P, 2 * NSL, KT, WC])
        signal = c.enter_context(semaphores(nc))
        S = lambda n: signal(n)
        landed = [S(f"a_landed{i}") for i in range(2 * NSL)]
        used, stored, dve_chain = S("a_used"), S("a_stored"), S("a_dve")
        spread_done, spread_out, rows_ready = S("a_spread"), S("a_spread_out"), S("a_rows")
        xs_in, xs_done, xs_out = S("a_xs_in"), S("a_xs_done"), S("a_xs_out")
        sshift, sscale, xs = sb("sshift", [NB, D]), sb("sscale", [NB, D]), sb("xs", [NB, ST, D])
        rows, copied, turned = sb("a_row", [NC9, 2, D]), S("a_copied"), S("a_turned")
        blk = c.enter_context(nc.Block())
        runs = [(a["w_ada"][0], 0, 3), (a["w_ada"][1], 3, 3), (a["w_ada_kv"], 6, 1)]

        def loads(queue, parity):
            for src, first, pairs in runs:
                view = src.rearrange("(k p) n -> p k n", p=P)
                with queue.Fori(0, pairs) as i:
                    for s in range(parity, 2 * NSL, 2):
                        queue.wait_ge(used, (i + first) * (2 * NSL) + s + 1)
                        queue.dma_start(wada[:, s], view[:, :, bass.ds(i * (2 * D) + s * WC, WC)]).then_inc(landed[s], 16)

        @blk.scalar
        def _(act):
            loads(act, 1)

        @blk.sync
        def _(sp):
            sp.dma_start(xs[:], a["x_sample"]).then_inc(xs_in, 16)
            loads(sp, 0)
            sp.wait_ge(xs_done, 1)
            sp.dma_start(a["s_xs"], xs[:]).then_inc(xs_out, 16)
            sp.wait_ge(xs_out, 16)

        @blk.tensor
        def _(pe):
            pe.sem_inc(used, 2 * NSL)
            for _, first, pairs in runs:
                with pe.Fori(0, pairs) as i:
                    for j in range(2):
                        for s in range(NSL):
                            slot = j * NSL + s
                            pe.wait_ge(landed[slot], (i + first + 1) * 16)
                            for k in range(KT):
                                q = pe.matmul(m.ps[0:NC9, 2 * j + s // 2, (s % 2) * WC:(s % 2 + 1) * WC],
                                              m.sct[:, k, :], wada[:, slot, k, :], start=(k == 0), stop=(k == KT - 1))
                            q.then_inc(used, 1)
                    for j in range(2):
                        n = (i + first) * 2 + j
                        pe.wait_ge(copied, n + 1)
                        pe.wait_ge(stored, n + 1)
                        for t in range(KT):
                            q = pe.matmul(m.ps[:, 4 + j, t * NC9:(t + 1) * NC9], rows[:, j, t * P:(t + 1) * P],
                                          m.ident[0:NC9, 0:NC9], start=True, stop=True)
                        q.then_inc(turned, 1)
            pe.wait_ge(rows_ready, 1)
            for g in range(GB):
                q = pe.matmul(m.ps[:, 2, g * 16:(g + 1) * 16], m.select[:, g * P:(g + 1) * P],
                              m.modt[:, 0:16, 0], start=True, stop=True)
            q.then_inc(spread_done, 1)
            for j in range(2):
                for t in range(KT):
                    q = pe.transpose(m.ps[0:NB, 3 + 2 * j + t // 4, (t % 4) * P:(t % 4 + 1) * P],
                                     m.modt[:, j * KT + t, 1:NC9], m.ident[:])
                q.then_inc(spread_done, 1)

        @blk.vector
        def _(v):
            ch = Chain(v, dve_chain)
            tt, ts = v.tensor_tensor, v.tensor_scalar
            v.sem_inc(stored, 2)
            for _, first, pairs in runs:
                with v.Fori(0, pairs) as i:
                    for j in range(2):
                        v.wait_ge(used, ((i + first) * 2 + j) * NSL + 3 * NSL)
                        v.tensor_copy(rows[:, j, :], m.ps[0:NC9, 2 * j:2 * j + 2, :].rearrange("b u f -> b (u f)")
                                      ).then_inc(copied, 1)
                    for j in range(2):
                        n = (i + first) * 2 + j
                        v.wait_ge(turned, n + 1)
                        tt(m.modt[:, bass.ds(n * KT, KT), :],
                           m.ps[:, 4 + j, 0:KT * NC9].rearrange("p (t b) -> p t b", b=NC9),
                           m.bat[:, bass.ds(n * KT, KT)].rearrange("p (t o) -> p t o", o=1)
                           .to_broadcast([P, KT, NC9]), ALU.add).then_inc(stored, 1)
            v.wait_ge(stored, 2 + NMOD)
            md = lambda j, w=1: m.modt[:, j * KT:(j + w) * KT, :]
            for j, w in ((1, 2), (4, 2), (7, 2), (10, 2)):
                ts(md(j, w), md(j, w), 1.0, None, ALU.add)
            ts(md(13), md(13), 1.0, None, ALU.add).then_inc(rows_ready, 1)
            v.wait_ge(rows_ready, 1)
            for n, scale, shift in ((0, 4, 3), (1, 13, 12), (2, 10, 9)):
                g = m.lnt[:, n * KT:(n + 1) * KT].rearrange("p (t o) -> p t o", o=1).to_broadcast([P, KT, NC9])
                b = m.lnt[:, 32 + n * KT:32 + (n + 1) * KT].rearrange("p (t o) -> p t o", o=1).to_broadcast([P, KT, NC9])
                tt(m.cs[:, n], md(scale), g, ALU.mult)
                ch(tt(m.cb[:, n], md(scale), b, ALU.mult))
                ch(tt(m.cb[:, n], m.cb[:, n], md(shift), ALU.add))
            ts(m.cs[:, 3], md(7), 1.0 / ALPHA, None, ALU.mult)
            v.tensor_copy(m.cb[:, 3], md(6))
            ts(m.lna[:, 0:24], m.lnt[:, 0:24], ALPHA, None, ALU.mult)
            ts(m.lna[:, 32:56], m.lnt[:, 32:56], ALPHA, None, ALU.mult)
            v.tensor_copy(m.lna[:, 24:32], m.lnt[:, 24:32])
            v.tensor_copy(m.lna[:, 56:64], m.lnt[:, 56:64])
            v.wait_ge(spread_done, 1)
            for j in range(2):
                v.tensor_copy(m.spread[:, j, :].rearrange("p (t g) -> p t g", g=GB),
                              m.ps[:, 2, 0:GB * 16].rearrange("p (g j t) -> p j t g", g=GB, j=2)[:, j])
            for j, dst in ((0, sshift), (1, sscale)):
                v.wait_ge(spread_done, j + 2)
                q = v.tensor_copy(dst[:], m.ps[0:NB, 3 + 2 * j:5 + 2 * j, :].rearrange("b u f -> b (u f)"))
            ch(q)
            v.wait_ge(xs_in, 16)
            wide = lambda x: x[:].rearrange("b (o f) -> b o f", o=1).to_broadcast([NB, ST, D])
            ch(tt(xs[:], xs[:], wide(sscale), ALU.mult))
            tt(xs[:], xs[:], wide(sshift), ALU.add).then_inc(xs_done, 1)


def ssm_block(nc, a, m):
    with ExitStack() as c:
        sb = lambda n, s, d=F32: c.enter_context(nc.sbuf_tensor(n, s, d, side="right"))
        signal = c.enter_context(semaphores(nc))
        S = lambda n: signal(n)
        NU = NCK + NB
        xnat, xsh, xsg = sb("xnat", [P, L, P]), sb("xsh", [NB, L, P]), sb("xsg", [NB, GB, P])
        regrouped = S("s_regrouped")
        u, w, wx = sb("u", [P, GB, NU]), sb("w", [P, GB, P]), sb("wx", [P, GB, P])
        wt, v1, v2 = sb("wt", [P, GB, L, GC]), sb("v1", [P, GB, NPOW, GC]), sb("v2", [P, GB, L, GC])
        bcur, h0cur, h0xcur = sb("bcur", [P, GB, GC]), sb("h0cur", [P, GB, NB]), sb("h0xcur", [P, GB, NB])
        kb, tz = sb("kb", [GC, GB, (2 * L - 1) * GC]), sb("tz", [P, GB, P])
        ec, es = sb("ec", [P, GB, NCK]), sb("es", [P, GB, NCK])
        rt1, rt2, rt3 = (sb(f"rt{n}", [P, GB, NCK // 2]) for n in (1, 2, 3))
        tg, xm, xs = sb("tg", [P, GB, NPOW * GC]), sb("xm", [P, GB, NCK]), sb("xs_", [P, GB, NCK])
        pb, qb = sb("pb", [P, GB, NCK + 1]), sb("qb", [P, GB, NCK + 1])
        gys = sb("gys", [NB, ST, P])
        gy = xnat
        pend, qend, ss = sb("pend", [P, G]), sb("qend", [P, G]), sb("ss", [P, NB, G])
        sout = tg[0:G].rearrange("g a b -> g (a b)").rearrange("g (n q) -> g n q", q=P)
        x_in, xs_in, tz_in, st_out = S("s_x_in"), S("s_xs_in"), S("s_tz_in"), S("s_st_out")
        y_done = S("s_y_done")
        u_turned, w_turned, k_done, xx_done, g_turned, st_done = (
            S("s_u_turned"), S("s_w_turned"), S("s_k_done"), S("s_xx_done"), S("s_g_turned"), S("s_st_done"))
        u_out, w_out, gelu_out, g_hi = S("s_u_out"), S("s_w_out"), S("s_gelu"), S("s_g_hi")
        gen, kb_ready, pq_ready, xs_out, g_lo, st_copied = (S("s_gen"), S("s_kb"), S("s_pq"), S("s_xs_out"), S("s_g_lo"), S("s_st_cp"))
        rot_ready, rot_used, zero_ready = S("s_rot"), S("s_rot_used"), S("s_zero")
        dve_chain, pool_chain = S("s_dve"), S("s_pool")
        blk = c.enter_context(nc.Block())

        @blk.sync
        def _(sp):
            xin = a["x_prompt"][0].rearrange("(c t) f -> c t f", t=L)
            sp.wait_ge(zero_ready, 5)
            with sp.Fori(0, KT) as i:
                cols = bass.ds(i * P, P)
                sp.wait_ge(g_turned, i + 1)
                sp.dma_start(xnat[:], xin[:, :, cols]).then_inc(x_in, 16)
                sp.dma_start(xsh[:, ST:L, :], a["s_xs"][:, :, cols]).then_inc(xs_in, 16)
                sp.wait_ge(kb_ready, i + 1)
                sp.wait_ge(y_done, i + 1)
                for s in range(L):
                    sp.dma_start(tz[s * GC:(s + 1) * GC, :, :],
                                 kb[:, :, (L - 1 - s) * GC:(L - 1 - s) * GC + P]).then_inc(tz_in, 16)
            sp.wait_ge(st_copied, 2)
            for half, re in ((0, "re"), (1, "im")):
                cols = slice(half * NP, (half + 1) * NP)
                sp.dma_start(a[f"o_ssm_{re}_prompt"][0, 0], sout[:, 0, cols]).then_inc(st_out, 16)
                sp.dma_start(a[f"o_ssm_{re}_sample"][0].rearrange("b g p -> g b p"),
                             sout[:, 1:NC9, cols]).then_inc(st_out, 16)
            sp.wait_ge(st_out, 64)

        @blk.gpsimd
        def _(pool):
            ch = Chain(pool, pool_chain)
            zeros = [(xsh[:, 0:ST, :], 0.0), (kb[:], 0.0), (pb[:, :, 0:1], 0.0), (qb[:, :, 0:1], 0.0),
                     (es[:, :, 0:1], 0.0), (ec[:, :, 0:1], 1.0)]
            for n, (dst, value) in enumerate(zeros):
                pool.memset(dst, value).then_inc(zero_ready, 1)
                pool.wait_ge(zero_ready, n + 1)
            PER = 3 * NROT
            with pool.Fori(0, KT) as i:
                ch.turn(i, PER)
                pool.wait_ge(rot_used, i + 1)
                for k in range(NROT):
                    n = 1 << k
                    rot = lambda r: m.pt[:, r + k, bass.ds(i * GB, GB)].rearrange("p (g o) -> p g o", o=1).to_broadcast([P, GB, n])
                    c0, s0, c1, s1 = ec[:, :, 0:n], es[:, :, 0:n], ec[:, :, n:2 * n], es[:, :, n:2 * n]
                    pool.tensor_tensor(rt1[:, :, 0:n], c0, rot(ROTC), ALU.mult)
                    ch(pool.tensor_tensor(rt2[:, :, 0:n], s0, rot(ROTS), ALU.mult))
                    pool.tensor_tensor(c1, rt1[:, :, 0:n], rt2[:, :, 0:n], ALU.subtract)
                    pool.tensor_tensor(s1, c0, rot(ROTS), ALU.mult)
                    ch(pool.tensor_tensor(rt3[:, :, 0:n], s0, rot(ROTC), ALU.mult))
                    q = pool.tensor_tensor(s1, s1, rt3[:, :, 0:n], ALU.add)
                    ch(q)
                pool.sem_inc(rot_ready, 1)
            assert ch.n == PER

        @blk.scalar
        def _(act):
            act.wait_ge(zero_ready, 6)
            with act.Fori(0, KT) as i:
                act.wait_ge(x_in, i * 16 + 16)
                act.wait_ge(xs_in, i * 16 + 16)
                act.copy(wx[:].rearrange("c g (t h) -> c g t h", h=GC), xnat[:].rearrange("c t (g h) -> c g t h", h=GC))
                act.copy(xsg[:].rearrange("c g (t h) -> c g t h", h=GC),
                         xsh[:].rearrange("c t (g h) -> c g t h", h=GC)).then_inc(regrouped, 1)
                act.wait_ge(u_turned, i + 1)
                for g in range(GB):
                    act.activation(u[:, g, 0:NCK], m.ps[:, g // 4, (g % 4) * P:(g % 4 + 1) * P], ACT.Identity,
                                   scale=m.spread[:, 1, bass.ds(i * GB + g, 1)], bias=m.spread[:, 0, bass.ds(i * GB + g, 1)])
                act.copy(u[:, :, NCK:NU],
                         m.ps[:, 6, 0:GB * NB].rearrange("p (g b) -> p g b", b=NB)).then_inc(u_out, 1)
                act.wait_ge(w_turned, i + 1)
                act.copy(w[:], m.ps[:, 4:6, :].rearrange("p u (g q) -> p (u g) q", q=P))
                for h in range(2):
                    q = act.copy(wx[:, :, h * NP:(h + 1) * NP],
                                 m.ps[:, 4:6, :].rearrange("p u (g q) -> p (u g) q", q=P)[:, :, (1 - h) * NP:(2 - h) * NP])
                q.then_inc(w_out, 1)
                act.wait_ge(y_done, i + 2)
                act.activation(gy[:].rearrange("c t (g h) -> c g t h", h=GC),
                               m.ps[:, 4:6, :].rearrange("c u (g t h) -> c (u g) t h", h=GC, t=L), ACT.Gelu_apprx_tanh)
                act.activation(gys[:].rearrange("b t (g h) -> b g t h", h=GC),
                               m.ps[0:NB, 7, :].rearrange("b (g t h) -> b g t h", h=GC, t=ST),
                               ACT.Gelu_apprx_tanh).then_inc(gelu_out, 1)
                act.wait_ge(g_turned, i + 2)
                act.copy(m.hhi[:, bass.ds(i, 1), 0:SEQ].rearrange("p o (c t) -> p (o t) c", t=L),
                         m.ps[:, 0:2, :].rearrange("p u (t c) -> p (u t) c", c=NCK))
                act.copy(m.hhi[:, bass.ds(i, 1), SEQ:NT].rearrange("p o (b t) -> p (o t) b", t=ST),
                         m.ps[:, 6, 0:NS].rearrange("p (t b) -> p t b", b=NB)).then_inc(g_hi, 1)

        @blk.tensor
        def _(pe):
            pe.sem_inc(g_turned, 1)
            pe.sem_inc(y_done, 1)
            bank = lambda b, g: m.ps[:, b + g // 4, (g % 4) * P:(g % 4 + 1) * P]
            with pe.Fori(0, KT) as i:
                pe.wait_ge(regrouped, i + 1)
                pe.wait_ge(g_lo, i + 1)
                for g in range(GB):
                    pe.transpose(bank(0, g), wx[:, g, :], m.ident[:])
                for g in range(GB):
                    q = pe.transpose(m.ps[:, 6, g * NB:(g + 1) * NB], xsg[:, g, :], m.ident[0:NB, 0:NB])
                q.then_inc(u_turned, 1)
                pe.wait_ge(gen, i + 1)
                for g in range(GB):
                    q = pe.transpose(bank(4, g), wt[:, g, :, :], m.ident[:])
                q.then_inc(w_turned, 1)
                pe.wait_ge(u_out, i + 1)
                for g in range(GB):
                    q = pe.matmul(m.ps[0:GC, 7 - g // 4, (g % 4) * P:(g % 4 + 1) * P], bcur[:, g, :], v1[:, g, 0:L, :],
                                  start=True, stop=True)
                q.then_inc(k_done, 1)
                pe.wait_ge(w_out, i + 1)
                for g in range(GB):
                    pe.matmul(bank(0, g), w[:, g, :], u[:, g, 0:NCK], start=True, stop=True)
                pe.wait_ge(xs_out, i + 1)
                for g in range(GB):
                    pe.matmul(bank(2, g), wx[:, g, :], u[:, g, 0:NCK], start=True, stop=True)
                pe.wait_ge(kb_ready, i + 1)
                for g in range(GB):
                    q = pe.matmul(m.ps[:, 6, g * NB:(g + 1) * NB], w[:, g, :], u[:, g, NCK:NU], start=True, stop=True)
                q.then_inc(xx_done, 1)
                pe.wait_ge(tz_in, i * (16 * L) + 16 * L)
                pe.wait_ge(pq_ready, i + 1)
                for g in range(GB):
                    pe.matmul(bank(4, g), u[:, g, 0:NCK], tz[:, g, :], start=True, stop=False)
                    pe.matmul(bank(4, g), pb[:, g, 0:NCK], v1[:, g, 1:NPOW, :], start=False, stop=False)
                    pe.matmul(bank(4, g), qb[:, g, 0:NCK], v2[:, g, :, :], start=False, stop=True)
                for g in range(GB):
                    out = m.ps[0:NB, 7, g * 64:(g + 1) * 64]
                    pe.matmul(out, u[:, g, NCK:NU], tz[:, g, 64:P], start=True, stop=False)
                    q = pe.matmul(out, h0cur[:, g, :], v1[:, g, 1:1 + ST, :], start=False, stop=True)
                q.then_inc(y_done, 1)
                pe.wait_ge(gelu_out, i + 1)
                pe.wait_ge(xs_out, i + 2)
                for t in range(L):
                    pe.transpose(bank(0, t), gy[:, t, :], m.ident[:])
                for t in range(ST):
                    q = pe.transpose(m.ps[:, 6, t * NB:(t + 1) * NB], gys[:, t, :], m.ident[0:NB, 0:NB])
                q.then_inc(g_turned, 1)
            pe.wait_ge(g_lo, KT + 1)
            pe.matmul(m.ps[0:G, 0, 0:P], pend[:], m.ident[:], start=True, stop=False)
            pe.matmul(m.ps[0:G, 0, 0:P], qend[:], m.swap[:], start=False, stop=True).then_inc(st_done, 1)
            for b in range(NB):
                q = pe.transpose(m.ps[0:G, 1 + b // 4, (b % 4) * P:(b % 4 + 1) * P], ss[:, b, :], m.ident[:])
            q.then_inc(st_done, 1)

        @blk.vector
        def _(v):
            ch = Chain(v, dve_chain)
            tt = v.tensor_tensor
            v.sem_inc(rot_used, 1)
            v.sem_inc(g_lo, 1)
            v.sem_inc(xs_out, 1)
            v.wait_ge(zero_ready, 6)
            PER = 11
            with v.Fori(0, KT) as i:
                ch.turn(i, PER)
                v.wait_ge(y_done, i + 1)
                gsl = bass.ds(i * GB, GB)
                pw = lambda first, n, rev=False: (m.ptr if rev else m.pt)[:, first:first + n, gsl].rearrange(
                    "p n (g o) -> p g n o", o=1).to_broadcast([P, GB, n, GC])
                bm = lambda x, n: x[:, gsl, :].rearrange("p g (o h) -> p g o h", o=1).to_broadcast([P, GB, n, GC])
                cm = lambda x, n: x[:, bass.ds(i, 1), :].rearrange("p o (g h) -> p g o h", h=GC).to_broadcast([P, GB, n, GC])
                tg9, tg8 = (tg[:, :, 0:n * GC].rearrange("p g (n h) -> p g n h", h=GC) for n in (NPOW, L))
                tt(wt[:], pw(0, L, True), bm(m.bst, L), ALU.mult)
                ch(tt(tg8, pw(L, L, True), bm(m.bsw, L), ALU.mult))
                ch(tt(wt[:], wt[:], tg8, ALU.add))
                tt(v1[:], pw(0, NPOW), cm(m.cst, NPOW), ALU.mult)
                ch(tt(tg9, pw(IMP, NPOW), cm(m.csx, NPOW), ALU.mult))
                ch(tt(v1[:], v1[:], tg9, ALU.subtract))
                tt(v2[:], pw(1, L), cm(m.csx, L), ALU.mult)
                ch(tt(tg8, pw(IMP + 1, L), cm(m.cst, L), ALU.mult))
                v.tensor_scalar(bcur[:], m.bst[:, gsl, :], 1.0, None, ALU.mult)
                v.tensor_copy(h0cur[:], m.h0s[:, :, gsl].rearrange("p b g -> p g b"))
                v.tensor_copy(h0xcur[:], m.h0x[:, :, gsl].rearrange("p b g -> p g b"))
                tt(v2[:], v2[:], tg8, ALU.add).then_inc(gen, 1)
                v.wait_ge(k_done, i + 1)
                v.tensor_copy(kb[:, 0:4, (L - 1) * GC:], m.ps[0:GC, 7, :].rearrange("h (g q) -> h g q", q=P))
                ch(v.tensor_copy(kb[:, 4:8, (L - 1) * GC:], m.ps[0:GC, 6, :].rearrange("h (g q) -> h g q", q=P)))
                tt(kb[:, :, (L - 1) * GC:L * GC], kb[:, :, (L - 1) * GC:L * GC], m.dskipd[:, gsl, :],
                   ALU.add).then_inc(kb_ready, 1)
                v.wait_ge(xx_done, i + 1)
                v.wait_ge(rot_ready, i + 1)
                banks = lambda b: m.ps[:, b:b + 2, :].rearrange("p u (g c) -> p (u g) c", c=NCK)
                tt(xs[:], banks(0), ec[:], ALU.mult)
                ch(tt(xm[:], banks(2), es[:], ALU.mult))
                ch(tt(xm[:], xs[:], xm[:], ALU.add))
                for g in range(GB):
                    q = v.tensor_tensor_scan(xs[:, g, :], m.pt[:, R8, bass.ds(i * GB + g, 1)].to_broadcast([P, NCK]),
                                             xm[:, g, :], 0.0, ALU.mult, ALU.add)
                ch(q)
                tt(pb[:, :, 1:NCK + 1], xs[:], ec[:], ALU.mult)
                q = tt(qb[:, :, 1:NCK + 1], xs[:], es[:], ALU.mult)
                q.then_inc(pq_ready, 1)
                v.wait_ge(pq_ready, i + 1)
                v.sem_inc(rot_used, 1)
                v.tensor_scalar(pend[:, gsl], pb[:, :, NCK], 1.0, None, ALU.mult)
                v.tensor_copy(qend[:, gsl], qb[:, :, NCK])
                p4 = lambda r: m.pt[:, r + ST, gsl].rearrange("p (g o) -> p g o", o=1).to_broadcast([P, GB, NB])
                t1, t2 = tg[:, :, 0:NB], tg[:, :, NB:2 * NB]
                tt(t1, h0cur[:], p4(0), ALU.mult)
                ch(tt(t2, h0xcur[:], p4(IMP), ALU.mult))
                ch(tt(t1, t1, t2, ALU.add))
                tt(ss[:, :, gsl].rearrange("p b g -> p g b"), t1,
                   m.ps[:, 6, 0:GB * NB].rearrange("p (g b) -> p g b", b=NB), ALU.add).then_inc(xs_out, 1)
                v.wait_ge(g_hi, i + 1)
                for dst, src in (
                    (lambda x: x[:, bass.ds(i, 1), 0:SEQ].rearrange("p o (c t) -> p (o t) c", t=L),
                     m.ps[:, 0:2, :].rearrange("p u (t c) -> p (u t) c", c=NCK)),
                    (lambda x: x[:, bass.ds(i, 1), SEQ:NT].rearrange("p o (b t) -> p (o t) b", t=ST),
                     m.ps[:, 6, 0:NS].rearrange("p (t b) -> p t b", b=NB))):
                    q = tt(dst(m.hlo), src, dst(m.hhi).bitcast(F32), ALU.subtract)
                q.then_inc(g_lo, 1)
            assert ch.n == PER, ch.n
            v.wait_ge(st_done, 1)
            v.tensor_copy(sout[:, 0, :], m.ps[0:G, 0, 0:P]).then_inc(st_copied, 1)
            v.wait_ge(st_done, 2)
            v.tensor_copy(sout[:, 1:NC9, :], m.ps[0:G, 1:3, :].rearrange("g u (b q) -> g (u b) q", q=P)).then_inc(st_copied, 1)


class Stream:

    def __init__(self, nc, c, name):
        sb = lambda n, d=F32: c.enter_context(nc.sbuf_tensor(f"{name}_{n}", [P, 2, KT * WC], d))
        self.raw, self.hi, self.lo = sb("wraw"), sb("whi", F32R), sb("wlo", F32R)

    def sems(self, nc, c, name):
        signal = c.enter_context(semaphores(nc))
        S = lambda n: signal(f"{name}_{n}")
        self.landed = [S("landed0"), S("landed1")]
        self.hi_ready, self.lo_ready = S("hi_ready"), S("lo_ready")

    def load(self, sp, n, slot, src, parts=KT):
        sp.wait_ge(self.hi_ready, n + 1)
        sp.wait_ge(self.lo_ready, n + 1)
        sp.dma_start(self.raw[:, slot].rearrange("p (k n) -> p k n", k=parts), src).then_inc(self.landed[slot], 16)

    def start_hi(self, act):
        act.sem_inc(self.hi_ready, 2)

    def cut_hi(self, act, slot, landed, done=None, count=None):
        act.wait_ge(self.landed[slot], landed)
        if done is not None:
            act.wait_ge(done, count)
        act.copy(self.hi[:, slot], self.raw[:, slot]).then_inc(self.hi_ready, 1)

    def start_lo(self, pool):
        pool.sem_inc(self.lo_ready, 2)

    def cut_lo(self, pool, n, slot):
        pool.wait_ge(self.hi_ready, n + 3)
        pool.tensor_tensor(self.lo[:, slot], self.raw[:, slot], self.hi[:, slot].bitcast(F32),
                           ALU.subtract).then_inc(self.lo_ready, 1)

    def wait_cut(self, pe, n):
        pe.wait_ge(self.lo_ready, n + 3)

    def parts(self, slot, k):
        return tuple(x[:, slot].rearrange("p (k n) -> p k n", k=k) for x in (self.hi, self.lo))


def three_pass(pe, out, lhs, rhs, first, last):
    pe.matmul(out, lhs[0], rhs[0], start=first, stop=False)
    pe.matmul(out, lhs[1], rhs[0], start=False, stop=False)
    return pe.matmul(out, lhs[0], rhs[1], start=False, stop=last)


def chunk(n):
    return slice(n * CH, (n + 1) * CH)


def gated_add(v, ch, m, src, gate, tile, n, free, tmp):
    w = LASTP if n == NCH - 1 else CH
    gp = m.modt[:, bass.ds(tile + gate * KT, 1), 0:1].rearrange("p o b -> p (o b)")
    xt = m.x[:, bass.ds(tile, 1), :].rearrange("p o t -> p (o t)")
    if n == NCH - 1:
        gs = m.modt[:, bass.ds(tile + gate * KT, 1), 1:NC9].rearrange("p o (b u) -> p (o b) u", u=1).to_broadcast([P, NB, ST])
        ch(v.tensor_tensor(tmp.rearrange("p (b t) -> p b t", t=ST), src[:, w:CH].rearrange("p (b t) -> p b t", t=ST),
                           gs, ALU.mult))
        ch(v.tensor_tensor(xt[:, SEQ:NT], xt[:, SEQ:NT], tmp, ALU.add))
    q = v.scalar_tensor_tensor(xt[:, n * CH:n * CH + w], src[:, 0:w], gp, xt[:, n * CH:n * CH + w], ALU.mult, ALU.add)
    if free is not None:
        q.then_inc(free, 1)


def residual_block(nc, a, m):
    with ExitStack() as c:
        rows = c.enter_context(nc.sbuf_tensor("r_rows", [P, 2, D], F32, side="right"))
        signal = c.enter_context(semaphores(nc))
        S = lambda n: signal(n)
        landed, turned, copied = [S("r_landed0"), S("r_landed1")], S("r_turned"), S("r_copied")
        blk = c.enter_context(nc.Block())
        tiles = [(a["x_prompt"][0, t * P:(t + 1) * P, :], P) for t in range(SEQ // P)]
        tiles.append((a["x_sample"].rearrange("b t f -> (b t) f"), NS))

        @blk.sync
        def _(sp):
            for t, (src, n) in enumerate(tiles):
                if t >= 2:
                    sp.wait_ge(turned, t - 1)
                sp.dma_start(rows[0:n, t % 2, :], src).then_inc(landed[t % 2], 16)

        @blk.tensor
        def _(pe):
            for t, (_, n) in enumerate(tiles):
                pe.wait_ge(landed[t % 2], 16 * (t // 2 + 1))
                if t >= 4:
                    pe.wait_ge(copied, t - 3)
                for k in range(KT):
                    q = pe.transpose(m.ps[:, 2 * (t % 4) + k // 4, (k % 4) * P:(k % 4) * P + n],
                                     rows[0:n, t % 2, k * P:(k + 1) * P], m.ident[0:n, 0:n])
                q.then_inc(turned, 1)

        @blk.scalar
        def _(act):
            for t, (_, n) in enumerate(tiles):
                act.wait_ge(turned, t + 1)
                act.mul(m.x[:, :, t * P:t * P + n],
                        m.ps[:, 2 * (t % 4):2 * (t % 4) + 2, :].rearrange("p u (k q) -> p (u k) q", q=P)[:, :, 0:n],
                        ALPHA).then_inc(copied, 1)


def glu_block(nc, a, m, st):
    with ExitStack() as c:
        sb = lambda n, s, d=F32: c.enter_context(nc.sbuf_tensor(n, s, d, side="right"))
        signal = c.enter_context(semaphores(nc))
        S = lambda n: signal(n)
        sig, prod, tmp = sb("g_sig", [P, 2, CH]), sb("g_prod", [P, 2, CH]), sb("g_tmp", [P, NS])
        st.sems(nc, c, "g")
        pair_done, sig_ready, pair_out, chain = S("g_pair"), S("g_sig_ready"), S("g_out"), S("g_dve")
        blk = c.enter_context(nc.Block())
        TURNS, PAIRS = D // WC, 2 * NCH
        halves = lambda x: [x[:, h * KT * P:(h + 1) * KT * P].rearrange("p (k n) -> p k n", n=P) for h in range(2)]

        @blk.sync
        def _(sp):
            with sp.Fori(0, TURNS) as i:
                for j in range(2):
                    sp.wait_ge(st.hi_ready, i * 2 + j + 1)
                    sp.wait_ge(st.lo_ready, i * 2 + j + 1)
                    for dst, src in zip(halves(st.raw[:, j]), (a["ssm_w_glu_a"], a["ssm_w_glu_b"])):
                        sp.dma_start(dst, src[0].rearrange("(k p) n -> p k n", p=P)[:, :, bass.ds(i * WC + j * P, P)]
                                     ).then_inc(st.landed[j], 16)

        @blk.gpsimd
        def _(pool):
            st.start_lo(pool)
            with pool.Fori(0, TURNS) as i:
                for j in range(2):
                    st.cut_lo(pool, i * 2 + j, j)

        @blk.scalar
        def _(act):
            def sigmoids(i, j):
                for p in range(j * NCH, (j + 1) * NCH):
                    act.wait_ge(pair_done, i * PAIRS + p + 1)
                    act.wait_ge(pair_out, i * PAIRS + p + 2)
                    act.activation(sig[:, p % 2], m.ps[:, 2 * (p % 3) + 1, 0:CH], ACT.Sigmoid).then_inc(sig_ready, 1)

            st.start_hi(act)
            for j in range(2):
                st.cut_hi(act, j, 32)
            with act.Fori(0, TURNS - 1) as i:
                for j in range(2):
                    sigmoids(i, j)
                    st.cut_hi(act, j, i * 32 + 64, pair_done, i * PAIRS + (j + 1) * NCH)
            for j in range(2):
                sigmoids(TURNS - 1, j)

        @blk.vector
        def _(v):
            ch = Chain(v, chain)
            v.sem_inc(pair_out, 3)
            with v.Fori(0, TURNS) as i:
                ch.turn(i, 4)
                for p in range(PAIRS):
                    v.wait_ge(sig_ready, i * PAIRS + p + 1)
                    v.tensor_tensor(prod[:, p % 2], m.ps[:, 2 * (p % 3), 0:CH], sig[:, p % 2],
                                    ALU.mult).then_inc(pair_out, 1)
                    v.wait_ge(pair_out, i * PAIRS + p + 4)
                    gated_add(v, ch, m, prod[:, p % 2], 2, i * 2 + p // NCH, p % NCH, None, tmp[:])
            assert ch.n == 4, ch.n

        @blk.tensor
        def _(pe):
            with pe.Fori(0, TURNS) as i:
                for p in range(PAIRS):
                    if p % NCH == 0:
                        st.wait_cut(pe, i * 2 + p // NCH)
                    pe.wait_ge(pair_out, i * PAIRS + p + 1)
                    hi, lo = halves(st.hi[:, p // NCH]), halves(st.lo[:, p // NCH])
                    for j in range(2):
                        for k in range(KT):
                            q = three_pass(pe, m.ps[:, 2 * (p % 3) + j, 0:CH], (hi[j][:, k], lo[j][:, k]),
                                           [x[:, k, chunk(p % NCH)] for x in (m.hhi, m.hlo)], k == 0, k == KT - 1)
                    q.then_inc(pair_done, 1)


def norm_block(nc, a, m, n, name):
    last = n == 3
    with ExitStack() as c:
        sb = lambda nn, s, d=F32: c.enter_context(nc.sbuf_tensor(name + nn, s, d, side="right"))
        signal = c.enter_context(semaphores(nc))
        S = lambda nn: signal(name + nn)
        work, std, rstd = sb("work", [P, NCH, KT, CH]), sb("std", [P, 2, CH]), sb("rstd", [P, 2, CH])
        mean_done, centred, squared, var_done = S("mean"), S("centred"), S("squared"), S("var")
        std_ready, scaled, h_ready, hi_ready, lo_ready, chain = (
            S("stdr"), S("scaled"), S("h"), S("hi"), S("lo"), S("dve"))
        blk = c.enter_context(nc.Block())
        coef = lambda x, o: x[:, n * KT + o:n * KT + o + 1]
        bank = lambda i, j: m.ps[:, (2 * i + j) % 6, 0:CH]

        @blk.tensor
        def _(pe):
            for i in range(NCH):
                for k in range(KT):
                    q = pe.matmul(bank(i, 0), m.ones[:], m.x[:, k, chunk(i)], start=(k == 0), stop=(k == KT - 1))
                q.then_inc(mean_done, 1)
            for i in range(NCH):
                pe.wait_ge(squared, i + 1)
                for k in range(KT):
                    q = pe.matmul(bank(i, 1), m.ones[:], work[:, i, k, :], start=(k == 0), stop=(k == KT - 1))
                q.then_inc(var_done, 1)

        @blk.scalar
        def _(act):
            for i in range(NCH):
                act.wait_ge(centred, i + 1)
                act.activation(work[:, i], m.x[:, :, chunk(i)], ACT.Square).then_inc(squared, 1)
            for i in range(NCH):
                act.wait_ge(var_done, i + 1)
                if i >= 2:
                    act.wait_ge(scaled, i - 1)
                act.activation(std[:, i % 2], bank(i, 1), ACT.Sqrt, bias=m.eps[:]).then_inc(std_ready, 1)
                if last:
                    continue
                act.wait_ge(scaled, i + 1)
                w = LASTP if i == NCH - 1 else CH
                for k in range(KT):
                    q = act.activation(work[:, i, k, 0:w], m.x[:, k, i * CH:i * CH + w], ACT.Identity,
                                       scale=m.cs[:, n, k, 0:1], bias=m.cb[:, n, k, 0:1])
                q.then_inc(h_ready, 1)
                if i == NCH - 1:
                    act.wait_ge(h_ready, NCH + 1)
                else:
                    act.wait_ge(h_ready, i + 1)
                act.copy(m.hhi[:, :, chunk(i)], work[:, i]).then_inc(hi_ready, 1)

        @blk.gpsimd
        def _(pool):
            if last:
                return
            for i in range(NCH):
                pool.wait_ge(hi_ready, i + 1)
                pool.tensor_tensor(m.hlo[:, :, chunk(i)], work[:, i], m.hhi[:, :, chunk(i)].bitcast(F32),
                                   ALU.subtract).then_inc(lo_ready, 1)
            pool.wait_ge(lo_ready, NCH)

        @blk.vector
        def _(v):
            ch = Chain(v, chain)
            wide = lambda x: x.rearrange("p (o t) -> p o t", o=1).to_broadcast([P, KT, CH])
            for i in range(NCH):
                v.wait_ge(mean_done, i + 1)
                v.tensor_tensor(m.x[:, :, chunk(i)], m.x[:, :, chunk(i)], wide(bank(i, 0)), ALU.subtract).then_inc(centred, 1)
            for i in range(NCH):
                v.wait_ge(std_ready, i + 1)
                ch(v.reciprocal(rstd[:, i % 2], std[:, i % 2]))
                v.wait_ge(squared, i + 1)
                v.tensor_tensor(m.x[:, :, chunk(i)], m.x[:, :, chunk(i)], wide(rstd[:, i % 2]), ALU.mult).then_inc(scaled, 1)
                if last:
                    v.wait_ge(scaled, i + 1)
                elif i < NCH - 1:
                    v.wait_ge(h_ready, i + 1)
                else:
                    v.wait_ge(scaled, i + 1)
                    four = lambda x: x[:, n, :, 1:NC9].rearrange("p k (b o) -> p k b o", o=1).to_broadcast([P, KT, NB, ST])
                    dst = work[:, i, :, LASTP:CH].rearrange("p k (b t) -> p k b t", t=ST)
                    ch(v.tensor_tensor(dst, m.x[:, :, SEQ:NT].rearrange("p k (b t) -> p k b t", t=ST), four(m.cs), ALU.mult))
                    v.tensor_tensor(dst, dst, four(m.cb), ALU.add).then_inc(h_ready, 1)
                    v.wait_ge(h_ready, NCH + 1)
                for k in range(KT):
                    q = v.tensor_scalar(m.x[:, k, chunk(i)], m.x[:, k, chunk(i)], coef(m.lna, k), coef(m.lna, 32 + k),
                                        ALU.mult, ALU.add)
            ch(q)


def remod_block(nc, a, m):
    with ExitStack() as c:
        work = c.enter_context(nc.sbuf_tensor("q_work", [P, 2, KT, CH], F32, side="right"))
        signal = c.enter_context(semaphores(nc))
        S = lambda n: signal("q_" + n)
        h_ready, s_ready, hi_ready, lo_ready, chain = S("h"), S("s"), S("hi"), S("lo"), S("dve")
        blk = c.enter_context(nc.Block())

        @blk.scalar
        def _(act):
            for i in range(NCH):
                if i >= 2:
                    act.wait_ge(lo_ready, i - 1)
                w = LASTP if i == NCH - 1 else CH
                for k in range(KT):
                    q = act.activation(work[:, i % 2, k, 0:w], m.x[:, k, i * CH:i * CH + w], ACT.Identity,
                                       scale=m.cs[:, 3, k, 0:1], bias=m.cb[:, 3, k, 0:1])
                q.then_inc(h_ready, 1)
                act.wait_ge(h_ready, i + 1)
                if i == NCH - 1:
                    act.wait_ge(s_ready, 1)
                act.copy(m.hhi[:, :, chunk(i)], work[:, i % 2]).then_inc(hi_ready, 1)

        @blk.gpsimd
        def _(pool):
            for i in range(NCH):
                pool.wait_ge(hi_ready, i + 1)
                pool.tensor_tensor(m.hlo[:, :, chunk(i)], work[:, i % 2], m.hhi[:, :, chunk(i)].bitcast(F32),
                                   ALU.subtract).then_inc(lo_ready, 1)

        @blk.vector
        def _(v):
            ch = Chain(v, chain)
            v.wait_ge(lo_ready, 1)
            four = lambda x: x[:, 3, :, 1:NC9].rearrange("p k (b o) -> p k b o", o=1).to_broadcast([P, KT, NB, ST])
            dst = work[:, 0, :, LASTP:CH].rearrange("p k (b t) -> p k b t", t=ST)
            ch(v.tensor_tensor(dst, m.x[:, :, SEQ:NT].rearrange("p k (b t) -> p k b t", t=ST), four(m.cs), ALU.mult))
            v.tensor_tensor(dst, dst, four(m.cb), ALU.add).then_inc(s_ready, 1)


def mlp_block(nc, a, m, st, layer):
    name = f"m{layer}_"
    with ExitStack() as c:
        sb = lambda n, s, d=F32: c.enter_context(nc.sbuf_tensor(name + n, s, d, side="right"))
        signal = c.enter_context(semaphores(nc))
        S = lambda n: signal(name + n)
        HK, TURNS = 4, 8
        khi, klo = sb("khi", [P, HK, NT], F32R), sb("klo", [P, HK, NT], F32R)
        relu, sq, tmp = sb("relu", [P, 2, CH]), sb("sq", [P, 2, CH]), sb("tmp", [P, NS])
        st.sems(nc, c, name)
        up_done, down_done, relu_ready, bank_free, hi_ready, hid_ready, chain = (
            S("up"), S("down"), S("relu_r"), S("free"), S("khi_r"), S("hid"), S("dve"))
        blk = c.enter_context(nc.Block())
        UP, DOWN = HK * NCH, KT * NCH
        w1 = a["mlp_w1"][layer].rearrange("(k p) n -> p k n", p=P)
        w2 = a["mlp_w2"][layer].rearrange("(k p) n -> p k n", p=P)

        @blk.sync
        def _(sp):
            with sp.Fori(0, TURNS) as e:
                for j in range(2):
                    st.load(sp, e * 4 + j, j, w1[:, :, bass.ds(e * (HK * P) + j * WC, WC)])
                for j in range(2):
                    st.load(sp, e * 4 + 2 + j, j, w2[:, bass.ds(e * HK, HK), j * 512:(j + 1) * 512], HK)

        @blk.gpsimd
        def _(pool):
            def lows(e, groups):
                for g in groups:
                    pool.wait_ge(hi_ready, e * UP + g + 1)
                    f, n = divmod(g, NCH)
                    pool.tensor_tensor(klo[:, f, chunk(n)], sq[:, g % 2], khi[:, f, chunk(n)].bitcast(F32),
                                       ALU.subtract).then_inc(hid_ready, 1)

            def turn(e, last):
                st.cut_lo(pool, e * 4 + 1, 1)
                lows(e, range(UP // 2))
                st.cut_lo(pool, e * 4 + 2, 0)
                lows(e, range(UP // 2, UP))
                st.cut_lo(pool, e * 4 + 3, 1)
                if not last:
                    st.cut_lo(pool, e * 4 + 4, 0)

            st.start_lo(pool)
            st.cut_lo(pool, 0, 0)
            with pool.Fori(0, TURNS - 1) as e:
                turn(e, False)
            turn(TURNS - 1, True)

        @blk.scalar
        def _(act):
            def squares(e, groups):
                for g in groups:
                    f, n = divmod(g, NCH)
                    act.wait_ge(up_done, e * UP + g + 1)
                    act.activation(relu[:, g % 2], m.ps[:, g % 6, 0:CH], ACT.Relu).then_inc(relu_ready, 1)
                    act.wait_ge(bank_free, e * (UP + DOWN) + g + 7)
                    act.copy(khi[:, f, chunk(n)], sq[:, g % 2]).then_inc(hi_ready, 1)

            def turn(e, last):
                st.cut_hi(act, 1, e * 32 + 16, down_done, e * DOWN + DOWN)
                squares(e, range(UP // 2))
                st.cut_hi(act, 0, e * 32 + 32, up_done, e * UP + UP // 2)
                squares(e, range(UP // 2, UP))
                st.cut_hi(act, 1, e * 32 + 32, up_done, e * UP + UP)
                if not last:
                    st.cut_hi(act, 0, e * 32 + 48, down_done, e * DOWN + DOWN + DOWN // 2)

            st.start_hi(act)
            st.cut_hi(act, 0, 16)
            with act.Fori(0, TURNS - 1) as e:
                turn(e, False)
            turn(TURNS - 1, True)

        @blk.vector
        def _(v):
            ch = Chain(v, chain)
            v.sem_inc(bank_free, 6)
            with v.Fori(0, TURNS) as e:
                ch.turn(e, 2 * KT)
                for g in range(UP):
                    v.wait_ge(relu_ready, e * UP + g + 1)
                    if g >= 2:
                        v.wait_ge(hid_ready, e * UP + g - 1)
                    v.scalar_tensor_tensor(sq[:, g % 2], m.ps[:, g % 6, 0:CH], 0.0, relu[:, g % 2], ALU.max,
                                           ALU.mult).then_inc(bank_free, 1)
                for g in range(DOWN):
                    v.wait_ge(down_done, e * DOWN + DOWN + g + 1)
                    gated_add(v, ch, m, m.ps[:, g % 6, 0:CH], 6 * layer + 5, g // NCH, g % NCH, bank_free, tmp[:])
            assert ch.n == 2 * KT, ch.n

        @blk.tensor
        def _(pe):
            pe.sem_inc(down_done, DOWN)
            with pe.Fori(0, TURNS) as e:
                for g in range(UP):
                    f, n = divmod(g, NCH)
                    if g % (UP // 2) == 0:
                        st.wait_cut(pe, e * 4 + f // 2)
                    w = st.parts(f // 2, KT)
                    cols = slice((f % 2) * P, (f % 2 + 1) * P)
                    pe.wait_ge(bank_free, e * (UP + DOWN) + g + 1)
                    for k in range(KT):
                        q = three_pass(pe, m.ps[:, g % 6, 0:CH], [x[:, k, cols] for x in w],
                                       [x[:, k, chunk(n)] for x in (m.hhi, m.hlo)], k == 0, k == KT - 1)
                    q.then_inc(up_done, 1)
                for g in range(DOWN):
                    t, n = divmod(g, NCH)
                    if g % (DOWN // 2) == 0:
                        st.wait_cut(pe, e * 4 + 2 + t // 4)
                    w = st.parts(t // 4, HK)
                    cols = slice((t % 4) * P, (t % 4 + 1) * P)
                    pe.wait_ge(bank_free, e * (UP + DOWN) + UP + g + 1)
                    for k in range(HK):
                        if t == 0:
                            pe.wait_ge(hid_ready, e * UP + k * NCH + n + 1)
                        q = three_pass(pe, m.ps[:, g % 6, 0:CH], [x[:, k, cols] for x in w],
                                       [x[:, k, chunk(n)] for x in (khi, klo)], k == 0, k == HK - 1)
                    q.then_inc(down_done, 1)


def column_block(nc, a, m, st, name, w, gate=None, dst=None):
    with ExitStack() as c:
        sb = lambda n, s, d=F32: c.enter_context(nc.sbuf_tensor(name + n, s, d, side="right"))
        signal = c.enter_context(semaphores(nc))
        S = lambda n: signal(name + n)
        stage, tmp = sb("stage", [P, 2, NT]), sb("tmp", [P, NS])
        st.sems(nc, c, name)
        done, bank_free, stored, staged, chain = S("done"), S("free"), [S("stored0"), S("stored1")], S("staged"), S("dve")
        blk = c.enter_context(nc.Block())
        TURNS, TPT = D // (2 * WC), 2 * WC // P
        GR = TPT * NCH
        wv = w.rearrange("(k p) n -> p k n", p=P)

        @blk.sync
        def _(sp):
            with sp.Fori(0, TURNS) as i:
                for j in range(2):
                    st.load(sp, i * 2 + j, j, wv[:, :, bass.ds(i * (2 * WC) + j * WC, WC)])

        @blk.gpsimd
        def _(pool):
            st.start_lo(pool)
            with pool.Fori(0, TURNS) as i:
                for j in range(2):
                    st.cut_lo(pool, i * 2 + j, j)

        @blk.scalar
        def _(act):
            st.start_hi(act)
            for j in range(2):
                st.cut_hi(act, j, 16)
            if dst is not None:
                act.sem_inc(stored[0], 16)
                act.sem_inc(stored[1], 16)

            def turn(i, last):
                for j in range(2):
                    for t in range(2 * j, 2 * j + 2) if dst is not None else ():
                        act.wait_ge(staged, i * TPT + t + 1)
                        act.dma_start(dst[bass.ds(i * TPT + t, 1), :, :].rearrange("o p t -> (o p) t"),
                                      stage[:, t % 2]).then_inc(stored[t % 2], 16)
                    if not last:
                        st.cut_hi(act, j, i * 16 + 32, done, i * GR + (j + 1) * GR // 2)

            with act.Fori(0, TURNS - 1) as i:
                turn(i, False)
            turn(TURNS - 1, True)
            if dst is not None:
                for t in range(2):
                    act.wait_ge(stored[t], 16 + 16 * TURNS * TPT // 2)

        @blk.vector
        def _(v):
            ch = Chain(v, chain)
            v.sem_inc(bank_free, 6)
            with v.Fori(0, TURNS) as i:
                ch.turn(i, 2 * TPT)
                for g in range(GR):
                    t, n = divmod(g, NCH)
                    v.wait_ge(done, i * GR + g + 1)
                    if dst is None:
                        gated_add(v, ch, m, m.ps[:, g % 6, 0:CH], gate, i * TPT + t, n, bank_free, tmp[:])
                    else:
                        if n == 0:
                            v.wait_ge(stored[t % 2], i * (16 * TPT // 2) + 16 * (t // 2) + 16)
                        q = v.tensor_copy(stage[:, t % 2, chunk(n)], m.ps[:, g % 6, 0:CH]).then_inc(bank_free, 1)
                        if n == NCH - 1:
                            v.wait_ge(bank_free, i * GR + g + 7)
                            v.sem_inc(staged, 1)

        @blk.tensor
        def _(pe):
            with pe.Fori(0, TURNS) as i:
                for g in range(GR):
                    t, n = divmod(g, NCH)
                    if g % (GR // 2) == 0:
                        st.wait_cut(pe, i * 2 + g // (GR // 2))
                    w_ = st.parts(t // 2, KT)
                    cols = slice((t % 2) * P, (t % 2 + 1) * P)
                    pe.wait_ge(bank_free, i * GR + g + 1)
                    for k in range(KT):
                        q = three_pass(pe, m.ps[:, g % 6, 0:CH], [x[:, k, cols] for x in w_],
                                       [x[:, k, chunk(n)] for x in (m.hhi, m.hlo)], k == 0, k == KT - 1)
                    q.then_inc(done, 1)


def kv_block(nc, a, m, st):
    name = "kv_"
    with ExitStack() as c:
        sb = lambda n, s, d=F32: c.enter_context(nc.sbuf_tensor(name + n, s, d, side="right"))
        signal = c.enter_context(semaphores(nc))
        S = lambda n: signal(name + n)
        TT = SEQ // P + 1
        stage = sb("stage", [P, 2, TT, WC])
        st.sems(nc, c, name)
        done, bank_free, stored, staged = S("done"), S("free"), [S("stored0"), S("stored1")], S("staged")
        blk = c.enter_context(nc.Block())
        GR = 2 * TT
        wv = a["w_kv"].rearrange("(k p) n -> p k n", p=P)
        outs = [(a["o_k_prompt"][0].rearrange("(t p) h c d -> p t (h c d)", p=P), a["o_k_sample"].rearrange("b t h c d -> (b t) (h c d)")),
                (a["o_v_prompt"][0].rearrange("(t p) h e -> p t (h e)", p=P), a["o_v_sample"].rearrange("b t h e -> (b t) (h e)"))]

        @blk.sync
        def _(sp):
            with sp.Fori(0, 4) as i:
                for j in range(2):
                    st.load(sp, i * 2 + j, j, wv[:, :, bass.ds(i * (2 * WC) + j * WC, WC)])

        @blk.gpsimd
        def _(pool):
            st.start_lo(pool)
            with pool.Fori(0, 4) as i:
                for j in range(2):
                    st.cut_lo(pool, i * 2 + j, j)

        @blk.scalar
        def _(act):
            act.sem_inc(stored[0], 32)
            act.sem_inc(stored[1], 32)
            st.start_hi(act)
            for j in range(2):
                st.cut_hi(act, j, 16)

            def store(n, col, j, out):
                act.wait_ge(staged, n + 1)
                act.dma_start(out[0][:, :, bass.ds(col, WC)], stage[:, j, 0:TT - 1, :]).then_inc(stored[j], 16)
                act.dma_start(out[1][:, bass.ds(col, WC)], stage[P - NS:P, j, TT - 1, :]).then_inc(stored[j], 16)

            def turn(half, i, last):
                for j in range(2):
                    n = i + 2 * half
                    if not last:
                        st.cut_hi(act, j, n * 16 + 32, done, n * GR + (j + 1) * TT)
                    store(n * 2 + j, i * (2 * WC) + j * WC, j, outs[half])

            with act.Fori(0, 2) as i:
                turn(0, i, False)
            turn(1, 0, False)
            turn(1, 1, True)
            for j in range(2):
                act.wait_ge(stored[j], 32 + 32 * 4)

        @blk.vector
        def _(v):
            v.sem_inc(bank_free, 6)
            with v.Fori(0, 4) as i:
                for g in range(GR):
                    j, t = divmod(g, TT)
                    if t == 0:
                        v.wait_ge(stored[j], i * 32 + 32)
                    v.wait_ge(done, i * GR + g + 1)
                    v.tensor_copy(stage[:, j, t, :], m.ps[:, g % 6, 0:WC]).then_inc(bank_free, 1)
                    if t == TT - 1:
                        v.wait_ge(bank_free, i * GR + g + 7)
                        v.sem_inc(staged, 1)

        @blk.tensor
        def _(pe):
            with pe.Fori(0, 4) as i:
                for g in range(GR):
                    j, t = divmod(g, TT)
                    if t == 0:
                        st.wait_cut(pe, i * 2 + j)
                    w_ = st.parts(j, KT)
                    first = t * P if t < TT - 1 else NT - P
                    pe.wait_ge(bank_free, i * GR + g + 1)
                    for k in range(KT):
                        q = three_pass(pe, m.ps[:, g % 6, 0:WC], [x[:, k, first:first + P] for x in (m.hhi, m.hlo)],
                                       [x[:, k, :] for x in w_], k == 0, k == KT - 1)
                    q.then_inc(done, 1)


def rms_block(nc, a, m):
    with ExitStack() as c:
        sb = lambda n, s, d=F32: c.enter_context(nc.sbuf_tensor("n_" + n, s, d, side="right"))
        signal = c.enter_context(semaphores(nc))
        S = lambda n: signal("n_" + n)
        o, sq, std, out = sb("o", [P, 2, NT]), sb("sq", [P, 2, NT]), sb("std", [P, 2, NT]), sb("out", [P, 2, NT])
        gain = sb("gain", [P, 1])
        landed, squared, summed, std_ready, ready, hi_ready, lo_ready, chain = (
            [S("landed0"), S("landed1")], S("sq_r"), S("sum"), S("std_r"), S("ready"), S("hi"), S("lo"), S("dve"))
        x_in = S("x_in")
        blk = c.enter_context(nc.Block())

        @blk.sync
        def _(sp):
            sp.dma_start(m.x[:], a["s_x"]).then_inc(x_in, 16)
            for t in range(KT):
                if t >= 2:
                    sp.wait_ge(ready, t - 1)
                sp.dma_start(o[:, t % 2], a["s_o"][t]).then_inc(landed[t % 2], 16)
            sp.wait_ge(x_in, 16)

        @blk.scalar
        def _(act):
            for t in range(KT):
                act.wait_ge(landed[t % 2], 16 * (t // 2 + 1))
                if t >= 2:
                    act.wait_ge(summed, t - 1)
                act.activation(sq[:, t % 2], o[:, t % 2], ACT.Square).then_inc(squared, 1)
                act.wait_ge(summed, t + 1)
                if t >= 2:
                    act.wait_ge(ready, t - 1)
                act.activation(std[:, t % 2].rearrange("p (n t) -> p n t", t=CH), m.ps[:, (t % 2) * 3:(t % 2) * 3 + 3, 0:CH],
                               ACT.Sqrt, bias=m.eps[:]).then_inc(std_ready, 1)
                act.wait_ge(ready, t + 1)
                act.copy(m.hhi[:, t], out[:, t % 2]).then_inc(hi_ready, 1)

        @blk.tensor
        def _(pe):
            for t in range(KT):
                pe.wait_ge(squared, t + 1)
                if t >= 2:
                    pe.wait_ge(std_ready, t - 1)
                for n in range(NCH):
                    q = pe.matmul(m.ps[:, (t % 2) * 3 + n, 0:CH], m.onesv[:], sq[:, t % 2, chunk(n)], start=True, stop=True)
                q.then_inc(summed, 1)

        @blk.vector
        def _(v):
            ch = Chain(v, chain)
            ch(v.tensor_scalar(gain[:], m.lnt[:, 64:65], 1.0 - LAM_INIT, None, ALU.mult))
            for t in range(KT):
                v.wait_ge(std_ready, t + 1)
                v.wait_ge(landed[t % 2], 16 * (t // 2 + 1))
                ch(v.reciprocal(std[:, t % 2], std[:, t % 2]))
                if t >= 2:
                    v.wait_ge(lo_ready, t - 1)
                v.scalar_tensor_tensor(out[:, t % 2], o[:, t % 2], gain[:, 0:1], std[:, t % 2], ALU.mult,
                                       ALU.mult).then_inc(ready, 1)

        @blk.gpsimd
        def _(pool):
            for t in range(KT):
                pool.wait_ge(hi_ready, t + 1)
                pool.tensor_tensor(m.hlo[:, t], out[:, t % 2], m.hhi[:, t].bitcast(F32), ALU.subtract).then_inc(lo_ready, 1)


def save_x_block(nc, a, m):
    with ExitStack() as c:
        saved = c.enter_context(nc.semaphore("x_saved"))
        blk = c.enter_context(nc.Block())

        @blk.sync
        def _(sp):
            sp.dma_start(a["s_x"], m.x[:]).then_inc(saved, 16)
            sp.wait_ge(saved, 16)


def rows_out_block(nc, a, m):
    with ExitStack() as c:
        rows = c.enter_context(nc.sbuf_tensor("y_rows", [P, 2, D], F32, side="right"))
        signal = c.enter_context(semaphores(nc))
        S = lambda n: signal("y_" + n)
        turned, copied, stored = S("turned"), S("copied"), [S("stored0"), S("stored1")]
        blk = c.enter_context(nc.Block())
        tiles = [(a["o_y_prompt"][0, t * P:(t + 1) * P, :], P) for t in range(SEQ // P)]
        tiles.append((a["o_y_sample"].rearrange("b t f -> (b t) f"), NS))

        @blk.tensor
        def _(pe):
            for t, (_, n) in enumerate(tiles):
                if t >= 4:
                    pe.wait_ge(copied, t - 3)
                for k in range(KT):
                    q = pe.transpose(m.ps[0:n, 2 * (t % 4) + k // 4, (k % 4) * P:(k % 4 + 1) * P],
                                     m.x[:, k, t * P:t * P + n], m.ident[:])
                q.then_inc(turned, 1)

        @blk.vector
        def _(v):
            for t, (_, n) in enumerate(tiles):
                v.wait_ge(turned, t + 1)
                if t >= 2:
                    v.wait_ge(stored[t % 2], 16 * (t // 2))
                v.tensor_copy(rows[0:n, t % 2], m.ps[0:n, 2 * (t % 4):2 * (t % 4) + 2, :].rearrange("p u q -> p (u q)")
                              ).then_inc(copied, 1)

        @blk.sync
        def _(sp):
            for t, (dst, n) in enumerate(tiles):
                sp.wait_ge(copied, t + 1)
                sp.dma_start(dst, rows[0:n, t % 2]).then_inc(stored[t % 2], 16)
            sp.wait_ge(stored[0], 16 * 5)
            sp.wait_ge(stored[1], 16 * 4)


def attention_block(nc, a, m):
    with ExitStack() as c:
        sb = lambda n, s, d=F32: c.enter_context(nc.sbuf_tensor("t_" + n, s, d, side="right"))
        signal = c.enter_context(semaphores(nc))
        S = lambda n: signal("t_" + n)
        QB = SEQ // P
        NK = PAST + NS
        R = 2 * NS
        SCALE = HD ** -0.5
        ptab = sb("ptab", [1, NB * NPG], I32)
        flip, comp = sb("flip", [P, P]), sb("comp", [R, 2])
        lamv, lamt, lams = sb("lamv", [P, 4 * HD]), sb("lamt", [P, HD]), sb("lams", [P, 2])
        neglam, rowlam = sb("neglam", [P, 1]), sb("rowlam", [R, 1])
        pastb, newb = sb("pastb", [R, PAST]), sb("newb", [R, 2 * NS - ST])
        newc, pause = sb("newc", [R, NS]), sb("pause", [P, 1])
        krows, kn, vn, qs = sb("krows", [NS, D]), sb("kn", [P, H, NS]), sb("vn", [P, D]), sb("qs", [P, H, NS])
        osam = sb("osam", [P, H, NS])
        kp, vp, ktp = sb("kp", [P, NPG, D]), sb("vp", [P, NPG, D]), sb("ktp", [P, H, PAST])
        qbd = sb("qbd", [P, H, 9 * 2 * ST])
        ls, smax, ssum, wtc = sb("ls", [R, NK]), sb("smax", [R, 3]), sb("ssum", [R, 2]), sb("wtc", [P, NPG + 1, NS])
        qh, kr, vh, bd = sb("qh", [P, 2, SEQ]), sb("kr", [P, 2, QB, P]), sb("vh", [P, 2, QB, P]), sb("bd", [P, 2, SEQ])
        kt, bias, oh = sb("kt", [P, SEQ]), sb("bias", [P, SEQ]), sb("oh", [P, SEQ])
        lg = [[sb(f"lg{s}{k}", [P, SEQ]) for k in range(2)] for s in range(2)]
        wt = sb("wt", [P, QB, P])
        mx, nmx, sums, rec = sb("mx", [P, 2, 2]), sb("nmx", [P, 2, 2]), sb("sums", [P, 2, 2]), sb("rec", [P, 2, 2])

        once_in, pt_in, once_ready, lam_exp, kn_done = S("once_in"), S("pt_in"), S("once"), S("lam_exp"), S("kn_done")
        kp_in, vp_in, head_in, out_done = S("kp_in"), S("vp_in"), [S("head_in0"), S("head_in1")], S("out")
        zeroed, qbd_ready, ktp_done, ktp_a, ktp_v = S("zeroed"), S("qbd"), S("ktp"), S("ktp_a"), S("ktp_v")
        s_done, s_soft, s_exp, s_norm, comb_done, comb_out, pv_done, pv_out = (
            S("s_done"), S("s_soft"), S("s_exp"), S("s_norm"), S("comb"), S("comb_out"), S("pv"), S("pv_out"))
        kt_done, kt_out, bias_done, bias_out = S("kt_done"), S("kt_out"), S("bias_done"), S("bias_out")
        qk_done, soft, exped, w_ready, wt_done, wt_out, o_done, o_out = (
            S("qk"), S("soft"), S("exped"), S("w"), S("wt_done"), S("wt_out"), S("o_done"), S("o_out"))
        osam_stored, chain = S("osam_stored"), S("dve")
        blk = c.enter_context(nc.Block())
        ck = a["cache_k"].rearrange("n p h c d -> n p (h c d)")
        cv = a["cache_v"].rearrange("n p h e -> n p (h e)")
        kview = a["o_k_prompt"][0].rearrange("(t p) h c d -> p t (h c d)", p=P)
        vview = a["o_v_prompt"][0].rearrange("(t p) h e -> p t (h e)", p=P)
        fd = a["s_dist"]
        once = [(flip[:], a["c_flip"]), (comp[:], a["c_comp"]),
                (lamv[:], a["attn_lam"][0].rearrange("a b -> (a b)").partition_broadcast(P)),
                (krows[:], a["o_k_sample"].rearrange("b t h c d -> (b t) (h c d)")),
                (vn[0:NS, :], a["o_v_sample"].rearrange("b t h e -> (b t) (h e)")),
                (qs[:], a["s_q"][:, :, SEQ:NT].rearrange("h p t -> p h t"))]
        for r in range(2 * ST):
            first = fd.offset + D - 1 - r % ST
            once.append((pastb[r:R:2 * ST, :], bass.AP(fd.tensor, first - PAST, [[FM, H], [1, PAST]])))
            once.append((newb[r:R:2 * ST, NS - ST:NS], bass.AP(fd.tensor, first, [[FM, H], [1, ST]])))

        @blk.sync
        def _(sp):
            sp.dma_start(ptab[:], a["page_table"].rearrange("(o b) g -> o (b g)", o=1)).then_inc(pt_in, 16)
            sp.wait_ge(zeroed, 3)
            for dst, src in once:
                sp.dma_start(dst, src).then_inc(once_in, 16)
            sp.wait_ge(pt_in, 16)
            with sp.Fori(0, NB // 2) as j:
                for s in range(2):
                    i = j * 2 + s
                    pages = [sp.value_load(ptab[0:1, bass.ds(i * NPG + g, 1)], min_val=0, max_val=NPHYS - 1)
                             for g in range(NPG)]
                    for buf, cache, sem, used in ((kp, ck, kp_in, ktp_done), (vp, cv, vp_in, pv_done)):
                        sp.wait_ge(used, (i + 1) * H if used is ktp_done else i + 1)
                        for g in range(NPG):
                            sp.dma_start(buf[:, g, :], cache[bass.ds(pages[g], 1), :, :].rearrange("o p f -> (o p) f")
                                         ).then_inc(sem, 16)
                    sp.wait_ge(o_done, i * QB + QB)
                    cols = bass.ds(i * P, P)
                    for dst, src in ((qh[:, s], a["s_q"][bass.ds(i, 1), :, 0:SEQ].rearrange("o p t -> (o p) t")),
                                     (kr[:, s], kview[:, :, cols]), (vh[:, s], vview[:, :, cols]),
                                     (bd[:, s], bass.AP(fd.tensor, fd.offset + i * FM, [[1, P], [1, SEQ]]))):
                        sp.dma_start(dst, src).then_inc(head_in[s], 16)
            sp.wait_ge(pv_out, NB)
            sp.dma_start(a["s_o"][:, :, SEQ:NT].rearrange("h p t -> p h t"), osam[:]).then_inc(osam_stored, 16)
            sp.wait_ge(osam_stored, 16)
            sp.wait_ge(out_done, 16 * NB + 16)

        @blk.gpsimd
        def _(pool):
            for n, (dst, value) in enumerate(((newb[:], NEG), (vn[:], 0.0), (wtc[:], 0.0), (qbd[:], 0.0))):
                pool.memset(dst, value).then_inc(zeroed, 1)
                pool.wait_ge(zeroed, n + 1)

        @blk.scalar
        def _(act):
            act.wait_ge(once_ready, 1)
            act.activation(lams[:], lams[:], ACT.Exp).then_inc(lam_exp, 1)
            def turn(i, s):
                for h in range(0, H, 2):
                    act.wait_ge(ktp_done, i * H + H + h + 1)
                    act.copy(ktp[:, h, :], m.ps[:, h % 4, :]).then_inc(ktp_a, 1)
                act.wait_ge(s_soft, i + 1)
                act.activation(ls[:], ls[:], ACT.Exp, bias=smax[:, 2:3], accum_out=ssum[:, 0:1]).then_inc(s_exp, 1)
                act.wait_ge(kt_done, i + 1)
                act.copy(kt[:].rearrange("p (u q) -> p u q", q=512), m.ps[:, 0:2, :]).then_inc(kt_out, 1)

                def exps(q):
                    act.wait_ge(soft, i * QB + q + 1)
                    for k in range(2):
                        x = lg[q % 2][k][:, 0:(q + 1) * P]
                        r = act.activation(x, x, ACT.Exp, bias=nmx[:, q % 2, k:k + 1], accum_out=sums[:, q % 2, k:k + 1])
                    r.then_inc(exped, 1)

                exps(0)
                exps(1)
                for q in range(QB):
                    act.wait_ge(wt_done, i * QB + q + 1)
                    act.copy(wt[:].rearrange("p t q -> p (t q)")[:, 0:(q + 1) * P],
                             m.ps[:, 4:6, :].rearrange("p u q -> p (u q)")[:, 0:(q + 1) * P]).then_inc(wt_out, 1)
                    if q + 2 < QB:
                        exps(q + 2)
                    act.wait_ge(o_done, i * QB + 2 * QB + q + 1)
                    if q == 0:
                        act.wait_ge(out_done, i * 16 + 16)
                    act.copy(oh[:, q * P:(q + 1) * P], m.ps[:, 6 + q % 2, 0:P]).then_inc(o_out, 1)
                act.wait_ge(o_out, i * QB + 2 * QB)
                act.dma_start(a["s_o"][bass.ds(i, 1), :, 0:SEQ].rearrange("o p t -> (o p) t"), oh[:]).then_inc(out_done, 16)

            with act.Fori(0, NB // 2) as j:
                turn(j * 2, 0)
                turn(j * 2 + 1, 1)

        @blk.tensor
        def _(pe):
            pe.sem_inc(ktp_done, H)
            pe.sem_inc(pv_done, 1)
            pe.sem_inc(o_done, 2 * QB)
            pe.sem_inc(out_done, 16)
            pe.wait_ge(once_in, 16 * len(once))
            for h in range(H):
                q = pe.transpose(m.ps[:, 7, h * NS:(h + 1) * NS], krows[:, h * P:(h + 1) * P], m.ident[0:NS, 0:NS])
            q.then_inc(kn_done, 1)
            flat = qbd[:].rearrange("p h x -> p (h x)")
            def turn(i, s):
                pe.wait_ge(kp_in, i * (16 * NPG) + 16 * NPG)
                pe.wait_ge(o_out, i * QB + QB)
                for h in range(H):
                    if h >= 4:
                        pe.wait_ge(ktp_v if h % 2 else ktp_a, i * (H // 2) + (h - 4) // 2 + 1)
                    for g in range(NPG):
                        q = pe.transpose(m.ps[:, h % 4, g * P:(g + 1) * P], kp[:, g, h * P:(h + 1) * P], m.ident[:])
                    q.then_inc(ktp_done, 1)
                pe.wait_ge(qbd_ready, i + 2)
                for h in range(H):
                    if h % 2 == 0:
                        pe.wait_ge(ktp_a, i * (H // 2) + h // 2 + 1)
                    else:
                        pe.wait_ge(ktp_v, i * (H // 2) + h // 2 + 1)
                    pe.matmul(m.ps[0:R, 4, :], flat[:, h * R:(h + 1) * R], ktp[:, h, :], start=(h == 0), stop=(h == H - 1))
                for h in range(H):
                    q = pe.matmul(m.ps[0:R, 5, 0:NS], flat[:, h * R:(h + 1) * R], kn[:, h, :], start=(h == 0), stop=(h == H - 1))
                q.then_inc(s_done, 1)
                pe.wait_ge(s_norm, i + 1)
                for g in range(NPG + 1):
                    n = P if g < NPG else NS
                    q = pe.matmul(m.ps[0:n, 6, g * NS:(g + 1) * NS], ls[:, g * P:g * P + n], m.comb[:], start=True, stop=True)
                q.then_inc(comb_done, 1)
                pe.wait_ge(comb_out, i + 1)
                pe.wait_ge(vp_in, i * (16 * NPG) + 16 * NPG)
                for h in range(H):
                    for g in range(NPG + 1):
                        v_ = vp[:, g, h * P:(h + 1) * P] if g < NPG else vn[:, h * P:(h + 1) * P]
                        q = pe.matmul(m.ps[:, 7, h * ST:(h + 1) * ST], v_, wtc[:, g, h * ST:(h + 1) * ST],
                                      start=(g == 0), stop=(g == NPG))
                q.then_inc(pv_done, 1)
                pe.wait_ge(head_in[s], (i - s) * 32 + 64)
                for t in range(QB):
                    q = pe.transpose(m.ps[:, t // 4, (t % 4) * P:(t % 4 + 1) * P], kr[:, s, t, :], m.ident[:])
                q.then_inc(kt_done, 1)
                for u in range(2):
                    q = pe.matmul(m.ps[:, 2 + u, :], flip[:], bd[:, s, u * 512:(u + 1) * 512], start=True, stop=True)
                q.then_inc(bias_done, 1)

                def scores(qb):
                    if qb == 0:
                        pe.wait_ge(kt_out, i + 1)
                        pe.wait_ge(bias_out, i + 1)
                    else:
                        pe.wait_ge(soft, i * QB + qb)
                    w = (qb + 1) * P
                    for k in range(2):
                        for u in range(0, w, 512):
                            n = min(512, w - u)
                            q = pe.matmul(m.ps[:, 2 * k + u // 512, 0:n], qh[k * HD:(k + 1) * HD, s, qb * P:(qb + 1) * P],
                                          kt[k * HD:(k + 1) * HD, u:u + n], start=True, stop=True)
                    q.then_inc(qk_done, 1)

                scores(0)
                scores(1)
                for qb in range(QB):
                    pe.wait_ge(w_ready, i * QB + qb + 1)
                    if qb == 0:
                        pe.wait_ge(pv_out, i + 1)
                    else:
                        pe.wait_ge(wt_out, i * QB + qb)
                    for t in range(qb + 1):
                        q = pe.transpose(m.ps[:, 4 + t // 4, (t % 4) * P:(t % 4 + 1) * P],
                                         lg[qb % 2][0][:, t * P:(t + 1) * P], m.ident[:])
                    q.then_inc(wt_done, 1)
                    if qb + 2 < QB:
                        scores(qb + 2)
                    pe.wait_ge(wt_out, i * QB + qb + 1)
                    if qb >= 2:
                        pe.wait_ge(o_out, i * QB + QB + qb - 1)
                    for t in range(qb + 1):
                        q = pe.matmul(m.ps[:, 6 + qb % 2, 0:P], vh[:, s, t, :], wt[:, t, :], start=(t == 0), stop=(t == qb))
                    q.then_inc(o_done, 1)

            with pe.Fori(0, NB // 2) as j:
                turn(j * 2, 0)
                turn(j * 2 + 1, 1)

        @blk.vector
        def _(v):
            ch = Chain(v, chain)
            tt, ts, stt = v.tensor_tensor, v.tensor_scalar, v.scalar_tensor_tensor
            v.sem_inc(o_out, QB)
            v.sem_inc(qbd_ready, 1)
            v.wait_ge(once_in, 16 * len(once))
            v.wait_ge(zeroed, 4)
            ts(pastb[:], pastb[:], 1.0 / SCALE, None, ALU.mult)
            ts(newb[:], newb[:], 1.0 / SCALE, None, ALU.mult)
            for k in range(2):
                pair = [lamv[:, (2 * k + j) * HD:(2 * k + j + 1) * HD] for j in range(2)]
                q = v.tensor_tensor_reduce(lamt[:], pair[0], pair[1], 1.0, 0.0, ALU.mult, ALU.add, lams[:, k:k + 1])
                ch(q)
            v.sem_inc(once_ready, 1)
            v.wait_ge(lam_exp, 1)
            ch(tt(neglam[:], lams[:, 1:2], lams[:, 0:1], ALU.subtract))
            ch(ts(neglam[:], neglam[:], -LAM_INIT, None, ALU.add))
            ch(stt(rowlam[:], comp[:, 1:2], neglam[0:R, 0:1], comp[:, 0:1], ALU.mult, ALU.add))
            v.wait_ge(kn_done, 1)
            ch(v.tensor_copy(kn[:], m.ps[:, 7, 0:H * NS].rearrange("p (h t) -> p h t", t=NS)))
            before, PER = ch.n, 4 + 3 * QB
            with v.Fori(0, NB) as i:
                ch.turn(i, PER, before)
                tok = bass.ds(i * ST, ST)
                v.wait_ge(pv_done, i + 1)
                ts(qbd[0:HD, :, 0:ST], qs[0:HD, :, tok], 1.0, None, ALU.mult)
                ts(qbd[HD:P, :, ST:2 * ST], qs[HD:P, :, tok], 1.0, None, ALU.mult).then_inc(qbd_ready, 1)
                for h in range(1, H, 2):
                    v.wait_ge(ktp_done, i * H + H + h + 1)
                    v.tensor_copy(ktp[:, h, :], m.ps[:, h % 4, :]).then_inc(ktp_v, 1)
                v.wait_ge(s_done, i + 1)
                v.memset(pause[:], 0.0)
                ch(v.tensor_tensor_reduce(ls[:, 0:PAST], m.ps[0:R, 4, :], pastb[:], SCALE, -3e38, ALU.add, ALU.max, smax[:, 0:1]))
                v.memset(pause[:], 0.0)
                ch(ts(newc[:], newb[:, bass.ds((NB - 1 - i) * ST, NS)], 1.0, None, ALU.mult))
                v.memset(pause[:], 0.0)
                ch(v.tensor_tensor_reduce(ls[:, PAST:NK], m.ps[0:R, 5, 0:NS], newc[:], SCALE, smax[:, 0:1], ALU.add, ALU.max,
                                          smax[:, 1:2]))
                ts(smax[:, 2:3], smax[:, 1:2], -1.0, None, ALU.mult).then_inc(s_soft, 1)
                v.wait_ge(s_exp, i + 1)
                ch(v.reciprocal(ssum[:, 1:2], ssum[:, 0:1]))
                ts(ls[:], ls[:], ssum[:, 1:2], rowlam[:, 0:1], ALU.mult, ALU.mult).then_inc(s_norm, 1)
                v.wait_ge(comb_done, i + 1)
                v.tensor_copy(wtc[:, 0:NPG, :], m.ps[:, 6, 0:NPG * NS].rearrange("p (g r) -> p g r", r=NS))
                v.tensor_copy(wtc[0:NS, NPG, :], m.ps[0:NS, 6, NPG * NS:(NPG + 1) * NS]).then_inc(comb_out, 1)
                v.wait_ge(pv_done, i + 2)
                ts(osam[:, :, tok], m.ps[:, 7, 0:NS].rearrange("p (h t) -> p h t", t=ST), 1.0, None,
                   ALU.mult).then_inc(pv_out, 1)
                v.wait_ge(bias_done, i + 1)
                ts(bias[:].rearrange("p (u q) -> p u q", q=512), m.ps[:, 2:4, :], 1.0 / SCALE, None, ALU.mult).then_inc(bias_out, 1)
                v.wait_ge(bias_out, i + 1)

                def logits(qb):
                    w, s = (qb + 1) * P, qb % 2
                    v.wait_ge(qk_done, i * QB + qb + 1)
                    if qb >= 2:
                        v.wait_ge(wt_done, i * QB + qb - 1)
                    v.memset(pause[:], 0.0)
                    for k in range(2):
                        src = m.ps[:, 2 * k:2 * k + 2, :].rearrange("p u q -> p (u q)")[:, 0:w]
                        q = v.tensor_tensor_reduce(lg[s][k][:, 0:w], src, bias[:, SEQ - w:SEQ], SCALE, -3e38,
                                                   ALU.add, ALU.max, mx[:, s, k:k + 1])
                    ch(q)
                    ts(nmx[:, s, :], mx[:, s, :], -1.0, None, ALU.mult).then_inc(soft, 1)

                logits(0)
                logits(1)
                for qb in range(QB):
                    w, s = (qb + 1) * P, qb % 2
                    v.wait_ge(exped, i * QB + qb + 1)
                    ch(v.reciprocal(rec[:, s, :], sums[:, s, :]))
                    ts(lg[s][0][:, 0:w], lg[s][0][:, 0:w], rec[:, s, 0:1], None, ALU.mult)
                    ch(ts(rec[:, s, 1:2], rec[:, s, 1:2], neglam[:, 0:1], None, ALU.mult))
                    stt(lg[s][0][:, 0:w], lg[s][1][:, 0:w], rec[:, s, 1:2], lg[s][0][:, 0:w], ALU.mult,
                        ALU.add).then_inc(w_ready, 1)
                    if qb + 2 < QB:
                        logits(qb + 2)
            assert ch.n == PER, ch.n


class Mem:
    pass


def program(nc, a):
    with ExitStack() as c:
        sb = lambda n, s, d=F32: c.enter_context(nc.sbuf_tensor(n, s, d))
        m = Mem()
        m.ps = c.enter_context(nc.psum_tensor("ps", [P, 8, 512], F32))
        m.ident, m.ones, m.onesv = sb("ident", [P, P]), sb("ones", [P, P]), sb("onesv", [P, P])
        m.eps = sb("eps", [P, 1])
        m.comb = sb("comb", [2 * NS, NS])
        m.modt = sb("modt", [P, NMOD * KT, NC9])
        m.lnt, m.lna, m.lam1 = sb("lnt", [P, 65]), sb("lna", [P, 64]), sb("lam1", [P, 4])
        m.cs, m.cb = sb("cs", [P, 4, KT, NC9]), sb("cb", [P, 4, KT, NC9])
        with ExitStack() as ch:
            with ExitStack() as c1:
                sb1 = lambda n, s, d=F32: c1.enter_context(nc.sbuf_tensor(n, s, d, side="right"))
                m.swap, m.select = sb1("swap", [P, P]), sb1("select", [P, GB * P])
                m.pt, m.ptr = sb1("pt", [P, NPT, G]), sb1("ptr", [P, 2 * L, G])
                m.bst, m.bsw = sb1("bst", [P, G, GC]), sb1("bsw", [P, G, GC])
                m.cst, m.csx = sb1("cst", [P, KT, P]), sb1("csx", [P, KT, P])
                m.h0s, m.h0x = sb1("h0s", [P, NB, G]), sb1("h0x", [P, NB, G])
                m.dskip, m.dskipd = sb1("dskip", [GC, G]), sb1("dskipd", [GC, G, GC])
                m.bat, m.sct = sb1("bat", [P, 112]), sb1("sct", [P, KT, NC9])
                m.spread = sb1("spread", [P, 2, G])
                params_block(nc, a, m)
                ada_block(nc, a, m)
                m.hhi, m.hlo = (ch.enter_context(nc.sbuf_tensor(n, [P, KT, NT], F32R)) for n in ("hhi", "hlo"))
                ssm_block(nc, a, m)
            m.x = ch.enter_context(nc.sbuf_tensor("x", [P, KT, NT], F32))
            st = Stream(nc, ch, "first")
            residual_block(nc, a, m)
            glu_block(nc, a, m, st)
            norm_block(nc, a, m, 0, "l0_")
            mlp_block(nc, a, m, st, 0)
            norm_block(nc, a, m, 1, "l1_")
            kv_block(nc, a, m, st)
            remod_block(nc, a, m)
            column_block(nc, a, m, st, "wq_", a["attn_w_q"][0], dst=a["s_q"])
            save_x_block(nc, a, m)
        attention_block(nc, a, m)
        with ExitStack() as ch:
            m.hhi, m.hlo = (ch.enter_context(nc.sbuf_tensor(n + "2", [P, KT, NT], F32R)) for n in ("hhi", "hlo"))
            m.x = ch.enter_context(nc.sbuf_tensor("x2", [P, KT, NT], F32))
            st = Stream(nc, ch, "second")
            rms_block(nc, a, m)
            column_block(nc, a, m, st, "wo_", a["attn_w_o"][0], gate=8)
            norm_block(nc, a, m, 2, "l2_")
            mlp_block(nc, a, m, st, 1)
            norm_block(nc, a, m, 3, "l3_")
            rows_out_block(nc, a, m)


_INS = ["x_prompt", "x_sample", "state_ssm_re", "state_ssm_im", "cache_k", "cache_v", "page_table", "c_prompt",
        "c_sample", "rel_bias", "w_ada", "b_ada", "ln_g", "ln_b", "ssm_lam_re", "ssm_lam_im", "ssm_log_dt",
        "ssm_b_re", "ssm_b_im", "ssm_c_re", "ssm_c_im", "ssm_d", "ssm_w_glu_a", "ssm_w_glu_b", "w_ada_kv",
        "b_ada_kv", "w_kv", "attn_w_q", "attn_lam", "attn_subln_g", "attn_w_o", "mlp_w1", "mlp_w2"]
_OUTS = [("y_prompt", (1, SEQ, D)), ("y_sample", (NB, ST, D)), ("ssm_re_prompt", (1, 1, G, NP)),
         ("ssm_im_prompt", (1, 1, G, NP)), ("k_prompt", (1, SEQ, H, 2, HD)), ("v_prompt", (1, SEQ, H, VD)),
         ("ssm_re_sample", (1, NB, G, NP)), ("ssm_im_sample", (1, NB, G, NP)),
         ("k_sample", (NB, ST, H, 2, HD)), ("v_sample", (NB, ST, H, VD))]
_SCRATCH = [("s_dist", (H, FM)), ("s_xs", (NB, ST, D)), ("s_q", (H, P, NT)), ("s_o", (H, P, NT)),
            ("s_x", (P, KT, NT))]


def kernel(**inputs):
    import numpy as _np
    import concourse.bacc as _bacc
    from concourse.bass_utils import run_bass_kernel_spmd as _run

    nc = _bacc.Bacc("TRN2", target_bir_lowering=False, num_devices=1)
    arrays, a = {}, {}
    for name in _INS:
        arrays[name + "_in"] = _np.ascontiguousarray(inputs[name])
    for name, x in constants().items():
        arrays[name + "_in"] = x
    for name, x in arrays.items():
        a[name[:-3]] = nc.dram_tensor(name, x.shape, mybir.dt.from_np(x.dtype), kind="ExternalInput").ap()
    for name, shape in _OUTS:
        a["o_" + name] = nc.dram_tensor("out_" + name, shape, F32, kind="ExternalOutput").ap()
    for name, shape in _SCRATCH:
        a[name] = nc.dram_tensor(name, shape, F32, kind="Internal").ap()
    program(nc, a)
    r = _run(nc, [arrays], core_ids=[0])
    return tuple(r.results[0]["out_" + name] for name, _ in _OUTS)
```

```python
import math
from contextlib import ExitStack, contextmanager

import numpy as np
import concourse.bass as bass
from concourse import mybir

F32 = mybir.dt.float32
F32R = mybir.dt.float32r
I32 = mybir.dt.int32
ALU = mybir.AluOpType
ACT = mybir.ActivationFunctionType
AX = mybir.AxisListType

P = 128
D = 1024
KT = D // P
SEQ = 1024
NB, ST = 8, 4
NS = NB * ST
NT = SEQ + NS
NCH = 3
CH = NT // NCH
LASTP = SEQ - 2 * CH
NC9 = 1 + NB
G, GC, NP = 64, 16, 64
GB = P // GC
L = 8
NCK = SEQ // L
H, HD, VD = 8, 64, 128
DFF = 4096
PAGE = 128
PAST = 512
NPG = PAST // PAGE
NPHYS = 40
ALPHA = (2.0 * 2) ** 0.25
LN_EPS = 1e-5
NEG = -1e30
LAM_INIT = 0.8 - 0.6 * math.exp(-0.3)
NMOD = 14
WC = 256
NSL = D // WC
FM = 1152
NPOW = L + 1
NROT = 7
IMP, ROTC, ROTS, R8, ERD, EIS = NPOW, 2 * NPOW, 2 * NPOW + NROT, 2 * NPOW + 2 * NROT, 2 * NPOW + 2 * NROT + 1, 2 * NPOW + 2 * NROT + 2
NPT = EIS + 1


class Chain:

    def __init__(self, eng, sem):
        self.eng, self.sem, self.n, self.base = eng, sem, 0, 0

    def __call__(self, ins):
        self.n += 1
        ins.then_inc(self.sem, 1)
        self.eng.wait_ge(self.sem, self.base + self.n)

    def turn(self, i, per_turn, before=0):
        self.base, self.n = i * per_turn + before, 0


@contextmanager
def semaphores(nc):
    taken = []

    def take(name):
        taken.append(nc.alloc_semaphore(name=name))
        return taken[-1]

    yield take
    nc.clear_and_free_semaphores(taken)
    nc.all_engine_barrier()


def bucket_onehot():
    dist = (D - 1) - np.arange(FM)
    n = np.maximum(dist, 0)
    large = 16 + (np.log(np.maximum(n, 1).astype(np.float32) / np.float32(16))
                  / np.float32(math.log(8.0)) * np.float32(16)).astype(np.int32)
    b = np.where(n < 16, n, np.minimum(large, 31))
    out = np.zeros((33, FM), np.float32)
    out[b, np.arange(FM)] = (dist >= 0)
    out[32] = (dist < 0)
    return out


def constants():
    ident = np.eye(P, dtype=np.float32)
    swap = np.roll(ident, P // 2, axis=1)
    flip = ident[::-1].copy()
    select = np.zeros((P, GB, L, GC), np.float32)
    for g in range(GB):
        for h in range(GC):
            select[g * GC + h, g, :, h] = 1
    comb = np.zeros((H, 2, ST, H, ST), np.float32)
    for h in range(H):
        for t in range(ST):
            comb[h, :, t, h, t] = 1
    comp = np.zeros((H, 2, ST, 2), np.float32)
    comp[:, 0, :, 0] = comp[:, 1, :, 1] = 1
    return {"c_comp": comp.reshape(2 * NS, 2), "c_ident": ident, "c_swap": swap, "c_flip": flip, "c_select": select.reshape(P, GB * P),
            "c_comb": comb.reshape(2 * NS, NS), "c_bucket": bucket_onehot()}


def params_block(nc, a, m):
    MAG = 12582912.0
    with ExitStack() as c:
        sb = lambda n, s, d=F32: c.enter_context(nc.sbuf_tensor(n, s, d, side="right"))
        lamr, lami, logdt = sb("lamr", [G, NP]), sb("lami", [G, NP]), sb("logdt", [G, 1])
        tmp = sb("ptmp", [G, 12, 4 * NP])
        tmpi = sb("ptmpi", [G, NP], I32)
        ar, ai = sb("ar", [G, NPOW, NP]), sb("ai", [G, NPOW, NP])
        rc, rs = sb("rc", [G, NROT, NP]), sb("rs", [G, NROT, NP])
        rows = sb("prows", [G, NPT, P])
        brow, browx = sb("brow", [G, P, GC]), sb("browx", [G, P, GC])
        crow, crowx = sb("crow", [P, KT, P]), sb("crowx", [P, KT, P])
        hrow, hrowx = sb("hrow", [P, 4, P]), sb("hrowx", [P, 4, P])
        bst0, bsw0 = sb("bst0", [P, GC, G]), sb("bsw0", [P, GC, G])
        mix = sb("bmix", [P, G, GC])
        cond = sb("cond", [NC9, D])
        csig = sb("csig", [NC9, D])
        brows1, brows2 = sb("brows1", [112, P]), sb("brows2", [65, P])
        onehot, relx = sb("onehot", [33, FM]), sb("relx", [33, H])
        fdist = onehot[0:H, :]
        eps = m.eps
        signal = c.enter_context(semaphores(nc))
        S = lambda n: signal(n)
        small_in, trig_in, tables_in, dist_out = S("p_small_in"), S("p_trig_in"), S("p_tables_in"), S("p_dist_out")
        params_ready, angle_ready, trig_done = S("p_rows_ready"), S("p_angle"), S("p_trig")
        turned, turned_out, silu_half, dve_chain, relx_set = S("p_turned"), S("p_turned_out"), S("p_silu"), S("p_dve"), S("p_relx")
        ada_in = S("p_ada_in")
        blk = c.enter_context(nc.Block())
        n_tables = 0

        @blk.sync
        def _(sp):
            for out, src in ((lamr, a["ssm_lam_re"][0]), (lami, a["ssm_lam_im"][0]),
                             (logdt, a["ssm_log_dt"].rearrange("l (g o) -> (l g) o", o=1))):
                sp.dma_start(out[:], src).then_inc(small_in, 16)
            tables = [
                (m.ident[:], a["c_ident"]), (m.swap[:], a["c_swap"]), (m.select[:], a["c_select"]),
                (m.comb[:], a["c_comb"]), (onehot[:], a["c_bucket"]), (relx[0:32, :], a["rel_bias"]),
                (cond[0:1, :], a["c_prompt"]), (cond[1:NC9, :], a["c_sample"]),
                (brows1[0:96, :], a["b_ada"].rearrange("l (r f) -> (l r) f", f=P)),
                (brows1[96:112, :], a["b_ada_kv"].rearrange("(r f) -> r f", f=P)),
                (brows2[0:32, :], a["ln_g"].rearrange("l i (r f) -> (l i r) f", f=P)),
                (brows2[32:64, :], a["ln_b"].rearrange("l i (r f) -> (l i r) f", f=P)),
                (brows2[64:65, :], a["attn_subln_g"]),
                (brow[:, 0:NP, :], a["ssm_b_re"][0]), (brow[:, NP:P, :], a["ssm_b_im"][0]),
                (browx[:, 0:NP, :], a["ssm_b_im"][0]), (browx[:, NP:P, :], a["ssm_b_re"][0]),
            ]
            for half, (x, y) in enumerate((("ssm_c_re", "ssm_c_im"), ("ssm_c_im", "ssm_c_re"))):
                dst = (crow, crowx)[half]
                for k, src in enumerate((x, y)):
                    tables.append((dst[:, :, k * NP:(k + 1) * NP],
                                   a[src][0].rearrange("(t g) h p -> (g h) t p", g=GB)))
            for half, (x, y) in enumerate((("state_ssm_re", "state_ssm_im"), ("state_ssm_im", "state_ssm_re"))):
                dst = (hrow, hrowx)[half]
                for k, src in enumerate((x, y)):
                    tables.append((dst[:, :, k * NP:(k + 1) * NP],
                                   a[src][0].rearrange("(q b) g p -> (b g) q p", b=2)))
            nonlocal n_tables
            n_tables = len(tables) + 1
            for out, src in tables:
                sp.dma_start(out, src).then_inc(tables_in, 16)
            with nc.allow_non_contiguous_dma(reason="1024 single values, once"):
                sp.dma_start(m.dskip[:], a["ssm_d"].rearrange("l (g h) -> (l h) g", h=GC)).then_inc(tables_in, 16)
            first = a["w_ada"][0].rearrange("(k p) n -> p k n", p=P)
            for s in range(2 * NSL):
                sp.dma_start(m.wada[:, s], first[:, :, s * WC:(s + 1) * WC]).then_inc(ada_in, 16)
            sp.wait_ge(turned_out, 11)
            sp.dma_start(a["s_dist"], fdist).then_inc(dist_out, 16)
            sp.wait_ge(dist_out, 16)
            sp.wait_ge(ada_in, 16 * 2 * NSL)

        @blk.gpsimd
        def _(pool):
            for n, (dst, value) in enumerate(((m.ones[:], 1.0 / D), (m.onesv[:], 1.0 / VD), (eps[:], LN_EPS),
                                              (relx[32:33, :], NEG))):
                pool.memset(dst, value).then_inc(relx_set, 1)
                pool.wait_ge(relx_set, n + 1)

        @blk.scalar
        def _(act):
            act.wait_ge(angle_ready, 1)
            act.activation(tmp[:, 1, 0:NP], tmp[:, 0, 0:NP], ACT.Sin).then_inc(trig_done, 1)
            act.activation(tmp[:, 3, 0:NP], tmp[:, 2, 0:NP], ACT.Sin).then_inc(trig_done, 1)
            act.wait_ge(tables_in, 16 * n_tables)
            act.activation(csig[:], cond[:], ACT.Sigmoid).then_inc(silu_half, 1)

        @blk.vector
        def _(v):
            ch = Chain(v, dve_chain)
            t = lambda i: tmp[:, i, 0:NP]
            tt, ts = v.tensor_tensor, v.tensor_scalar

            def exp(out, x, p1, p2, p3, pi):
                ch(ts(p1, x, -87.0, 88.0, ALU.max, ALU.min))
                ch(ts(p2, p1, 1.0 / math.log(2.0), MAG + 127.0, ALU.mult, ALU.add))
                ch(ts(p3, p2, MAG + 127.0, None, ALU.subtract))
                ch(ts(pi, p2.bitcast(I32), 23, None, ALU.logical_shift_left))
                ch(v.scalar_tensor_tensor(p1, p3, -0.693359375, p1, ALU.mult, ALU.add))
                ch(v.scalar_tensor_tensor(p1, p3, 2.12194440e-4, p1, ALU.mult, ALU.add))
                ch(ts(p2, p1, 1.0 / 5040, None, ALU.mult))
                for k in (720, 120, 24, 6, 2, 1):
                    ch(v.scalar_tensor_tensor(p2, p2, 1.0 / k, p1, ALU.add, ALU.mult))
                ch(ts(p2, p2, 1.0, None, ALU.add))
                ch(tt(out, p2, pi.bitcast(F32), ALU.mult))

            v.wait_ge(small_in, 48)
            dt = tmp[:, 11, 0:1]
            exp(dt, logdt[:], tmp[:, 8, 0:1], tmp[:, 9, 0:1], tmp[:, 10, 0:1], tmpi[:, 0:1])
            ch(ts(t(4), lamr[:], dt, None, ALU.mult))
            exp(t(5), t(4), t(8), t(9), t(10), tmpi[:])
            ch(ts(t(0), lami[:], dt, None, ALU.mult))
            ch(ts(t(8), t(0), 1.0 / (2 * math.pi), MAG, ALU.mult, ALU.add))
            ch(ts(t(8), t(8), MAG, None, ALU.subtract))
            c1 = 6.28125
            c2 = float(np.float32(2 * math.pi - c1))
            c2 = float(np.round(c2 * 2 ** 19) / 2 ** 19)
            for cc in (c1, c2, 2 * math.pi - c1 - c2):
                ch(v.scalar_tensor_tensor(t(0), t(8), -cc, t(0), ALU.mult, ALU.add))
            lim = float(np.float32(3.1415925))
            ch(ts(t(0), t(0), -lim, lim, ALU.max, ALU.min))
            ch(v.scalar_tensor_tensor(t(2), t(0), -1.0, t(0), ALU.mult, ALU.min))
            t2 = ts(t(2), t(2), math.pi / 2, None, ALU.add)
            t2.then_inc(angle_ready, 1)
            v.wait_ge(trig_done, 2)
            v.memset(ar[:, 0, :], 1.0)
            v.memset(ai[:, 0, :], 0.0)
            tt(ar[:, 1, :], t(5), t(3), ALU.mult)
            ch(tt(ai[:, 1, :], t(5), t(1), ALU.mult))

            def cmul(outr, outi, xr, xi, yr, yi, w):
                p = [tmp[:, i, 0:w * NP] if w == 1 else tmp[:, i, 0:w * NP].rearrange("g (w p) -> g w p", w=w)
                     for i in (6, 7, 8, 9)]
                tt(p[0], xr, yr, ALU.mult)
                tt(p[1], xi, yi, ALU.mult)
                tt(p[2], xr, yi, ALU.mult)
                ch(tt(p[3], xi, yr, ALU.mult))
                tt(outr, p[0], p[1], ALU.subtract)
                ch(tt(outi, p[2], p[3], ALU.add))

            for w in (1, 2, 4):
                b = lambda x: x[:, w:w + 1, :].to_broadcast([G, w, NP]) if w > 1 else x[:, 1, :]
                s = lambda x: x[:, 1:w + 1, :] if w > 1 else x[:, 1, :]
                o = lambda x: x[:, w + 1:2 * w + 1, :] if w > 1 else x[:, 2, :]
                cmul(o(ar), o(ai), b(ar), b(ai), s(ar), s(ai), w)

            def unit(r, i):
                tt(t(6), r, r, ALU.mult)
                ch(tt(t(7), i, i, ALU.mult))
                ch(tt(t(6), t(6), t(7), ALU.add))
                ch(ts(t(6), t(6), -0.5, 1.5, ALU.mult, ALU.add))
                tt(r, r, t(6), ALU.mult)
                ch(tt(i, i, t(6), ALU.mult))

            unit(t(3), t(1))
            xr, xi = t(3), t(1)
            for k in range(3 + NROT - 1):
                o = (t(3), t(1)) if k < 2 else (rc[:, k - 2, :], rs[:, k - 2, :])
                cmul(o[0], o[1], xr, xi, xr, xi, 1)
                unit(*o)
                xr, xi = o
            for _ in range(3):
                ch(tt(t(5), t(5), t(5), ALU.mult))
            tt(t(6), lamr[:], lamr[:], ALU.mult)
            ch(tt(t(7), lami[:], lami[:], ALU.mult))
            ch(tt(t(6), t(6), t(7), ALU.add))
            ts(t(8), ar[:, 1, :], -1.0, None, ALU.add)
            ch(v.reciprocal(t(6), t(6)))
            tt(t(0), t(8), lamr[:], ALU.mult)
            tt(t(1), ai[:, 1, :], lami[:], ALU.mult)
            tt(t(2), ai[:, 1, :], lamr[:], ALU.mult)
            ch(tt(t(3), t(8), lami[:], ALU.mult))
            tt(t(0), t(0), t(1), ALU.add)
            ch(tt(t(2), t(2), t(3), ALU.subtract))
            tt(t(0), t(0), t(6), ALU.mult)
            ch(tt(t(2), t(2), t(6), ALU.mult))
            lo, hi = slice(0, NP), slice(NP, P)
            for half in (lo, hi):
                v.tensor_copy(rows[:, 0:NPOW, half], ar[:])
                v.tensor_copy(rows[:, ROTC:ROTC + NROT, half], rc[:])
                v.tensor_copy(rows[:, R8, half], t(5))
                v.tensor_copy(rows[:, ERD, half], t(0))
            ts(rows[:, IMP:IMP + NPOW, lo], ai[:], -1.0, None, ALU.mult)
            v.tensor_copy(rows[:, IMP:IMP + NPOW, hi], ai[:])
            v.tensor_copy(rows[:, ROTS:ROTS + NROT, lo], rs[:])
            ts(rows[:, ROTS:ROTS + NROT, hi], rs[:], -1.0, None, ALU.mult)
            ts(rows[:, EIS, lo], t(2), -1.0, None, ALU.mult)
            ch(v.tensor_copy(rows[:, EIS, hi], t(2)))
            v.wait_ge(tables_in, 16 * n_tables)
            ts(crow[:, :, NP:P], crow[:, :, NP:P], -1.0, None, ALU.mult)
            ch(ts(crowx[:, :, 0:NP], crowx[:, :, 0:NP], -1.0, None, ALU.mult))
            v.wait_ge(silu_half, 1)
            tt(cond[:], cond[:], csig[:], ALU.mult).then_inc(params_ready, 1)
            k = 0

            def out(dst, src):
                nonlocal k
                k += 1
                v.wait_ge(turned, k)
                v.tensor_copy(dst, src).then_inc(turned_out, 1)

            for j in range(5):
                w = min(8, NPT - 8 * j)
                out(m.pt[:, 8 * j:8 * j + w, :], m.ps[:, j, 0:w * G].rearrange("p (n g) -> p n g", g=G))
            out(m.sct[:], m.ps[:, 5, 0:KT * NC9].rearrange("p (k b) -> p k b", b=NC9))
            out(m.bat[:], m.ps[:, 6, 0:112])
            out(m.lnt[:], m.ps[:, 7, 0:65])
            for j in range(3):
                out(fdist[:, j * 384:(j + 1) * 384], m.ps[0:H, j, 0:384])
            for j in range(2):
                out(bst0[:, 8 * j:8 * j + 8, :], m.ps[:, 3 + j, :].rearrange("p (h g) -> p h g", g=G))
            for j in range(2):
                out(bsw0[:, 8 * j:8 * j + 8, :], m.ps[:, 5 + j, :].rearrange("p (h g) -> p h g", g=G))
            for j in range(2):
                out(m.cst[:, 4 * j:4 * j + 4, :], m.ps[:, j, :].rearrange("p (t q) -> p t q", q=P))
            for j in range(2):
                out(m.csx[:, 4 * j:4 * j + 4, :], m.ps[:, 3 + j, :].rearrange("p (t q) -> p t q", q=P))
            out(m.h0s[:].rearrange("p b g -> p (b g)"), m.ps[:, 5, :])
            out(m.h0x[:].rearrange("p b g -> p (b g)"), m.ps[:, 6, :])
            v.wait_ge(turned_out, k)
            bc = lambda n: m.pt[:, n:n + 1, :].rearrange("p o g -> p g o").to_broadcast([P, G, GC])
            b0, bx = bst0[:].rearrange("p h g -> p g h"), bsw0[:].rearrange("p h g -> p g h")
            tt(m.bst[:], b0, bc(ERD), ALU.mult)
            tt(m.bsw[:], bx, bc(ERD), ALU.mult)
            ch(tt(mix[:], bx, bc(EIS), ALU.mult))
            ch(tt(m.bst[:], m.bst[:], mix[:], ALU.add))
            ch(tt(mix[:], b0, bc(EIS), ALU.mult))
            ch(tt(m.bsw[:], m.bsw[:], mix[:], ALU.subtract))
            for n in range(L):
                v.tensor_copy(m.ptr[:, n, :], m.pt[:, L - 1 - n, :])
                v.tensor_copy(m.ptr[:, L + n, :], m.pt[:, IMP + L - 1 - n, :])
            ch(tt(m.dskipd[:], m.ident[0:GC, 0:GC].rearrange("h (o j) -> h o j", o=1).to_broadcast([GC, G, GC]),
                  m.dskip[:].rearrange("h (g o) -> h g o", o=1).to_broadcast([GC, G, GC]), ALU.mult))

        @blk.tensor
        def _(pe):
            pe.wait_ge(tables_in, 16 * n_tables)
            pe.wait_ge(params_ready, 1)
            idg = m.ident[0:G, 0:G]
            for j in range(5):
                for n in range(8 * j, min(8 * j + 8, NPT)):
                    q = pe.transpose(m.ps[:, j, (n % 8) * G:(n % 8 + 1) * G], rows[:, n, :], idg)
                q.then_inc(turned, 1)
            for k in range(KT):
                q = pe.transpose(m.ps[:, 5, k * NC9:(k + 1) * NC9], cond[:, k * P:(k + 1) * P], m.ident[0:NC9, 0:NC9])
            q.then_inc(turned, 1)
            pe.transpose(m.ps[:, 6, 0:112], brows1[:], m.ident[0:112, 0:112]).then_inc(turned, 1)
            pe.transpose(m.ps[:, 7, 0:65], brows2[:], m.ident[0:65, 0:65]).then_inc(turned, 1)
            pe.wait_ge(relx_set, 4)
            for j in range(3):
                pe.wait_ge(turned_out, j + 1)
                pe.matmul(m.ps[0:H, j, 0:384], relx[:], onehot[:, j * 384:(j + 1) * 384],
                          start=True, stop=True).then_inc(turned, 1)
            for first, src, free in ((3, brow, 5), (5, browx, 7)):
                pe.wait_ge(turned_out, free)
                for j in range(2):
                    for h in range(8):
                        q = pe.transpose(m.ps[:, first + j, h * G:(h + 1) * G], src[:, :, 8 * j + h], idg)
                    q.then_inc(turned, 1)
            for first, src, free in ((0, crow, 10), (3, crowx, 13)):
                pe.wait_ge(turned_out, free)
                for j in range(2):
                    for t in range(4):
                        q = pe.transpose(m.ps[:, first + j, t * P:(t + 1) * P], src[:, 4 * j + t, :], m.ident[:])
                    q.then_inc(turned, 1)
            for bank, src in ((5, hrow), (6, hrowx)):
                pe.wait_ge(turned_out, 15)
                for t in range(4):
                    q = pe.transpose(m.ps[:, bank, t * P:(t + 1) * P], src[:, t, :], m.ident[:])
                q.then_inc(turned, 1)


def ada_block(nc, a, m):
    with ExitStack() as c:
        sb = lambda n, s, d=F32: c.enter_context(nc.sbuf_tensor(n, s, d, side="right"))
        wada = m.wada
        signal = c.enter_context(semaphores(nc))
        S = lambda n: signal(n)
        landed = [S(f"a_landed{i}") for i in range(2 * NSL)]
        used, stored, dve_chain = S("a_used"), S("a_stored"), S("a_dve")
        spread_done, spread_out, rows_ready = S("a_spread"), S("a_spread_out"), S("a_rows")
        xs_in, xs_done, xs_out = S("a_xs_in"), S("a_xs_done"), S("a_xs_out")
        sshift, sscale, xs = sb("sshift", [NB, D]), sb("sscale", [NB, D]), sb("xs", [NB, ST, D])
        rows, copied, turned = sb("a_row", [NC9, 2, D]), S("a_copied"), S("a_turned")
        blk = c.enter_context(nc.Block())
        runs = [(a["w_ada"][0], 0, 3), (a["w_ada"][1], 3, 3), (a["w_ada_kv"], 6, 1)]

        def loads(queue, parity):
            for s in range(parity, 2 * NSL, 2):
                queue.sem_inc(landed[s], 16)
            for src, first, pairs in runs:
                view = src.rearrange("(k p) n -> p k n", p=P)
                with queue.Fori(1 if first == 0 else 0, pairs) as i:
                    for s in range(parity, 2 * NSL, 2):
                        queue.wait_ge(used, (i + first) * (2 * NSL) + s + 1)
                        queue.dma_start(wada[:, s], view[:, :, bass.ds(i * (2 * D) + s * WC, WC)]).then_inc(landed[s], 16)

        @blk.scalar
        def _(act):
            loads(act, 1)

        @blk.sync
        def _(sp):
            sp.dma_start(xs[:], a["x_sample"]).then_inc(xs_in, 16)
            loads(sp, 0)
            sp.wait_ge(xs_done, 1)
            sp.dma_start(a["s_xs"], xs[:]).then_inc(xs_out, 16)
            sp.wait_ge(xs_out, 16)

        @blk.tensor
        def _(pe):
            pe.sem_inc(used, 2 * NSL)
            for _, first, pairs in runs:
                with pe.Fori(0, pairs) as i:
                    for j in range(2):
                        for s in range(NSL):
                            slot = j * NSL + s
                            pe.wait_ge(landed[slot], (i + first + 1) * 16)
                            for k in range(KT):
                                q = pe.matmul(m.ps[0:NC9, 2 * j + s // 2, (s % 2) * WC:(s % 2 + 1) * WC],
                                              m.sct[:, k, :], wada[:, slot, k, :], start=(k == 0), stop=(k == KT - 1))
                            q.then_inc(used, 1)
                    for j in range(2):
                        n = (i + first) * 2 + j
                        pe.wait_ge(copied, n + 1)
                        pe.wait_ge(stored, n + 1)
                        for t in range(KT):
                            q = pe.matmul(m.ps[:, 4 + j, t * NC9:(t + 1) * NC9], rows[:, j, t * P:(t + 1) * P],
                                          m.ident[0:NC9, 0:NC9], start=True, stop=True)
                        q.then_inc(turned, 1)
            pe.wait_ge(rows_ready, 1)
            for g in range(GB):
                q = pe.matmul(m.ps[:, 2, g * 16:(g + 1) * 16], m.select[:, g * P:(g + 1) * P],
                              m.modt[:, 0:16, 0], start=True, stop=True)
            q.then_inc(spread_done, 1)
            for j in range(2):
                for t in range(KT):
                    q = pe.transpose(m.ps[0:NB, 3 + 2 * j + t // 4, (t % 4) * P:(t % 4 + 1) * P],
                                     m.modt[:, j * KT + t, 1:NC9], m.ident[:])
                q.then_inc(spread_done, 1)

        @blk.vector
        def _(v):
            ch = Chain(v, dve_chain)
            tt, ts = v.tensor_tensor, v.tensor_scalar
            v.sem_inc(stored, 2)
            for _, first, pairs in runs:
                with v.Fori(0, pairs) as i:
                    for j in range(2):
                        v.wait_ge(used, ((i + first) * 2 + j) * NSL + 3 * NSL)
                        v.tensor_copy(rows[:, j, :], m.ps[0:NC9, 2 * j:2 * j + 2, :].rearrange("b u f -> b (u f)")
                                      ).then_inc(copied, 1)
                    for j in range(2):
                        n = (i + first) * 2 + j
                        v.wait_ge(turned, n + 1)
                        tt(m.modt[:, bass.ds(n * KT, KT), :],
                           m.ps[:, 4 + j, 0:KT * NC9].rearrange("p (t b) -> p t b", b=NC9),
                           m.bat[:, bass.ds(n * KT, KT)].rearrange("p (t o) -> p t o", o=1)
                           .to_broadcast([P, KT, NC9]), ALU.add).then_inc(stored, 1)
            v.wait_ge(stored, 2 + NMOD)
            md = lambda j, w=1: m.modt[:, j * KT:(j + w) * KT, :]
            for j, w in ((1, 2), (4, 2), (7, 2), (10, 2)):
                ts(md(j, w), md(j, w), 1.0, None, ALU.add)
            ts(md(13), md(13), 1.0, None, ALU.add).then_inc(rows_ready, 1)
            v.wait_ge(rows_ready, 1)
            for n, scale, shift in ((0, 4, 3), (1, 13, 12), (2, 10, 9)):
                g = m.lnt[:, n * KT:(n + 1) * KT].rearrange("p (t o) -> p t o", o=1).to_broadcast([P, KT, NC9])
                b = m.lnt[:, 32 + n * KT:32 + (n + 1) * KT].rearrange("p (t o) -> p t o", o=1).to_broadcast([P, KT, NC9])
                tt(m.cs[:, n], md(scale), g, ALU.mult)
                ch(tt(m.cb[:, n], md(scale), b, ALU.mult))
                ch(tt(m.cb[:, n], m.cb[:, n], md(shift), ALU.add))
            ts(m.cs[:, 3], md(7), 1.0 / ALPHA, None, ALU.mult)
            v.tensor_copy(m.cb[:, 3], md(6))
            ts(m.lna[:, 0:24], m.lnt[:, 0:24], ALPHA, None, ALU.mult)
            ts(m.lna[:, 32:56], m.lnt[:, 32:56], ALPHA, None, ALU.mult)
            v.tensor_copy(m.lna[:, 24:32], m.lnt[:, 24:32])
            v.tensor_copy(m.lna[:, 56:64], m.lnt[:, 56:64])
            v.wait_ge(spread_done, 1)
            for j in range(2):
                v.tensor_copy(m.spread[:, j, :].rearrange("p (t g) -> p t g", g=GB),
                              m.ps[:, 2, 0:GB * 16].rearrange("p (g j t) -> p j t g", g=GB, j=2)[:, j])
            for j, dst in ((0, sshift), (1, sscale)):
                v.wait_ge(spread_done, j + 2)
                q = v.tensor_copy(dst[:], m.ps[0:NB, 3 + 2 * j:5 + 2 * j, :].rearrange("b u f -> b (u f)"))
            ch(q)
            v.wait_ge(xs_in, 16)
            wide = lambda x: x[:].rearrange("b (o f) -> b o f", o=1).to_broadcast([NB, ST, D])
            ch(tt(xs[:], xs[:], wide(sscale), ALU.mult))
            tt(xs[:], xs[:], wide(sshift), ALU.add).then_inc(xs_done, 1)


def ssm_block(nc, a, m):
    with ExitStack() as c:
        sb = lambda n, s, d=F32: c.enter_context(nc.sbuf_tensor(n, s, d, side="right"))
        signal = c.enter_context(semaphores(nc))
        S = lambda n: signal(n)
        NU = NCK + NB
        xnat, xsh, xsg = sb("xnat", [P, L, P]), sb("xsh", [NB, L, P]), sb("xsg", [NB, GB, P])
        regrouped = S("s_regrouped")
        u, w, wx = sb("u", [P, GB, NU]), sb("w", [P, GB, P]), sb("wx", [P, GB, P])
        xg = m.select[:].rearrange("p (g q) -> p g q", q=P)
        wt, v1s, v2s = sb("wt", [P, GB, L, GC]), sb("v1", [P, 2, GB, NPOW, GC]), sb("v2", [P, 2, GB, L, GC])
        bcur, h0s, h0xs = sb("bcur", [P, GB, GC]), sb("h0cur", [P, 2, GB, NB]), sb("h0xcur", [P, 2, GB, NB])
        kb, tz = sb("kb", [GC, GB, (2 * L - 1) * GC]), sb("tz", [P, GB, P])
        ec, es = sb("ec", [P, GB, NCK]), sb("es", [P, GB, NCK])
        rt1, rt2, rt3 = (sb(f"rt{n}", [P, GB, NCK // 2]) for n in (1, 2, 3))
        tg = sb("tg", [P, GB, NPOW * GC])
        xm = wt[:].rearrange("p g n h -> p g (n h)")
        xs = tg[:, :, 0:NCK]
        pb, qb = sb("pb", [P, GB, NCK + 1]), sb("qb", [P, GB, NCK + 1])
        gy, gys = wx, w[0:NB, 0:ST, :]
        pend, qend, ss = sb("pend", [P, G]), sb("qend", [P, G]), sb("ss", [P, NB, G])
        sout = tg[0:G].rearrange("g a b -> g (a b)").rearrange("g (n q) -> g n q", q=P)
        x_in, xs_in, tz_in, st_out = S("s_x_in"), S("s_xs_in"), S("s_tz_in"), S("s_st_out")
        y_done = S("s_y_done")
        u_turned, w_turned, k_done, xx_done, g_turned, st_done = (
            S("s_u_turned"), S("s_w_turned"), S("s_k_done"), S("s_xx_done"), S("s_g_turned"), S("s_st_done"))
        u_out, w_out, gelu_out, g_hi = S("s_u_out"), S("s_w_out"), S("s_gelu"), S("s_g_hi")
        gen, kb_ready, pq_ready, xs_out, g_lo, st_copied = (S("s_gen"), S("s_kb"), S("s_pq"), S("s_xs_out"), S("s_g_lo"), S("s_st_cp"))
        rot_ready, rot_used, zero_ready = S("s_rot"), S("s_rot_used"), S("s_zero")
        dve_chain, pool_chain = S("s_dve"), S("s_pool")
        blk = c.enter_context(nc.Block())

        def turns(engine, turn):
            with engine.Fori(0, KT // 2 - 1) as j:
                turn(j * 2, 0, False)
                turn(j * 2 + 1, 1, False)
            turn(KT - 2, 0, False)
            turn(KT - 1, 1, True)

        @blk.sync
        def _(sp):
            xin = a["x_prompt"][0].rearrange("(c t) f -> c t f", t=L)
            sp.wait_ge(zero_ready, 5)
            with sp.Fori(0, KT) as i:
                cols = bass.ds(i * P, P)
                sp.wait_ge(regrouped, i + 1)
                sp.dma_start(xnat[:], xin[:, :, cols]).then_inc(x_in, 16)
                sp.dma_start(xsh[:, ST:L, :], a["s_xs"][:, :, cols]).then_inc(xs_in, 16)
                sp.wait_ge(kb_ready, i + 1)
                sp.wait_ge(y_done, i + 1)
                for s in range(L):
                    sp.dma_start(tz[s * GC:(s + 1) * GC, :, :],
                                 kb[:, :, (L - 1 - s) * GC:(L - 1 - s) * GC + P]).then_inc(tz_in, 16)
            sp.wait_ge(st_copied, 2)
            for half, re in ((0, "re"), (1, "im")):
                cols = slice(half * NP, (half + 1) * NP)
                sp.dma_start(a[f"o_ssm_{re}_prompt"][0, 0], sout[:, 0, cols]).then_inc(st_out, 16)
                sp.dma_start(a[f"o_ssm_{re}_sample"][0].rearrange("b g p -> g b p"),
                             sout[:, 1:NC9, cols]).then_inc(st_out, 16)
            sp.wait_ge(st_out, 64)

        @blk.gpsimd
        def _(pool):
            ch = Chain(pool, pool_chain)
            zeros = [(xsh[:, 0:ST, :], 0.0), (kb[:], 0.0), (pb[:, :, 0:1], 0.0), (qb[:, :, 0:1], 0.0),
                     (es[:, :, 0:1], 0.0), (ec[:, :, 0:1], 1.0)]
            for n, (dst, value) in enumerate(zeros):
                pool.memset(dst, value).then_inc(zero_ready, 1)
                pool.wait_ge(zero_ready, n + 1)
            PER = 3 * NROT
            with pool.Fori(0, KT) as i:
                ch.turn(i, PER)
                pool.wait_ge(rot_used, i + 1)
                for k in range(NROT):
                    n = 1 << k
                    rot = lambda r: m.pt[:, r + k, bass.ds(i * GB, GB)].rearrange("p (g o) -> p g o", o=1).to_broadcast([P, GB, n])
                    c0, s0, c1, s1 = ec[:, :, 0:n], es[:, :, 0:n], ec[:, :, n:2 * n], es[:, :, n:2 * n]
                    pool.tensor_tensor(rt1[:, :, 0:n], c0, rot(ROTC), ALU.mult)
                    ch(pool.tensor_tensor(rt2[:, :, 0:n], s0, rot(ROTS), ALU.mult))
                    pool.tensor_tensor(c1, rt1[:, :, 0:n], rt2[:, :, 0:n], ALU.subtract)
                    pool.tensor_tensor(s1, c0, rot(ROTS), ALU.mult)
                    ch(pool.tensor_tensor(rt3[:, :, 0:n], s0, rot(ROTC), ALU.mult))
                    q = pool.tensor_tensor(s1, s1, rt3[:, :, 0:n], ALU.add)
                    ch(q)
                pool.sem_inc(rot_ready, 1)
            assert ch.n == PER

        @blk.scalar
        def _(act):
            act.wait_ge(zero_ready, 6)
            act.sem_inc(regrouped, 1)

            def regroup(i):
                act.wait_ge(x_in, i * 16 + 16)
                act.wait_ge(xs_in, i * 16 + 16)
                act.copy(xg.rearrange("c g (t h) -> c g t h", h=GC), xnat[:].rearrange("c t (g h) -> c g t h", h=GC))
                act.copy(xsg[:].rearrange("c g (t h) -> c g t h", h=GC),
                         xsh[:].rearrange("c t (g h) -> c g t h", h=GC)).then_inc(regrouped, 1)

            def turn(i, s, last):
                act.wait_ge(u_turned, i + 1)
                for g in range(GB):
                    act.activation(u[:, g, 0:NCK], m.ps[:, g // 4, (g % 4) * P:(g % 4 + 1) * P], ACT.Identity,
                                   scale=m.spread[:, 1, bass.ds(i * GB + g, 1)], bias=m.spread[:, 0, bass.ds(i * GB + g, 1)])
                act.copy(u[:, :, NCK:NU],
                         m.ps[:, 6, 0:GB * NB].rearrange("p (g b) -> p g b", b=NB)).then_inc(u_out, 1)
                act.wait_ge(w_turned, i + 1)
                act.copy(w[:], m.ps[:, 4:6, :].rearrange("p u (g q) -> p (u g) q", q=P))
                for h in range(2):
                    q = act.copy(wx[:, :, h * NP:(h + 1) * NP],
                                 m.ps[:, 4:6, :].rearrange("p u (g q) -> p (u g) q", q=P)[:, :, (1 - h) * NP:(2 - h) * NP])
                q.then_inc(w_out, 1)
                if not last:
                    regroup(i + 1)
                act.wait_ge(y_done, i + 2)
                act.activation(gy[:].rearrange("c t (g h) -> c g t h", h=GC),
                               m.ps[:, 4:6, :].rearrange("c u (g t h) -> c (u g) t h", h=GC, t=L), ACT.Gelu_apprx_tanh)
                act.activation(gys.rearrange("b t (g h) -> b g t h", h=GC),
                               m.ps[0:NB, 7, :].rearrange("b (g t h) -> b g t h", h=GC, t=ST),
                               ACT.Gelu_apprx_tanh).then_inc(gelu_out, 1)
                act.wait_ge(g_turned, i + 2)
                act.copy(m.hhi[:, bass.ds(i, 1), 0:SEQ].rearrange("p o (c t) -> p (o t) c", t=L),
                         m.ps[:, 0:2, :].rearrange("p u (t c) -> p (u t) c", c=NCK))
                act.copy(m.hhi[:, bass.ds(i, 1), SEQ:NT].rearrange("p o (b t) -> p (o t) b", t=ST),
                         m.ps[:, 6, 0:NS].rearrange("p (t b) -> p t b", b=NB)).then_inc(g_hi, 1)

            regroup(0)
            turns(act, turn)

        @blk.tensor
        def _(pe):
            pe.sem_inc(g_turned, 1)
            pe.sem_inc(y_done, 1)
            bank = lambda b, g: m.ps[:, b + g // 4, (g % 4) * P:(g % 4 + 1) * P]

            def turn(i, s, last):
                v1, v2, h0cur = v1s[:, s], v2s[:, s], h0s[:, s]
                pe.wait_ge(regrouped, i + 2)
                pe.wait_ge(g_lo, i + 1)
                for g in range(GB):
                    pe.transpose(bank(0, g), xg[:, g, :], m.ident[:])
                for g in range(GB):
                    q = pe.transpose(m.ps[:, 6, g * NB:(g + 1) * NB], xsg[:, g, :], m.ident[0:NB, 0:NB])
                q.then_inc(u_turned, 1)
                pe.wait_ge(gen, i + 1)
                for g in range(GB):
                    q = pe.transpose(bank(4, g), wt[:, g, :, :], m.ident[:])
                q.then_inc(w_turned, 1)
                pe.wait_ge(u_out, i + 1)
                for g in range(GB):
                    q = pe.matmul(m.ps[0:GC, 7 - g // 4, (g % 4) * P:(g % 4 + 1) * P], bcur[:, g, :], v1[:, g, 0:L, :],
                                  start=True, stop=True)
                q.then_inc(k_done, 1)
                pe.wait_ge(w_out, i + 1)
                for g in range(GB):
                    pe.matmul(bank(0, g), w[:, g, :], u[:, g, 0:NCK], start=True, stop=True)
                pe.wait_ge(xs_out, i + 1)
                for g in range(GB):
                    pe.matmul(bank(2, g), wx[:, g, :], u[:, g, 0:NCK], start=True, stop=True)
                pe.wait_ge(kb_ready, i + 1)
                for g in range(GB):
                    q = pe.matmul(m.ps[:, 6, g * NB:(g + 1) * NB], w[:, g, :], u[:, g, NCK:NU], start=True, stop=True)
                q.then_inc(xx_done, 1)
                pe.wait_ge(tz_in, i * (16 * L) + 16 * L)
                pe.wait_ge(pq_ready, i + 1)
                for g in range(GB):
                    pe.matmul(bank(4, g), u[:, g, 0:NCK], tz[:, g, :], start=True, stop=False)
                    pe.matmul(bank(4, g), pb[:, g, 0:NCK], v1[:, g, 1:NPOW, :], start=False, stop=False)
                    pe.matmul(bank(4, g), qb[:, g, 0:NCK], v2[:, g, :, :], start=False, stop=True)
                for g in range(GB):
                    out = m.ps[0:NB, 7, g * 64:(g + 1) * 64]
                    pe.matmul(out, u[:, g, NCK:NU], tz[:, g, 64:P], start=True, stop=False)
                    q = pe.matmul(out, h0cur[:, g, :], v1[:, g, 1:1 + ST, :], start=False, stop=True)
                q.then_inc(y_done, 1)
                pe.wait_ge(gelu_out, i + 1)
                pe.wait_ge(xs_out, i + 2)
                for t in range(L):
                    pe.transpose(bank(0, t), gy[:, t, :], m.ident[:])
                for t in range(ST):
                    q = pe.transpose(m.ps[:, 6, t * NB:(t + 1) * NB], gys[:, t, :], m.ident[0:NB, 0:NB])
                q.then_inc(g_turned, 1)

            turns(pe, turn)
            pe.wait_ge(g_lo, KT + 1)
            pe.matmul(m.ps[0:G, 0, 0:P], pend[:], m.ident[:], start=True, stop=False)
            pe.matmul(m.ps[0:G, 0, 0:P], qend[:], m.swap[:], start=False, stop=True).then_inc(st_done, 1)
            for b in range(NB):
                q = pe.transpose(m.ps[0:G, 1 + b // 4, (b % 4) * P:(b % 4 + 1) * P], ss[:, b, :], m.ident[:])
            q.then_inc(st_done, 1)

        @blk.vector
        def _(v):
            ch = Chain(v, dve_chain)
            tt = v.tensor_tensor
            v.sem_inc(rot_used, 1)
            v.sem_inc(g_lo, 1)
            v.sem_inc(xs_out, 1)
            v.wait_ge(zero_ready, 6)

            def generate(i, s):
                v1, v2, h0cur, h0xcur = v1s[:, s], v2s[:, s], h0s[:, s], h0xs[:, s]
                gsl = bass.ds(i * GB, GB)
                pw = lambda first, n, rev=False: (m.ptr if rev else m.pt)[:, first:first + n, gsl].rearrange(
                    "p n (g o) -> p g n o", o=1).to_broadcast([P, GB, n, GC])
                bm = lambda x, n: x[:, gsl, :].rearrange("p g (o h) -> p g o h", o=1).to_broadcast([P, GB, n, GC])
                cm = lambda x, n: x[:, bass.ds(i, 1), :].rearrange("p o (g h) -> p g o h", h=GC).to_broadcast([P, GB, n, GC])
                tg9, tg8 = (tg[:, :, 0:n * GC].rearrange("p g (n h) -> p g n h", h=GC) for n in (NPOW, L))
                tt(wt[:], pw(0, L, True), bm(m.bst, L), ALU.mult)
                ch(tt(tg8, pw(L, L, True), bm(m.bsw, L), ALU.mult))
                ch(tt(wt[:], wt[:], tg8, ALU.add))
                tt(v1, pw(0, NPOW), cm(m.cst, NPOW), ALU.mult)
                ch(tt(tg9, pw(IMP, NPOW), cm(m.csx, NPOW), ALU.mult))
                ch(tt(v1, v1, tg9, ALU.subtract))
                tt(v2, pw(1, L), cm(m.csx, L), ALU.mult)
                ch(tt(tg8, pw(IMP + 1, L), cm(m.cst, L), ALU.mult))
                v.tensor_scalar(bcur[:], m.bst[:, gsl, :], 1.0, None, ALU.mult)
                v.tensor_copy(h0cur, m.h0s[:, :, gsl].rearrange("p b g -> p g b"))
                v.tensor_copy(h0xcur, m.h0x[:, :, gsl].rearrange("p b g -> p g b"))
                tt(v2, v2, tg8, ALU.add).then_inc(gen, 1)

            def turn(i, s, last):
                h0cur, h0xcur, gsl = h0s[:, s], h0xs[:, s], bass.ds(i * GB, GB)
                ch.turn(i, PER, before)
                v.wait_ge(k_done, i + 1)
                v.tensor_copy(kb[:, 0:4, (L - 1) * GC:], m.ps[0:GC, 7, :].rearrange("h (g q) -> h g q", q=P))
                ch(v.tensor_copy(kb[:, 4:8, (L - 1) * GC:], m.ps[0:GC, 6, :].rearrange("h (g q) -> h g q", q=P)))
                tt(kb[:, :, (L - 1) * GC:L * GC], kb[:, :, (L - 1) * GC:L * GC], m.dskipd[:, gsl, :],
                   ALU.add).then_inc(kb_ready, 1)
                v.wait_ge(xx_done, i + 1)
                v.wait_ge(rot_ready, i + 1)
                banks = lambda b: m.ps[:, b:b + 2, :].rearrange("p u (g c) -> p (u g) c", c=NCK)
                tt(xs, banks(0), ec[:], ALU.mult)
                ch(tt(xm, banks(2), es[:], ALU.mult))
                ch(tt(xm, xs, xm, ALU.add))
                for g in range(GB):
                    q = v.tensor_tensor_scan(xs[:, g, :], m.pt[:, R8, bass.ds(i * GB + g, 1)].to_broadcast([P, NCK]),
                                             xm[:, g, :], 0.0, ALU.mult, ALU.add)
                ch(q)
                tt(pb[:, :, 1:NCK + 1], xs, ec[:], ALU.mult)
                q = tt(qb[:, :, 1:NCK + 1], xs, es[:], ALU.mult)
                q.then_inc(pq_ready, 1)
                v.wait_ge(pq_ready, i + 1)
                v.sem_inc(rot_used, 1)
                v.tensor_scalar(pend[:, gsl], pb[:, :, NCK], 1.0, None, ALU.mult)
                v.tensor_copy(qend[:, gsl], qb[:, :, NCK])
                p4 = lambda r: m.pt[:, r + ST, gsl].rearrange("p (g o) -> p g o", o=1).to_broadcast([P, GB, NB])
                t1, t2 = tg[:, :, 0:NB], tg[:, :, NB:2 * NB]
                tt(t1, h0cur, p4(0), ALU.mult)
                ch(tt(t2, h0xcur, p4(IMP), ALU.mult))
                ch(tt(t1, t1, t2, ALU.add))
                tt(ss[:, :, gsl].rearrange("p b g -> p g b"), t1,
                   m.ps[:, 6, 0:GB * NB].rearrange("p (g b) -> p g b", b=NB), ALU.add).then_inc(xs_out, 1)
                v.wait_ge(xs_out, i + 2)
                if not last:
                    generate(i + 1, 1 - s)
                v.wait_ge(g_hi, i + 1)
                for dst, src in (
                    (lambda x: x[:, bass.ds(i, 1), 0:SEQ].rearrange("p o (c t) -> p (o t) c", t=L),
                     m.ps[:, 0:2, :].rearrange("p u (t c) -> p (u t) c", c=NCK)),
                    (lambda x: x[:, bass.ds(i, 1), SEQ:NT].rearrange("p o (b t) -> p (o t) b", t=ST),
                     m.ps[:, 6, 0:NS].rearrange("p (t b) -> p t b", b=NB))):
                    q = tt(dst(m.hlo), src, dst(m.hhi).bitcast(F32), ALU.subtract)
                q.then_inc(g_lo, 1)

            generate(0, 0)
            before, PER = ch.n, 11
            turns(v, turn)
            assert ch.n == PER - before, ch.n
            v.wait_ge(st_done, 1)
            v.tensor_copy(sout[:, 0, :], m.ps[0:G, 0, 0:P]).then_inc(st_copied, 1)
            v.wait_ge(st_done, 2)
            v.tensor_copy(sout[:, 1:NC9, :], m.ps[0:G, 1:3, :].rearrange("g u (b q) -> g (u b) q", q=P)).then_inc(st_copied, 1)


class Stream:

    def __init__(self, nc, c, name):
        sb = lambda n, d=F32: c.enter_context(nc.sbuf_tensor(f"{name}_{n}", [P, 2, KT * WC], d))
        self.ahead = 0
        self.raw, self.hi, self.lo = sb("wraw"), sb("whi", F32R), sb("wlo", F32R)

    def sems(self, nc, c, name):
        signal = c.enter_context(semaphores(nc))
        S = lambda n: signal(f"{name}_{n}")
        self.landed = [S("landed0"), S("landed1")]
        self.hi_ready, self.lo_ready = S("hi_ready"), S("lo_ready")

    def load(self, sp, n, slot, src, parts=KT):
        sp.wait_ge(self.hi_ready, n + 1)
        sp.wait_ge(self.lo_ready, n + 1)
        sp.dma_start(self.raw[:, slot].rearrange("p (k n) -> p k n", k=parts), src).then_inc(self.landed[slot], 16)

    def prime(self, S):
        self.first_in, self.first_hi, self.first_lo = [S("w_in0"), S("w_in1")], S("w_hi"), S("w_lo")
        self.ahead = 2

    def prime_load(self, sp, w):
        for j in range(2):
            sp.dma_start(self.raw[:, j].rearrange("p (k n) -> p k n", k=KT), w[:, :, j * WC:(j + 1) * WC]
                         ).then_inc(self.first_in[j], 16)

    def prime_hi(self, act, j, landed=16):
        act.wait_ge(self.first_in[j], landed)
        act.copy(self.hi[:, j], self.raw[:, j]).then_inc(self.first_hi, 1)

    def prime_lo(self, pool):
        for j in range(2):
            pool.wait_ge(self.first_hi, j + 1)
            pool.tensor_tensor(self.lo[:, j], self.raw[:, j], self.hi[:, j].bitcast(F32), ALU.subtract
                               ).then_inc(self.first_lo, 1)

    def start_hi(self, act):
        act.sem_inc(self.hi_ready, 2 + self.ahead)

    def cut_hi(self, act, slot, landed, done=None, count=None):
        act.wait_ge(self.landed[slot], landed - 8 * self.ahead)
        if done is not None:
            act.wait_ge(done, count)
        act.copy(self.hi[:, slot], self.raw[:, slot]).then_inc(self.hi_ready, 1)

    def start_lo(self, pool):
        pool.sem_inc(self.lo_ready, 2 + self.ahead)

    def cut_lo(self, pool, n, slot):
        pool.wait_ge(self.hi_ready, n + 3)
        pool.tensor_tensor(self.lo[:, slot], self.raw[:, slot], self.hi[:, slot].bitcast(F32),
                           ALU.subtract).then_inc(self.lo_ready, 1)

    def wait_cut(self, pe, n):
        pe.wait_ge(self.lo_ready, n + 3)

    def parts(self, slot, k):
        return tuple(x[:, slot].rearrange("p (k n) -> p k n", k=k) for x in (self.hi, self.lo))


def three_pass(pe, out, lhs, rhs, first, last):
    pe.matmul(out, lhs[0], rhs[0], start=first, stop=False)
    pe.matmul(out, lhs[1], rhs[0], start=False, stop=False)
    return pe.matmul(out, lhs[0], rhs[1], start=False, stop=last)


def chunk(n):
    return slice(n * CH, (n + 1) * CH)


def gated_add(v, ch, m, src, gate, tile, n, free, tmp):
    w = LASTP if n == NCH - 1 else CH
    gp = m.modt[:, bass.ds(tile + gate * KT, 1), 0:1].rearrange("p o b -> p (o b)")
    xt = m.x[:, bass.ds(tile, 1), :].rearrange("p o t -> p (o t)")
    if n == NCH - 1:
        gs = m.modt[:, bass.ds(tile + gate * KT, 1), 1:NC9].rearrange("p o (b u) -> p (o b) u", u=1).to_broadcast([P, NB, ST])
        ch(v.tensor_tensor(tmp.rearrange("p (b t) -> p b t", t=ST), src[:, w:CH].rearrange("p (b t) -> p b t", t=ST),
                           gs, ALU.mult))
        ch(v.tensor_tensor(xt[:, SEQ:NT], xt[:, SEQ:NT], tmp, ALU.add))
    q = v.scalar_tensor_tensor(xt[:, n * CH:n * CH + w], src[:, 0:w], gp, xt[:, n * CH:n * CH + w], ALU.mult, ALU.add)
    if free is not None:
        q.then_inc(free, 1)


def glu_halves(a, st, slot, first):
    view = st.raw[:, slot].rearrange("p (h k n) -> p h k n", h=2, n=P)
    return [(view[:, h], w[0].rearrange("(k p) n -> p k n", p=P)[:, :, bass.ds(first, P)])
            for h, w in enumerate((a["ssm_w_glu_a"], a["ssm_w_glu_b"]))]


def residual_block(nc, a, m, st):
    with ExitStack() as c:
        SLOTS = 4
        rows = c.enter_context(nc.sbuf_tensor("r_rows", [P, SLOTS, D], F32, side="right"))
        signal = c.enter_context(semaphores(nc))
        S = lambda n: signal(n)
        landed, turned, copied = [S(f"r_landed{t}") for t in range(SLOTS)], S("r_turned"), S("r_copied")
        st.prime(S)
        blk = c.enter_context(nc.Block())
        tiles = [(a["x_prompt"][0, t * P:(t + 1) * P, :], P) for t in range(SEQ // P)]
        tiles.append((a["x_sample"].rearrange("b t f -> (b t) f"), NS))

        @blk.sync
        def _(sp):
            for t, (src, n) in enumerate(tiles):
                if t >= SLOTS:
                    sp.wait_ge(turned, t - SLOTS + 1)
                sp.dma_start(rows[0:n, t % SLOTS, :], src).then_inc(landed[t % SLOTS], 16)
            for j in range(2):
                for dst, src in glu_halves(a, st, j, j * P):
                    sp.dma_start(dst, src).then_inc(st.first_in[j], 16)

        @blk.gpsimd
        def _(pool):
            st.prime_lo(pool)

        @blk.tensor
        def _(pe):
            for t, (_, n) in enumerate(tiles):
                pe.wait_ge(landed[t % SLOTS], 16 * (t // SLOTS + 1))
                if t >= 4:
                    pe.wait_ge(copied, t - 3)
                for k in range(KT):
                    q = pe.transpose(m.ps[:, 2 * (t % 4) + k // 4, (k % 4) * P:(k % 4) * P + n],
                                     rows[0:n, t % SLOTS, k * P:(k + 1) * P], m.ident[0:n, 0:n])
                q.then_inc(turned, 1)

        @blk.scalar
        def _(act):
            for t, (_, n) in enumerate(tiles):
                act.wait_ge(turned, t + 1)
                act.mul(m.x[:, :, t * P:t * P + n],
                        m.ps[:, 2 * (t % 4):2 * (t % 4) + 2, :].rearrange("p u (k q) -> p (u k) q", q=P)[:, :, 0:n],
                        ALPHA).then_inc(copied, 1)
            for j in range(2):
                st.prime_hi(act, j, 32)


def glu_block(nc, a, m, st):
    with ExitStack() as c:
        sb = lambda n, s, d=F32: c.enter_context(nc.sbuf_tensor(n, s, d, side="right"))
        signal = c.enter_context(semaphores(nc))
        S = lambda n: signal(n)
        sig, prod, tmp = sb("g_sig", [P, 2, CH]), sb("g_prod", [P, 2, CH]), sb("g_tmp", [P, NS])
        st.sems(nc, c, "g")
        pair_done, sig_ready, pair_out, chain = S("g_pair"), S("g_sig_ready"), S("g_out"), S("g_dve")
        blk = c.enter_context(nc.Block())
        TURNS, PAIRS = D // WC, 2 * NCH
        halves = lambda x: [x[:, h * KT * P:(h + 1) * KT * P].rearrange("p (k n) -> p k n", n=P) for h in range(2)]

        @blk.sync
        def _(sp):
            with sp.Fori(0, TURNS - 1) as i:
                for j in range(2):
                    sp.wait_ge(st.hi_ready, i * 2 + j + 3)
                    sp.wait_ge(st.lo_ready, i * 2 + j + 3)
                    for dst, src in glu_halves(a, st, j, (i + 1) * WC + j * P):
                        sp.dma_start(dst, src).then_inc(st.landed[j], 16)

        @blk.gpsimd
        def _(pool):
            st.start_lo(pool)
            with pool.Fori(0, TURNS - 1) as i:
                for j in range(2):
                    st.cut_lo(pool, i * 2 + 2 + j, j)

        @blk.scalar
        def _(act):
            def sigmoids(i, j):
                for p in range(j * NCH, (j + 1) * NCH):
                    act.wait_ge(pair_done, i * PAIRS + p + 1)
                    act.wait_ge(pair_out, i * PAIRS + p + 2)
                    act.activation(sig[:, p % 2], m.ps[:, 2 * (p % 3) + 1, 0:CH], ACT.Sigmoid).then_inc(sig_ready, 1)

            st.start_hi(act)
            with act.Fori(0, TURNS - 1) as i:
                for j in range(2):
                    sigmoids(i, j)
                    st.cut_hi(act, j, i * 32 + 48, pair_done, i * PAIRS + (j + 1) * NCH)
            for j in range(2):
                sigmoids(TURNS - 1, j)

        @blk.vector
        def _(v):
            ch = Chain(v, chain)
            v.sem_inc(pair_out, 3)
            with v.Fori(0, TURNS) as i:
                ch.turn(i, 4)
                for p in range(PAIRS):
                    v.wait_ge(sig_ready, i * PAIRS + p + 1)
                    v.tensor_tensor(prod[:, p % 2], m.ps[:, 2 * (p % 3), 0:CH], sig[:, p % 2],
                                    ALU.mult).then_inc(pair_out, 1)
                    v.wait_ge(pair_out, i * PAIRS + p + 4)
                    gated_add(v, ch, m, prod[:, p % 2], 2, i * 2 + p // NCH, p % NCH, None, tmp[:])
            assert ch.n == 4, ch.n

        @blk.tensor
        def _(pe):
            with pe.Fori(0, TURNS) as i:
                for p in range(PAIRS):
                    if p % NCH == 0:
                        st.wait_cut(pe, i * 2 + p // NCH)
                    pe.wait_ge(pair_out, i * PAIRS + p + 1)
                    hi, lo = halves(st.hi[:, p // NCH]), halves(st.lo[:, p // NCH])
                    for j in range(2):
                        for k in range(KT):
                            q = three_pass(pe, m.ps[:, 2 * (p % 3) + j, 0:CH], (hi[j][:, k], lo[j][:, k]),
                                           [x[:, k, chunk(p % NCH)] for x in (m.hhi, m.hlo)], k == 0, k == KT - 1)
                    q.then_inc(pair_done, 1)


def norm_block(nc, a, m, n, name, st=None, w=None):
    last = n == 3
    with ExitStack() as c:
        sb = lambda nn, s, d=F32: c.enter_context(nc.sbuf_tensor(name + nn, s, d, side="right"))
        signal = c.enter_context(semaphores(nc))
        S = lambda nn: signal(name + nn)
        work, std, rstd = sb("work", [P, NCH, KT, CH]), sb("std", [P, NCH, CH]), sb("rstd", [P, 2, CH])
        mean_done, centred, squared, var_done = S("mean"), S("centred"), S("squared"), S("var")
        sample_ready = S("sample")
        std_ready, scaled, h_ready, hi_ready, lo_ready, chain = (
            S("stdr"), S("scaled"), S("h"), S("hi"), S("lo"), S("dve"))
        if w is not None:
            st.prime(S)
        blk = c.enter_context(nc.Block())

        @blk.sync
        def _(sp):
            if w is not None:
                st.prime_load(sp, w)
        coef = lambda x, o: x[:, n * KT + o:n * KT + o + 1]
        bank = lambda i, j: m.ps[:, (2 * i + j) % 6, 0:CH]

        @blk.tensor
        def _(pe):
            for i in range(NCH):
                for k in range(KT):
                    q = pe.matmul(bank(i, 0), m.ones[:], m.x[:, k, chunk(i)], start=(k == 0), stop=(k == KT - 1))
                q.then_inc(mean_done, 1)
            for i in range(NCH):
                pe.wait_ge(squared, i + 1)
                for k in range(KT):
                    q = pe.matmul(bank(i, 1), m.ones[:], work[:, i, k, :], start=(k == 0), stop=(k == KT - 1))
                q.then_inc(var_done, 1)

        @blk.scalar
        def _(act):
            for i in range(NCH):
                act.wait_ge(centred, i + 1)
                act.activation(work[:, i], m.x[:, :, chunk(i)], ACT.Square).then_inc(squared, 1)
                if w is not None and i < 2:
                    st.prime_hi(act, i)

            def deviation(i):
                act.wait_ge(var_done, i + 1)
                act.activation(std[:, i], bank(i, 1), ACT.Sqrt, bias=m.eps[:]).then_inc(std_ready, 1)

            deviation(0)
            for i in range(NCH):
                if i + 1 < NCH:
                    deviation(i + 1)
                if last:
                    continue
                act.wait_ge(scaled, i + 1)
                width = LASTP if i == NCH - 1 else CH
                for k in range(KT):
                    q = act.activation(work[:, i, k, 0:width], m.x[:, k, i * CH:i * CH + width], ACT.Identity,
                                       scale=m.cs[:, n, k, 0:1], bias=m.cb[:, n, k, 0:1])
                q.then_inc(h_ready, 1)
                act.wait_ge(h_ready, i + 1)
                if i == NCH - 1:
                    act.wait_ge(sample_ready, 1)
                act.copy(m.hhi[:, :, chunk(i)], work[:, i]).then_inc(hi_ready, 1)

        @blk.gpsimd
        def _(pool):
            if last:
                return
            st.prime_lo(pool)
            for i in range(NCH):
                pool.wait_ge(hi_ready, i + 1)
                pool.tensor_tensor(m.hlo[:, :, chunk(i)], work[:, i], m.hhi[:, :, chunk(i)].bitcast(F32),
                                   ALU.subtract).then_inc(lo_ready, 1)
            pool.wait_ge(lo_ready, NCH)

        @blk.vector
        def _(v):
            ch = Chain(v, chain)
            wide = lambda x: x.rearrange("p (o t) -> p o t", o=1).to_broadcast([P, KT, CH])
            for i in range(NCH):
                v.wait_ge(mean_done, i + 1)
                v.tensor_tensor(m.x[:, :, chunk(i)], m.x[:, :, chunk(i)], wide(bank(i, 0)), ALU.subtract).then_inc(centred, 1)
            for i in range(NCH):
                v.wait_ge(std_ready, i + 1)
                ch(v.reciprocal(rstd[:, i % 2], std[:, i]))
                v.wait_ge(squared, i + 1)
                v.tensor_tensor(m.x[:, :, chunk(i)], m.x[:, :, chunk(i)], wide(rstd[:, i % 2]), ALU.mult).then_inc(scaled, 1)
                if i == NCH - 1 and not last:
                    v.wait_ge(scaled, i + 1)
                    four = lambda x: x[:, n, :, 1:NC9].rearrange("p k (b o) -> p k b o", o=1).to_broadcast([P, KT, NB, ST])
                    dst = work[:, i, :, LASTP:CH].rearrange("p k (b t) -> p k b t", t=ST)
                    ch(v.tensor_tensor(dst, m.x[:, :, SEQ:NT].rearrange("p k (b t) -> p k b t", t=ST), four(m.cs), ALU.mult))
                    v.tensor_tensor(dst, dst, four(m.cb), ALU.add).then_inc(sample_ready, 1)
            for i in range(NCH):
                if last:
                    v.wait_ge(scaled, i + 1)
                else:
                    v.wait_ge(h_ready, i + 1)
                if i == NCH - 1 and not last:
                    v.wait_ge(sample_ready, 1)
                for k in range(KT):
                    q = v.tensor_scalar(m.x[:, k, chunk(i)], m.x[:, k, chunk(i)], coef(m.lna, k), coef(m.lna, 32 + k),
                                        ALU.mult, ALU.add)
            ch(q)


def remod_block(nc, a, m, st, w):
    with ExitStack() as c:
        work = c.enter_context(nc.sbuf_tensor("q_work", [P, 2, KT, CH], F32, side="right"))
        signal = c.enter_context(semaphores(nc))
        S = lambda n: signal("q_" + n)
        h_ready, s_ready, hi_ready, lo_ready, chain = S("h"), S("s"), S("hi"), S("lo"), S("dve")
        st.prime(S)
        blk = c.enter_context(nc.Block())

        @blk.sync
        def _(sp):
            st.prime_load(sp, w)

        @blk.scalar
        def _(act):
            for i in range(NCH):
                if i >= 2:
                    act.wait_ge(lo_ready, i - 1)
                width = LASTP if i == NCH - 1 else CH
                for k in range(KT):
                    q = act.activation(work[:, i % 2, k, 0:width], m.x[:, k, i * CH:i * CH + width], ACT.Identity,
                                       scale=m.cs[:, 3, k, 0:1], bias=m.cb[:, 3, k, 0:1])
                q.then_inc(h_ready, 1)
                act.wait_ge(h_ready, i + 1)
                if i == NCH - 1:
                    act.wait_ge(s_ready, 1)
                act.copy(m.hhi[:, :, chunk(i)], work[:, i % 2]).then_inc(hi_ready, 1)
                if i == 0:
                    st.prime_hi(act, 0)
                    st.prime_hi(act, 1)

        @blk.gpsimd
        def _(pool):
            for i in range(NCH):
                pool.wait_ge(hi_ready, i + 1)
                pool.tensor_tensor(m.hlo[:, :, chunk(i)], work[:, i % 2], m.hhi[:, :, chunk(i)].bitcast(F32),
                                   ALU.subtract).then_inc(lo_ready, 1)
                if i == 0:
                    st.prime_lo(pool)

        @blk.vector
        def _(v):
            ch = Chain(v, chain)
            v.wait_ge(lo_ready, 1)
            four = lambda x: x[:, 3, :, 1:NC9].rearrange("p k (b o) -> p k b o", o=1).to_broadcast([P, KT, NB, ST])
            dst = work[:, 0, :, LASTP:CH].rearrange("p k (b t) -> p k b t", t=ST)
            ch(v.tensor_tensor(dst, m.x[:, :, SEQ:NT].rearrange("p k (b t) -> p k b t", t=ST), four(m.cs), ALU.mult))
            v.tensor_tensor(dst, dst, four(m.cb), ALU.add).then_inc(s_ready, 1)


def mlp_block(nc, a, m, st, layer):
    name = f"m{layer}_"
    with ExitStack() as c:
        sb = lambda n, s, d=F32: c.enter_context(nc.sbuf_tensor(name + n, s, d, side="right"))
        signal = c.enter_context(semaphores(nc))
        S = lambda n: signal(name + n)
        HK, TURNS = 4, 8
        khi, klo = sb("khi", [P, HK, NT], F32R), sb("klo", [P, HK, NT], F32R)
        relu, sq, tmp = sb("relu", [P, 2, CH]), sb("sq", [P, 2, CH]), sb("tmp", [P, NS])
        st.sems(nc, c, name)
        up_done, down_done, relu_ready, bank_free, hi_ready, hid_ready, chain = (
            S("up"), S("down"), S("relu_r"), S("free"), S("khi_r"), S("hid"), S("dve"))
        blk = c.enter_context(nc.Block())
        UP, DOWN = HK * NCH, KT * NCH
        w1 = a["mlp_w1"][layer].rearrange("(k p) n -> p k n", p=P)
        w2 = a["mlp_w2"][layer].rearrange("(k p) n -> p k n", p=P)

        @blk.sync
        def _(sp):
            def load_w2(e):
                for j in range(2):
                    st.load(sp, e * 4 + 2 + j, j, w2[:, bass.ds(e * HK, HK), j * 512:(j + 1) * 512], HK)

            with sp.Fori(0, TURNS - 1) as e:
                load_w2(e)
                for j in range(2):
                    st.load(sp, e * 4 + 4 + j, j, w1[:, :, bass.ds((e + 1) * (HK * P) + j * WC, WC)])
            load_w2(TURNS - 1)

        @blk.gpsimd
        def _(pool):
            def lows(e, groups):
                for g in groups:
                    pool.wait_ge(hi_ready, e * UP + g + 1)
                    f, n = divmod(g, NCH)
                    pool.tensor_tensor(klo[:, f, chunk(n)], sq[:, g % 2], khi[:, f, chunk(n)].bitcast(F32),
                                       ALU.subtract).then_inc(hid_ready, 1)

            def turn(e, first, last):
                if not first:
                    st.cut_lo(pool, e * 4 + 1, 1)
                lows(e, range(UP // 2))
                st.cut_lo(pool, e * 4 + 2, 0)
                lows(e, range(UP // 2, UP))
                st.cut_lo(pool, e * 4 + 3, 1)
                if not last:
                    st.cut_lo(pool, e * 4 + 4, 0)

            st.start_lo(pool)
            turn(0, True, False)
            with pool.Fori(1, TURNS - 1) as e:
                turn(e, False, False)
            turn(TURNS - 1, False, True)

        @blk.scalar
        def _(act):
            def squares(e, groups):
                for g in groups:
                    f, n = divmod(g, NCH)
                    act.wait_ge(up_done, e * UP + g + 1)
                    act.activation(relu[:, g % 2], m.ps[:, g % 6, 0:CH], ACT.Relu).then_inc(relu_ready, 1)
                    act.wait_ge(bank_free, e * (UP + DOWN) + g + 7)
                    act.copy(khi[:, f, chunk(n)], sq[:, g % 2]).then_inc(hi_ready, 1)

            def turn(e, first, last):
                if not first:
                    st.cut_hi(act, 1, e * 32 + 16, down_done, e * DOWN + DOWN)
                squares(e, range(UP // 2))
                st.cut_hi(act, 0, e * 32 + 32, up_done, e * UP + UP // 2)
                squares(e, range(UP // 2, UP))
                st.cut_hi(act, 1, e * 32 + 32, up_done, e * UP + UP)
                if not last:
                    st.cut_hi(act, 0, e * 32 + 48, down_done, e * DOWN + DOWN + DOWN // 2)

            st.start_hi(act)
            turn(0, True, False)
            with act.Fori(1, TURNS - 1) as e:
                turn(e, False, False)
            turn(TURNS - 1, False, True)

        @blk.vector
        def _(v):
            ch = Chain(v, chain)
            v.sem_inc(bank_free, 6)
            with v.Fori(0, TURNS) as e:
                ch.turn(e, 2 * KT)
                for g in range(UP):
                    v.wait_ge(relu_ready, e * UP + g + 1)
                    if g >= 2:
                        v.wait_ge(hid_ready, e * UP + g - 1)
                    v.scalar_tensor_tensor(sq[:, g % 2], m.ps[:, g % 6, 0:CH], 0.0, relu[:, g % 2], ALU.max,
                                           ALU.mult).then_inc(bank_free, 1)
                for g in range(DOWN):
                    v.wait_ge(down_done, e * DOWN + DOWN + g + 1)
                    gated_add(v, ch, m, m.ps[:, g % 6, 0:CH], 6 * layer + 5, g // NCH, g % NCH, bank_free, tmp[:])
            assert ch.n == 2 * KT, ch.n

        @blk.tensor
        def _(pe):
            pe.sem_inc(down_done, DOWN)
            with pe.Fori(0, TURNS) as e:
                for g in range(UP):
                    f, n = divmod(g, NCH)
                    if g % (UP // 2) == 0:
                        st.wait_cut(pe, e * 4 + f // 2)
                    w = st.parts(f // 2, KT)
                    cols = slice((f % 2) * P, (f % 2 + 1) * P)
                    pe.wait_ge(bank_free, e * (UP + DOWN) + g + 1)
                    for k in range(KT):
                        q = three_pass(pe, m.ps[:, g % 6, 0:CH], [x[:, k, cols] for x in w],
                                       [x[:, k, chunk(n)] for x in (m.hhi, m.hlo)], k == 0, k == KT - 1)
                    q.then_inc(up_done, 1)
                for g in range(DOWN):
                    t, n = divmod(g, NCH)
                    if g % (DOWN // 2) == 0:
                        st.wait_cut(pe, e * 4 + 2 + t // 4)
                    w = st.parts(t // 4, HK)
                    cols = slice((t % 4) * P, (t % 4 + 1) * P)
                    pe.wait_ge(bank_free, e * (UP + DOWN) + UP + g + 1)
                    for k in range(HK):
                        if t == 0:
                            pe.wait_ge(hid_ready, e * UP + k * NCH + n + 1)
                        q = three_pass(pe, m.ps[:, g % 6, 0:CH], [x[:, k, cols] for x in w],
                                       [x[:, k, chunk(n)] for x in (khi, klo)], k == 0, k == HK - 1)
                    q.then_inc(down_done, 1)


def column_block(nc, a, m, st, name, w, gate=None, dst=None, save=None):
    with ExitStack() as c:
        sb = lambda n, s, d=F32: c.enter_context(nc.sbuf_tensor(name + n, s, d, side="right"))
        signal = c.enter_context(semaphores(nc))
        S = lambda n: signal(name + n)
        stage, tmp = sb("stage", [P, 2, NT]), sb("tmp", [P, NS])
        st.sems(nc, c, name)
        done, bank_free, stored, staged, chain = S("done"), S("free"), [S("stored0"), S("stored1")], S("staged"), S("dve")
        saved = S("saved")
        blk = c.enter_context(nc.Block())
        TURNS, TPT = D // (2 * WC), 2 * WC // P
        GR = TPT * NCH
        wv = w.rearrange("(k p) n -> p k n", p=P)

        @blk.sync
        def _(sp):
            with sp.Fori(0, TURNS - 1) as i:
                for j in range(2):
                    st.load(sp, i * 2 + 2 + j, j, wv[:, :, bass.ds((i + 1) * (2 * WC) + j * WC, WC)])

        @blk.gpsimd
        def _(pool):
            st.start_lo(pool)
            with pool.Fori(0, TURNS - 1) as i:
                for j in range(2):
                    st.cut_lo(pool, i * 2 + 2 + j, j)

        @blk.scalar
        def _(act):
            st.start_hi(act)
            if save is not None:
                act.dma_start(save, m.x[:]).then_inc(saved, 16)
            if dst is not None:
                act.sem_inc(stored[0], 16)
                act.sem_inc(stored[1], 16)

            def turn(i, last):
                for j in range(2):
                    for t in range(2 * j, 2 * j + 2) if dst is not None else ():
                        act.wait_ge(staged, i * TPT + t + 1)
                        act.dma_start(dst[bass.ds(i * TPT + t, 1), :, :].rearrange("o p t -> (o p) t"),
                                      stage[:, t % 2]).then_inc(stored[t % 2], 16)
                    if not last:
                        st.cut_hi(act, j, i * 16 + 32, done, i * GR + (j + 1) * GR // 2)

            with act.Fori(0, TURNS - 1) as i:
                turn(i, False)
            turn(TURNS - 1, True)
            if save is not None:
                act.wait_ge(saved, 16)
            if dst is not None:
                for t in range(2):
                    act.wait_ge(stored[t], 16 + 16 * TURNS * TPT // 2)

        @blk.vector
        def _(v):
            ch = Chain(v, chain)
            v.sem_inc(bank_free, 6)
            with v.Fori(0, TURNS) as i:
                ch.turn(i, 2 * TPT)
                for g in range(GR):
                    t, n = divmod(g, NCH)
                    v.wait_ge(done, i * GR + g + 1)
                    if dst is None:
                        gated_add(v, ch, m, m.ps[:, g % 6, 0:CH], gate, i * TPT + t, n, bank_free, tmp[:])
                    else:
                        if n == 0:
                            v.wait_ge(stored[t % 2], i * (16 * TPT // 2) + 16 * (t // 2) + 16)
                        q = v.tensor_copy(stage[:, t % 2, chunk(n)], m.ps[:, g % 6, 0:CH]).then_inc(bank_free, 1)
                        if n == NCH - 1:
                            v.wait_ge(bank_free, i * GR + g + 7)
                            v.sem_inc(staged, 1)

        @blk.tensor
        def _(pe):
            with pe.Fori(0, TURNS) as i:
                for g in range(GR):
                    t, n = divmod(g, NCH)
                    if g % (GR // 2) == 0:
                        st.wait_cut(pe, i * 2 + g // (GR // 2))
                    w_ = st.parts(t // 2, KT)
                    cols = slice((t % 2) * P, (t % 2 + 1) * P)
                    pe.wait_ge(bank_free, i * GR + g + 1)
                    for k in range(KT):
                        q = three_pass(pe, m.ps[:, g % 6, 0:CH], [x[:, k, cols] for x in w_],
                                       [x[:, k, chunk(n)] for x in (m.hhi, m.hlo)], k == 0, k == KT - 1)
                    q.then_inc(done, 1)


def kv_block(nc, a, m, st):
    name = "kv_"
    with ExitStack() as c:
        sb = lambda n, s, d=F32: c.enter_context(nc.sbuf_tensor(name + n, s, d, side="right"))
        signal = c.enter_context(semaphores(nc))
        S = lambda n: signal(name + n)
        TT = SEQ // P + 1
        stage = sb("stage", [P, 2, TT, WC])
        st.sems(nc, c, name)
        done, bank_free, stored, staged = S("done"), S("free"), [S("stored0"), S("stored1")], S("staged")
        blk = c.enter_context(nc.Block())
        GR = 2 * TT
        wv = a["w_kv"].rearrange("(k p) n -> p k n", p=P)
        outs = [(a["o_k_prompt"][0].rearrange("(t p) h c d -> p t (h c d)", p=P), a["o_k_sample"].rearrange("b t h c d -> (b t) (h c d)")),
                (a["o_v_prompt"][0].rearrange("(t p) h e -> p t (h e)", p=P), a["o_v_sample"].rearrange("b t h e -> (b t) (h e)"))]

        @blk.sync
        def _(sp):
            with sp.Fori(0, 3) as i:
                for j in range(2):
                    st.load(sp, i * 2 + 2 + j, j, wv[:, :, bass.ds((i + 1) * (2 * WC) + j * WC, WC)])

        @blk.gpsimd
        def _(pool):
            st.start_lo(pool)
            with pool.Fori(0, 3) as i:
                for j in range(2):
                    st.cut_lo(pool, i * 2 + 2 + j, j)

        @blk.scalar
        def _(act):
            act.sem_inc(stored[0], 32)
            act.sem_inc(stored[1], 32)
            st.start_hi(act)

            def store(n, col, j, out):
                act.wait_ge(staged, n + 1)
                act.dma_start(out[0][:, :, bass.ds(col, WC)], stage[:, j, 0:TT - 1, :]).then_inc(stored[j], 16)
                act.dma_start(out[1][:, bass.ds(col, WC)], stage[P - NS:P, j, TT - 1, :]).then_inc(stored[j], 16)

            def turn(half, i, last):
                for j in range(2):
                    n = i + 2 * half
                    if not last:
                        st.cut_hi(act, j, n * 16 + 32, done, n * GR + (j + 1) * TT)
                    store(n * 2 + j, i * (2 * WC) + j * WC, j, outs[half])

            with act.Fori(0, 2) as i:
                turn(0, i, False)
            turn(1, 0, False)
            turn(1, 1, True)
            for j in range(2):
                act.wait_ge(stored[j], 32 + 32 * 4)

        @blk.vector
        def _(v):
            v.sem_inc(bank_free, 6)
            with v.Fori(0, 4) as i:
                for g in range(GR):
                    j, t = divmod(g, TT)
                    if t == 0:
                        v.wait_ge(stored[j], i * 32 + 32)
                    v.wait_ge(done, i * GR + g + 1)
                    v.tensor_copy(stage[:, j, t, :], m.ps[:, g % 6, 0:WC]).then_inc(bank_free, 1)
                    if t == TT - 1:
                        v.wait_ge(bank_free, i * GR + g + 7)
                        v.sem_inc(staged, 1)

        @blk.tensor
        def _(pe):
            with pe.Fori(0, 4) as i:
                for g in range(GR):
                    j, t = divmod(g, TT)
                    if t == 0:
                        st.wait_cut(pe, i * 2 + j)
                    w_ = st.parts(j, KT)
                    first = t * P if t < TT - 1 else NT - P
                    pe.wait_ge(bank_free, i * GR + g + 1)
                    for k in range(KT):
                        q = three_pass(pe, m.ps[:, g % 6, 0:WC], [x[:, k, first:first + P] for x in (m.hhi, m.hlo)],
                                       [x[:, k, :] for x in w_], k == 0, k == KT - 1)
                    q.then_inc(done, 1)


def rms_block(nc, a, m, st, w):
    with ExitStack() as c:
        sb = lambda n, s, d=F32: c.enter_context(nc.sbuf_tensor("n_" + n, s, d, side="right"))
        signal = c.enter_context(semaphores(nc))
        S = lambda n: signal("n_" + n)
        o, sq, std, out = sb("o", [P, 2, NT]), sb("sq", [P, 2, NT]), sb("std", [P, 2, NT]), sb("out", [P, 2, NT])
        gain = sb("gain", [P, 1])
        landed, squared, summed, std_ready, ready, hi_ready, lo_ready, chain = (
            [S("landed0"), S("landed1")], S("sq_r"), S("sum"), S("std_r"), S("ready"), S("hi"), S("lo"), S("dve"))
        x_in = S("x_in")
        st.prime(S)
        blk = c.enter_context(nc.Block())

        @blk.sync
        def _(sp):
            for t in range(KT):
                if t >= 2:
                    sp.wait_ge(ready, t - 1)
                sp.dma_start(o[:, t % 2], a["s_o"][t]).then_inc(landed[t % 2], 16)
            st.prime_load(sp, w)
            sp.dma_start(m.x[:], a["s_x"]).then_inc(x_in, 16)
            sp.wait_ge(x_in, 16)

        @blk.scalar
        def _(act):
            def square(t):
                act.wait_ge(landed[t % 2], 16 * (t // 2 + 1))
                if t >= 2:
                    act.wait_ge(summed, t - 1)
                act.activation(sq[:, t % 2], o[:, t % 2], ACT.Square).then_inc(squared, 1)

            def high(t):
                act.wait_ge(ready, t + 1)
                act.copy(m.hhi[:, t], out[:, t % 2]).then_inc(hi_ready, 1)

            square(0)
            for t in range(KT):
                if t + 1 < KT:
                    square(t + 1)
                act.wait_ge(summed, t + 1)
                if t >= 2:
                    act.wait_ge(ready, t - 1)
                act.activation(std[:, t % 2].rearrange("p (n t) -> p n t", t=CH), m.ps[:, (t % 2) * 3:(t % 2) * 3 + 3, 0:CH],
                               ACT.Sqrt, bias=m.eps[:]).then_inc(std_ready, 1)
                if t >= 1:
                    high(t - 1)
            high(KT - 1)
            st.prime_hi(act, 0)
            st.prime_hi(act, 1)

        @blk.tensor
        def _(pe):
            for t in range(KT):
                pe.wait_ge(squared, t + 1)
                if t >= 2:
                    pe.wait_ge(std_ready, t - 1)
                for n in range(NCH):
                    q = pe.matmul(m.ps[:, (t % 2) * 3 + n, 0:CH], m.onesv[:], sq[:, t % 2, chunk(n)], start=True, stop=True)
                q.then_inc(summed, 1)

        @blk.vector
        def _(v):
            ch = Chain(v, chain)
            ch(v.tensor_scalar(gain[:], m.lnt[:, 64:65], 1.0 - LAM_INIT, None, ALU.mult))
            for t in range(KT):
                v.wait_ge(std_ready, t + 1)
                v.wait_ge(landed[t % 2], 16 * (t // 2 + 1))
                ch(v.reciprocal(std[:, t % 2], std[:, t % 2]))
                if t >= 2:
                    v.wait_ge(lo_ready, t - 1)
                v.scalar_tensor_tensor(out[:, t % 2], o[:, t % 2], gain[:, 0:1], std[:, t % 2], ALU.mult,
                                       ALU.mult).then_inc(ready, 1)

        @blk.gpsimd
        def _(pool):
            for t in range(KT):
                pool.wait_ge(hi_ready, t + 1)
                pool.tensor_tensor(m.hlo[:, t], out[:, t % 2], m.hhi[:, t].bitcast(F32), ALU.subtract).then_inc(lo_ready, 1)
            st.prime_lo(pool)


def rows_out_block(nc, a, m):
    with ExitStack() as c:
        SLOTS = 4
        rows = c.enter_context(nc.sbuf_tensor("y_rows", [P, SLOTS, D], F32, side="right"))
        signal = c.enter_context(semaphores(nc))
        S = lambda n: signal("y_" + n)
        turned, copied, stored = S("turned"), S("copied"), [S(f"stored{t}") for t in range(SLOTS)]
        blk = c.enter_context(nc.Block())
        tiles = [(a["o_y_prompt"][0, t * P:(t + 1) * P, :], P) for t in range(SEQ // P)]
        tiles.append((a["o_y_sample"].rearrange("b t f -> (b t) f"), NS))

        @blk.tensor
        def _(pe):
            for t, (_, n) in enumerate(tiles):
                if t >= 4:
                    pe.wait_ge(copied, t - 3)
                for k in range(KT):
                    q = pe.transpose(m.ps[0:n, 2 * (t % 4) + k // 4, (k % 4) * P:(k % 4 + 1) * P],
                                     m.x[:, k, t * P:t * P + n], m.ident[:])
                q.then_inc(turned, 1)

        @blk.vector
        def _(v):
            for t, (_, n) in enumerate(tiles):
                v.wait_ge(turned, t + 1)
                if t >= SLOTS:
                    v.wait_ge(stored[t % SLOTS], 16 * (t // SLOTS))
                v.tensor_copy(rows[0:n, t % SLOTS], m.ps[0:n, 2 * (t % 4):2 * (t % 4) + 2, :].rearrange("p u q -> p (u q)")
                              ).then_inc(copied, 1)

        @blk.sync
        def _(sp):
            for t, (dst, n) in enumerate(tiles):
                sp.wait_ge(copied, t + 1)
                sp.dma_start(dst, rows[0:n, t % SLOTS]).then_inc(stored[t % SLOTS], 16)
            for t in range(SLOTS):
                sp.wait_ge(stored[t], 16 * len(range(t, len(tiles), SLOTS)))


def attention_block(nc, a, m):
    with ExitStack() as c:
        sb = lambda n, s, d=F32: c.enter_context(nc.sbuf_tensor("t_" + n, s, d, side="right"))
        signal = c.enter_context(semaphores(nc))
        S = lambda n: signal("t_" + n)
        QB = SEQ // P
        NK = PAST + NS
        R = 2 * NS
        SCALE = HD ** -0.5
        ptab = sb("ptab", [1, NB * NPG], I32)
        flip, comp = sb("flip", [P, P]), sb("comp", [R, 2])
        lamv, lamt, lams = sb("lamv", [P, 4 * HD]), sb("lamt", [P, HD]), sb("lams", [P, 2])
        neglam, rowlam = sb("neglam", [P, 1]), sb("rowlam", [R, 1])
        pastb, newb = sb("pastb", [R, PAST]), sb("newb", [R, 2 * NS - ST])
        newc, pause = sb("newc", [R, NS]), sb("pause", [P, 1])
        krows, kn, vn, qs = sb("krows", [NS, D]), sb("kn", [P, H, NS]), sb("vn", [P, D]), sb("qs", [P, H, NS])
        osam = sb("osam", [P, H, NS])
        kp, vp, ktp = sb("kp", [P, NPG, D]), sb("vp", [P, NPG, D]), sb("ktp", [P, H, PAST])
        qbd = sb("qbd", [P, H, 9 * 2 * ST])
        ls, smax, ssum, wtc = sb("ls", [R, NK]), sb("smax", [R, 3]), sb("ssum", [R, 2]), sb("wtc", [P, NPG + 1, NS])
        qh, kr, vh, bd = sb("qh", [P, 2, SEQ]), sb("kr", [P, 2, QB, P]), sb("vh", [P, 2, QB, P]), sb("bd", [P, 2, SEQ])
        kt, bias, oh = sb("kt", [P, SEQ]), sb("bias", [P, SEQ]), sb("oh", [P, SEQ])
        lg = [[sb(f"lg{s}{k}", [P, SEQ]) for k in range(2)] for s in range(2)]
        wt = sb("wt", [P, 2, QB, P])
        mx, nmx, sums, rec = sb("mx", [P, 2, 2]), sb("nmx", [P, 2, 2]), sb("sums", [P, 2, 2]), sb("rec", [P, 2, 2])

        once_in, pt_in, once_ready, lam_exp, kn_done = S("once_in"), S("pt_in"), S("once"), S("lam_exp"), S("kn_done")
        kp_in, vp_in, head_in, out_done = S("kp_in"), S("vp_in"), [S("head_in0"), S("head_in1")], S("out")
        zeroed, qbd_ready, ktp_done, ktp_a, ktp_v = S("zeroed"), S("qbd"), S("ktp"), S("ktp_a"), S("ktp_v")
        s_done, s_soft, s_exp, s_norm, comb_done, comb_out, pv_done, pv_out = (
            S("s_done"), S("s_soft"), S("s_exp"), S("s_norm"), S("comb"), S("comb_out"), S("pv"), S("pv_out"))
        kt_done, kt_out, bias_done, bias_out = S("kt_done"), S("kt_out"), S("bias_done"), S("bias_out")
        qk_done, soft, exped, w_ready, wt_done, wt_out, o_done, o_out = (
            S("qk"), S("soft"), S("exped"), S("w"), S("wt_done"), S("wt_out"), S("o_done"), S("o_out"))
        tables_in = S("tables_in")
        osam_stored, chain = S("osam_stored"), S("dve")
        blk = c.enter_context(nc.Block())
        ck = a["cache_k"].rearrange("n p h c d -> n p (h c d)")
        cv = a["cache_v"].rearrange("n p h e -> n p (h e)")
        kview = a["o_k_prompt"][0].rearrange("(t p) h c d -> p t (h c d)", p=P)
        vview = a["o_v_prompt"][0].rearrange("(t p) h e -> p t (h e)", p=P)
        fd = a["s_dist"]
        once = [(flip[:], a["c_flip"]), (comp[:], a["c_comp"]),
                (lamv[:], a["attn_lam"][0].rearrange("a b -> (a b)").partition_broadcast(P)),
                (krows[:], a["o_k_sample"].rearrange("b t h c d -> (b t) (h c d)")),
                (vn[0:NS, :], a["o_v_sample"].rearrange("b t h e -> (b t) (h e)")),
                (qs[:], a["s_q"][:, :, SEQ:NT].rearrange("h p t -> p h t"))]
        tables = []
        for r in range(2 * ST):
            first = fd.offset + D - 1 - r % ST
            tables.append((pastb[r:R:2 * ST, :], bass.AP(fd.tensor, first - PAST, [[FM, H], [1, PAST]])))
            tables.append((newb[r:R:2 * ST, NS - ST:NS], bass.AP(fd.tensor, first, [[FM, H], [1, ST]])))

        def turns(engine, turn):
            with engine.Fori(0, NB // 2 - 1) as j:
                turn(j * 2, 0, False)
                turn(j * 2 + 1, 1, False)
            turn(NB - 2, 0, False)
            turn(NB - 1, 1, True)

        @blk.sync
        def _(sp):
            sp.dma_start(ptab[:], a["page_table"].rearrange("(o b) g -> o (b g)", o=1)).then_inc(pt_in, 16)
            sp.wait_ge(zeroed, 3)
            for dst, src in once:
                sp.dma_start(dst, src).then_inc(once_in, 16)
            sp.wait_ge(pt_in, 16)
            with sp.Fori(0, NB // 2) as j:
                for s in range(2):
                    i = j * 2 + s
                    pages = [sp.value_load(ptab[0:1, bass.ds(i * NPG + g, 1)], min_val=0, max_val=NPHYS - 1)
                             for g in range(NPG)]
                    for buf, cache, sem, used in ((kp, ck, kp_in, ktp_done), (vp, cv, vp_in, pv_done)):
                        sp.wait_ge(used, (i + 1) * H if used is ktp_done else i + 1)
                        for g in range(NPG):
                            sp.dma_start(buf[:, g, :], cache[bass.ds(pages[g], 1), :, :].rearrange("o p f -> (o p) f")
                                         ).then_inc(sem, 16)
                    sp.wait_ge(o_done, i * QB + QB)
                    cols = bass.ds(i * P, P)
                    for dst, src in ((qh[:, s], a["s_q"][bass.ds(i, 1), :, 0:SEQ].rearrange("o p t -> (o p) t")),
                                     (kr[:, s], kview[:, :, cols]), (vh[:, s], vview[:, :, cols]),
                                     (bd[:, s], bass.AP(fd.tensor, fd.offset + i * FM, [[1, P], [1, SEQ]]))):
                        sp.dma_start(dst, src).then_inc(head_in[s], 16)
            sp.wait_ge(pv_out, NB)
            sp.dma_start(a["s_o"][:, :, SEQ:NT].rearrange("h p t -> p h t"), osam[:]).then_inc(osam_stored, 16)
            sp.wait_ge(osam_stored, 16)
            sp.wait_ge(out_done, 16 * NB + 16)

        @blk.gpsimd
        def _(pool):
            for n, (dst, value) in enumerate(((newb[:], NEG), (vn[:], 0.0), (wtc[:], 0.0), (qbd[:], 0.0))):
                pool.memset(dst, value).then_inc(zeroed, 1)
                pool.wait_ge(zeroed, n + 1)

        @blk.scalar
        def _(act):
            act.wait_ge(zeroed, 1)
            for dst, src in tables:
                act.dma_start(dst, src).then_inc(tables_in, 16)
            act.wait_ge(once_ready, 1)
            act.activation(lams[:], lams[:], ACT.Exp).then_inc(lam_exp, 1)

            def pages(i, heads):
                for h in heads:
                    act.wait_ge(ktp_done, i * H + H + h + 1)
                    act.copy(ktp[:, h, :], m.ps[:, h % 4, :]).then_inc(ktp_a, 1)

            def turn(i, s, last):
                act.wait_ge(kt_done, i + 1)
                act.copy(kt[:].rearrange("p (u q) -> p u q", q=512), m.ps[:, 0:2, :]).then_inc(kt_out, 1)
                act.wait_ge(s_soft, i + 1)
                act.activation(ls[:], ls[:], ACT.Exp, bias=smax[:, 2:3], accum_out=ssum[:, 0:1]).then_inc(s_exp, 1)

                def exps(q):
                    act.wait_ge(soft, i * QB + q + 1)
                    for k in range(2):
                        x = lg[q % 2][k][:, 0:(q + 1) * P]
                        r = act.activation(x, x, ACT.Exp, bias=nmx[:, q % 2, k:k + 1], accum_out=sums[:, q % 2, k:k + 1])
                    r.then_inc(exped, 1)

                exps(0)
                exps(1)

                def output(q):
                    act.wait_ge(o_done, i * QB + 2 * QB + q + 1)
                    if q == 0:
                        act.wait_ge(out_done, i * 16 + 16)
                    act.copy(oh[:, q * P:(q + 1) * P], m.ps[:, 6 + q % 2, 0:P]).then_inc(o_out, 1)

                for q in range(QB):
                    act.wait_ge(wt_done, i * QB + q + 1)
                    act.copy(wt[:, q % 2].rearrange("p t q -> p (t q)")[:, 0:(q + 1) * P],
                             m.ps[:, 4:6, :].rearrange("p u q -> p (u q)")[:, 0:(q + 1) * P]).then_inc(wt_out, 1)
                    if q + 2 < QB:
                        exps(q + 2)
                    if q >= 1:
                        output(q - 1)
                    if q >= QB - 2 and not last:
                        pages(i + 1, (0, 2) if q == QB - 2 else (4, 6))
                output(QB - 1)
                act.wait_ge(o_out, i * QB + 2 * QB)
                act.dma_start(a["s_o"][bass.ds(i, 1), :, 0:SEQ].rearrange("o p t -> (o p) t"), oh[:]).then_inc(out_done, 16)

            pages(0, (0, 2, 4, 6))
            turns(act, turn)

        @blk.tensor
        def _(pe):
            pe.sem_inc(ktp_done, H)
            pe.sem_inc(pv_done, 1)
            pe.sem_inc(o_done, 2 * QB)
            pe.sem_inc(out_done, 16)
            pe.wait_ge(once_in, 16 * len(once))
            for h in range(H):
                q = pe.transpose(m.ps[:, 7, h * NS:(h + 1) * NS], krows[:, h * P:(h + 1) * P], m.ident[0:NS, 0:NS])
            q.then_inc(kn_done, 1)
            flat = qbd[:].rearrange("p h x -> p (h x)")

            def pages(i, heads):
                for h in heads:
                    if h >= 4:
                        pe.wait_ge(ktp_v if h % 2 else ktp_a, i * (H // 2) + (h - 4) // 2 + 1)
                    for g in range(NPG):
                        q = pe.transpose(m.ps[:, h % 4, g * P:(g + 1) * P], kp[:, g, h * P:(h + 1) * P], m.ident[:])
                    q.then_inc(ktp_done, 1)

            def turn(i, s, last):
                pe.wait_ge(o_out, i * QB + QB)
                pe.wait_ge(qbd_ready, i + 2)
                for h in range(H):
                    if h % 2 == 0:
                        pe.wait_ge(ktp_a, i * (H // 2) + h // 2 + 1)
                    else:
                        pe.wait_ge(ktp_v, i * (H // 2) + h // 2 + 1)
                    pe.matmul(m.ps[0:R, 4, :], flat[:, h * R:(h + 1) * R], ktp[:, h, :], start=(h == 0), stop=(h == H - 1))
                for h in range(H):
                    q = pe.matmul(m.ps[0:R, 5, 0:NS], flat[:, h * R:(h + 1) * R], kn[:, h, :], start=(h == 0), stop=(h == H - 1))
                q.then_inc(s_done, 1)
                pe.wait_ge(head_in[s], (i - s) * 32 + 64)
                for t in range(QB):
                    q = pe.transpose(m.ps[:, t // 4, (t % 4) * P:(t % 4 + 1) * P], kr[:, s, t, :], m.ident[:])
                q.then_inc(kt_done, 1)
                for u in range(2):
                    q = pe.matmul(m.ps[:, 2 + u, :], flip[:], bd[:, s, u * 512:(u + 1) * 512], start=True, stop=True)
                q.then_inc(bias_done, 1)
                def scores(qb):
                    if qb == 0:
                        pe.wait_ge(kt_out, i + 1)
                        pe.wait_ge(bias_out, i + 1)
                    else:
                        pe.wait_ge(soft, i * QB + qb)
                    w = (qb + 1) * P
                    for k in range(2):
                        for u in range(0, w, 512):
                            n = min(512, w - u)
                            q = pe.matmul(m.ps[:, 2 * k + u // 512, 0:n], qh[k * HD:(k + 1) * HD, s, qb * P:(qb + 1) * P],
                                          kt[k * HD:(k + 1) * HD, u:u + n], start=True, stop=True)
                    q.then_inc(qk_done, 1)

                pe.wait_ge(s_norm, i + 1)
                for g in range(NPG + 1):
                    n = P if g < NPG else NS
                    q = pe.matmul(m.ps[0:n, 6, g * NS:(g + 1) * NS], ls[:, g * P:g * P + n], m.comb[:], start=True, stop=True)
                q.then_inc(comb_done, 1)
                scores(0)
                pe.wait_ge(comb_out, i + 1)
                pe.wait_ge(vp_in, i * (16 * NPG) + 16 * NPG)
                for h in range(H):
                    for g in range(NPG + 1):
                        v_ = vp[:, g, h * P:(h + 1) * P] if g < NPG else vn[:, h * P:(h + 1) * P]
                        q = pe.matmul(m.ps[:, 7, h * ST:(h + 1) * ST], v_, wtc[:, g, h * ST:(h + 1) * ST],
                                      start=(g == 0), stop=(g == NPG))
                q.then_inc(pv_done, 1)

                def weigh(qb):
                    pe.wait_ge(wt_out, i * QB + qb + 1)
                    if qb >= 2:
                        pe.wait_ge(o_out, i * QB + QB + qb - 1)
                    for t in range(qb + 1):
                        q = pe.matmul(m.ps[:, 6 + qb % 2, 0:P], vh[:, s, t, :], wt[:, qb % 2, t, :],
                                      start=(t == 0), stop=(t == qb))
                    q.then_inc(o_done, 1)

                scores(1)
                for qb in range(QB):
                    if qb + 2 < QB:
                        scores(qb + 2)
                    pe.wait_ge(w_ready, i * QB + qb + 1)
                    if qb == 0:
                        pe.wait_ge(pv_out, i + 1)
                    else:
                        pe.wait_ge(wt_out, i * QB + qb)
                    for t in range(qb + 1):
                        q = pe.transpose(m.ps[:, 4 + t // 4, (t % 4) * P:(t % 4 + 1) * P],
                                         lg[qb % 2][0][:, t * P:(t + 1) * P], m.ident[:])
                    q.then_inc(wt_done, 1)
                    if qb >= 1:
                        weigh(qb - 1)
                    if qb == QB - 2 and not last:
                        pe.wait_ge(soft, i * QB + QB)
                        pe.wait_ge(kp_in, (i + 1) * (16 * NPG) + 16 * NPG)
                        pages(i + 1, range(4))
                    if qb == QB - 1 and not last:
                        pages(i + 1, range(4, H))
                weigh(QB - 1)

            pe.wait_ge(kp_in, 16 * NPG)
            pages(0, range(H))
            turns(pe, turn)

        @blk.vector
        def _(v):
            ch = Chain(v, chain)
            tt, ts, stt = v.tensor_tensor, v.tensor_scalar, v.scalar_tensor_tensor
            v.sem_inc(o_out, QB)
            v.sem_inc(qbd_ready, 1)
            v.wait_ge(once_in, 16 * len(once))
            v.wait_ge(tables_in, 16 * len(tables))
            v.wait_ge(zeroed, 4)
            ts(pastb[:], pastb[:], 1.0 / SCALE, None, ALU.mult)
            ts(newb[:], newb[:], 1.0 / SCALE, None, ALU.mult)
            for k in range(2):
                pair = [lamv[:, (2 * k + j) * HD:(2 * k + j + 1) * HD] for j in range(2)]
                q = v.tensor_tensor_reduce(lamt[:], pair[0], pair[1], 1.0, 0.0, ALU.mult, ALU.add, lams[:, k:k + 1])
                ch(q)
            v.sem_inc(once_ready, 1)
            v.wait_ge(lam_exp, 1)
            ch(tt(neglam[:], lams[:, 1:2], lams[:, 0:1], ALU.subtract))
            ch(ts(neglam[:], neglam[:], -LAM_INIT, None, ALU.add))
            ch(stt(rowlam[:], comp[:, 1:2], neglam[0:R, 0:1], comp[:, 0:1], ALU.mult, ALU.add))
            v.wait_ge(kn_done, 1)
            ch(v.tensor_copy(kn[:], m.ps[:, 7, 0:H * NS].rearrange("p (h t) -> p h t", t=NS)))
            before, PER = ch.n, 4 + 3 * QB

            def pages(i):
                for h in range(1, H, 2):
                    v.wait_ge(ktp_done, i * H + H + h + 1)
                    v.tensor_copy(ktp[:, h, :], m.ps[:, h % 4, :]).then_inc(ktp_v, 1)

            def turn(i, s, last):
                ch.turn(i, PER, before)
                tok = bass.ds(i * ST, ST)
                v.wait_ge(pv_done, i + 1)
                ts(qbd[0:HD, :, 0:ST], qs[0:HD, :, tok], 1.0, None, ALU.mult)
                ts(qbd[HD:P, :, ST:2 * ST], qs[HD:P, :, tok], 1.0, None, ALU.mult).then_inc(qbd_ready, 1)
                v.wait_ge(s_done, i + 1)
                v.memset(pause[:], 0.0)
                ch(v.tensor_tensor_reduce(ls[:, 0:PAST], m.ps[0:R, 4, :], pastb[:], SCALE, -3e38, ALU.add, ALU.max, smax[:, 0:1]))
                v.memset(pause[:], 0.0)
                ch(ts(newc[:], newb[:, bass.ds((NB - 1 - i) * ST, NS)], 1.0, None, ALU.mult))
                v.memset(pause[:], 0.0)
                ch(v.tensor_tensor_reduce(ls[:, PAST:NK], m.ps[0:R, 5, 0:NS], newc[:], SCALE, smax[:, 0:1], ALU.add, ALU.max,
                                          smax[:, 1:2]))
                ts(smax[:, 2:3], smax[:, 1:2], -1.0, None, ALU.mult).then_inc(s_soft, 1)
                v.wait_ge(bias_done, i + 1)
                ts(bias[:].rearrange("p (u q) -> p u q", q=512), m.ps[:, 2:4, :], 1.0 / SCALE, None, ALU.mult).then_inc(bias_out, 1)
                v.wait_ge(s_exp, i + 1)
                ch(v.reciprocal(ssum[:, 1:2], ssum[:, 0:1]))
                ts(ls[:], ls[:], ssum[:, 1:2], rowlam[:, 0:1], ALU.mult, ALU.mult).then_inc(s_norm, 1)
                v.wait_ge(comb_done, i + 1)
                v.tensor_copy(wtc[:, 0:NPG, :], m.ps[:, 6, 0:NPG * NS].rearrange("p (g r) -> p g r", r=NS))
                v.tensor_copy(wtc[0:NS, NPG, :], m.ps[0:NS, 6, NPG * NS:(NPG + 1) * NS]).then_inc(comb_out, 1)
                v.wait_ge(bias_out, i + 1)

                def logits(qb):
                    w, s = (qb + 1) * P, qb % 2
                    v.wait_ge(qk_done, i * QB + qb + 1)
                    if qb >= 2:
                        v.wait_ge(wt_done, i * QB + qb - 1)
                    v.memset(pause[:], 0.0)
                    for k in range(2):
                        src = m.ps[:, 2 * k:2 * k + 2, :].rearrange("p u q -> p (u q)")[:, 0:w]
                        q = v.tensor_tensor_reduce(lg[s][k][:, 0:w], src, bias[:, SEQ - w:SEQ], SCALE, -3e38,
                                                   ALU.add, ALU.max, mx[:, s, k:k + 1])
                    ch(q)
                    ts(nmx[:, s, :], mx[:, s, :], -1.0, None, ALU.mult).then_inc(soft, 1)

                logits(0)
                v.wait_ge(pv_done, i + 2)
                ts(osam[:, :, tok], m.ps[:, 7, 0:NS].rearrange("p (h t) -> p h t", t=ST), 1.0, None,
                   ALU.mult).then_inc(pv_out, 1)
                logits(1)
                for qb in range(QB):
                    w, s = (qb + 1) * P, qb % 2
                    v.wait_ge(exped, i * QB + qb + 1)
                    ch(v.reciprocal(rec[:, s, :], sums[:, s, :]))
                    ts(lg[s][0][:, 0:w], lg[s][0][:, 0:w], rec[:, s, 0:1], None, ALU.mult)
                    ch(ts(rec[:, s, 1:2], rec[:, s, 1:2], neglam[:, 0:1], None, ALU.mult))
                    stt(lg[s][0][:, 0:w], lg[s][1][:, 0:w], rec[:, s, 1:2], lg[s][0][:, 0:w], ALU.mult,
                        ALU.add).then_inc(w_ready, 1)
                    if qb + 2 < QB:
                        logits(qb + 2)
                if not last:
                    pages(i + 1)

            pages(0)
            turns(v, turn)
            assert ch.n == PER, ch.n


class Mem:
    pass


def program(nc, a):
    with ExitStack() as c:
        sb = lambda n, s, d=F32: c.enter_context(nc.sbuf_tensor(n, s, d))
        m = Mem()
        tiles = lambda w: w.rearrange("(k p) n -> p k n", p=P)
        w1 = lambda layer: tiles(a["mlp_w1"][layer])
        m.ps = c.enter_context(nc.psum_tensor("ps", [P, 8, 512], F32))
        m.ident, m.ones, m.onesv = sb("ident", [P, P]), sb("ones", [P, P]), sb("onesv", [P, P])
        m.eps = sb("eps", [P, 1])
        m.comb = sb("comb", [2 * NS, NS])
        m.modt = sb("modt", [P, NMOD * KT, NC9])
        m.lnt, m.lna, m.lam1 = sb("lnt", [P, 65]), sb("lna", [P, 64]), sb("lam1", [P, 4])
        m.cs, m.cb = sb("cs", [P, 4, KT, NC9]), sb("cb", [P, 4, KT, NC9])
        with ExitStack() as ch:
            with ExitStack() as c1:
                sb1 = lambda n, s, d=F32: c1.enter_context(nc.sbuf_tensor(n, s, d, side="right"))
                m.swap, m.select = sb1("swap", [P, P]), sb1("select", [P, GB * P])
                m.pt, m.ptr = sb1("pt", [P, NPT, G]), sb1("ptr", [P, 2 * L, G])
                m.bst, m.bsw = sb1("bst", [P, G, GC]), sb1("bsw", [P, G, GC])
                m.cst, m.csx = sb1("cst", [P, KT, P]), sb1("csx", [P, KT, P])
                m.h0s, m.h0x = sb1("h0s", [P, NB, G]), sb1("h0x", [P, NB, G])
                m.dskip, m.dskipd = sb1("dskip", [GC, G]), sb1("dskipd", [GC, G, GC])
                m.bat, m.sct = sb1("bat", [P, 112]), sb1("sct", [P, KT, NC9])
                m.spread = sb1("spread", [P, 2, G])
                with nc.sbuf_tensor("wada", [P, 2 * NSL, KT, WC], F32, side="right") as m.wada:
                    params_block(nc, a, m)
                    ada_block(nc, a, m)
                m.hhi, m.hlo = (ch.enter_context(nc.sbuf_tensor(n, [P, KT, NT], F32R)) for n in ("hhi", "hlo"))
                ssm_block(nc, a, m)
            m.x = ch.enter_context(nc.sbuf_tensor("x", [P, KT, NT], F32))
            st = Stream(nc, ch, "first")
            residual_block(nc, a, m, st)
            glu_block(nc, a, m, st)
            norm_block(nc, a, m, 0, "l0_", st, w1(0))
            mlp_block(nc, a, m, st, 0)
            norm_block(nc, a, m, 1, "l1_", st, tiles(a["w_kv"]))
            kv_block(nc, a, m, st)
            remod_block(nc, a, m, st, tiles(a["attn_w_q"][0]))
            column_block(nc, a, m, st, "wq_", a["attn_w_q"][0], dst=a["s_q"], save=a["s_x"])
        attention_block(nc, a, m)
        with ExitStack() as ch:
            m.hhi, m.hlo = (ch.enter_context(nc.sbuf_tensor(n + "2", [P, KT, NT], F32R)) for n in ("hhi", "hlo"))
            m.x = ch.enter_context(nc.sbuf_tensor("x2", [P, KT, NT], F32))
            st = Stream(nc, ch, "second")
            rms_block(nc, a, m, st, tiles(a["attn_w_o"][0]))
            column_block(nc, a, m, st, "wo_", a["attn_w_o"][0], gate=8)
            norm_block(nc, a, m, 2, "l2_", st, w1(1))
            mlp_block(nc, a, m, st, 1)
            norm_block(nc, a, m, 3, "l3_")
            rows_out_block(nc, a, m)


_INS = ["x_prompt", "x_sample", "state_ssm_re", "state_ssm_im", "cache_k", "cache_v", "page_table", "c_prompt",
        "c_sample", "rel_bias", "w_ada", "b_ada", "ln_g", "ln_b", "ssm_lam_re", "ssm_lam_im", "ssm_log_dt",
        "ssm_b_re", "ssm_b_im", "ssm_c_re", "ssm_c_im", "ssm_d", "ssm_w_glu_a", "ssm_w_glu_b", "w_ada_kv",
        "b_ada_kv", "w_kv", "attn_w_q", "attn_lam", "attn_subln_g", "attn_w_o", "mlp_w1", "mlp_w2"]
_OUTS = [("y_prompt", (1, SEQ, D)), ("y_sample", (NB, ST, D)), ("ssm_re_prompt", (1, 1, G, NP)),
         ("ssm_im_prompt", (1, 1, G, NP)), ("k_prompt", (1, SEQ, H, 2, HD)), ("v_prompt", (1, SEQ, H, VD)),
         ("ssm_re_sample", (1, NB, G, NP)), ("ssm_im_sample", (1, NB, G, NP)),
         ("k_sample", (NB, ST, H, 2, HD)), ("v_sample", (NB, ST, H, VD))]
_SCRATCH = [("s_dist", (H, FM)), ("s_xs", (NB, ST, D)), ("s_q", (H, P, NT)), ("s_o", (H, P, NT)),
            ("s_x", (P, KT, NT))]


def kernel(**inputs):
    import numpy as _np
    import concourse.bacc as _bacc
    from concourse.bass_utils import run_bass_kernel_spmd as _run

    nc = _bacc.Bacc("TRN2", target_bir_lowering=False, num_devices=1)
    arrays, a = {}, {}
    for name in _INS:
        arrays[name + "_in"] = _np.ascontiguousarray(inputs[name])
    for name, x in constants().items():
        arrays[name + "_in"] = x
    for name, x in arrays.items():
        a[name[:-3]] = nc.dram_tensor(name, x.shape, mybir.dt.from_np(x.dtype), kind="ExternalInput").ap()
    for name, shape in _OUTS:
        a["o_" + name] = nc.dram_tensor("out_" + name, shape, F32, kind="ExternalOutput").ap()
    for name, shape in _SCRATCH:
        a[name] = nc.dram_tensor(name, shape, F32, kind="Internal").ap()
    program(nc, a)
    r = _run(nc, [arrays], core_ids=[0])
    return tuple(r.results[0]["out_" + name] for name, _ in _OUTS)
```
